# Optimizing a Trainium2 kernel written in Bass

```python
import jax, jax.numpy as jnp
from jax import lax
import numpy as np

D_MODEL = 1024
BATCH = 1
SEQ = 512
DEPTH = 2
DEC_BATCH = 8
DEC_SEQ = 1
PAST_LEN = 1024
PAGE_SIZE = 128

N_HEADS = 16
QK_NOPE = 64
QK_ROPE = 32
V_HEAD = 64
Q_LORA = 384
KV_LORA = 256
ROPE_THETA = 10000.0
ATTN_SCALE = (QK_NOPE + QK_ROPE) ** -0.5
Q_BLOCK = 128
POOL_WINDOWS = (2, 4, 8, 16)
N_POOL_GROUPS = len(POOL_WINDOWS)
POOL_GROUP_WIDTH = D_MODEL // N_POOL_GROUPS
POOL_CTX = max(POOL_WINDOWS) - 1
N_EXPERTS = 16
N_EXPERT_GROUPS = 4
EXPERTS_PER_GROUP = N_EXPERTS // N_EXPERT_GROUPS
TOP_K = 2
D_EXPERT = 512
N_MIXERS = 2
N_MLA_LAYERS = (DEPTH + 1) // 2
N_POOL_LAYERS = DEPTH // 2
ALPHA = (2 * DEPTH) ** 0.25
BETA = (8 * DEPTH) ** -0.25
LN_EPS = 1e-5
RMS_EPS = 1e-6

kernel_name = 'mla_pool_hybrid_shared_router_moe_deepnorm_step'

def layer_norm(x, g, b):
    xf = x.astype(jnp.float32)
    mu = xf.mean(-1, keepdims=True)
    var = jnp.square(xf - mu).mean(-1, keepdims=True)
    return ((xf - mu) * lax.rsqrt(var + LN_EPS) * g.astype(jnp.float32) + b.astype(jnp.float32)).astype(x.dtype)

def rms_norm(x, g):
    xf = x.astype(jnp.float32)
    return (xf * lax.rsqrt(jnp.mean(xf * xf, -1, keepdims=True) + RMS_EPS) * g.astype(jnp.float32)).astype(x.dtype)

def rope(x, pos):
    half = QK_ROPE // 2
    inv = ROPE_THETA ** (-2.0 * jnp.arange(half, dtype=jnp.float32) / QK_ROPE)
    ang = pos.astype(jnp.float32)[:, None] * inv[None, :]
    cos, sin = jnp.cos(ang)[:, None, :], jnp.sin(ang)[:, None, :]
    x1, x2 = x[..., :half].astype(jnp.float32), x[..., half:].astype(jnp.float32)
    return jnp.concatenate([x1 * cos - x2 * sin, x1 * sin + x2 * cos], -1).astype(x.dtype)

def mla_project(x, pos, w_dq, g_q, w_uq, w_dkv, g_kv):
    B, S, _ = x.shape
    c_q = rms_norm(x @ w_dq, g_q)
    q = (c_q @ w_uq).reshape(B, S, N_HEADS, QK_NOPE + QK_ROPE)
    q_nope, q_rope = q[..., :QK_NOPE], rope(q[..., QK_NOPE:], pos)
    kv = x @ w_dkv
    c_kv = rms_norm(kv[..., :KV_LORA], g_kv)
    k_rope = rope(kv[..., None, KV_LORA:], pos)[:, :, 0]
    return q_nope, q_rope, c_kv, k_rope

def mla_attend_prompt(q_nope, q_rope, c_kv, k_rope, w_uk, w_uv):
    B, S, H, _ = q_nope.shape
    k_nope = jnp.einsum('bsr,rhd->bshd', c_kv, w_uk)
    v = jnp.einsum('bsr,rhd->bshd', c_kv, w_uv)
    nb = S // Q_BLOCK
    qn = q_nope.reshape(B, nb, Q_BLOCK, H, QK_NOPE).transpose(1, 0, 2, 3, 4)
    qr = q_rope.reshape(B, nb, Q_BLOCK, H, QK_ROPE).transpose(1, 0, 2, 3, 4)
    kpos = jnp.arange(S)

    def block(args):
        i, qn_b, qr_b = args
        s = jnp.einsum('bqhd,bkhd->bhqk', qn_b, k_nope) + jnp.einsum('bqhe,bke->bhqk', qr_b, k_rope)
        qpos = i * Q_BLOCK + jnp.arange(Q_BLOCK)
        s = jnp.where(kpos[None, :] <= qpos[:, None], s.astype(jnp.float32) * ATTN_SCALE, -jnp.inf)
        p = jax.nn.softmax(s, axis=-1).astype(v.dtype)
        return jnp.einsum('bhqk,bkhd->bqhd', p, v)

    o = lax.map(block, (jnp.arange(nb), qn, qr))
    return o.transpose(1, 0, 2, 3, 4).reshape(B, S, H * V_HEAD)

def mla_attend_sample(q_nope, q_rope, c_kv, k_rope, ckv_pages, kr_pages, page_table, w_uk, w_uv):
    DB, T, H, _ = q_nope.shape
    ckv_past = ckv_pages[page_table].reshape(DB, -1, KV_LORA)
    kr_past = kr_pages[page_table].reshape(DB, -1, QK_ROPE)
    past = ckv_past.shape[1]
    q_lat = jnp.einsum('bqhd,rhd->bqhr', q_nope, w_uk)
    s_past = jnp.einsum('bqhr,bkr->bhqk', q_lat, ckv_past) + jnp.einsum('bqhe,bke->bhqk', q_rope, kr_past)
    s_new = jnp.einsum('bqhr,bkr->bhqk', q_lat, c_kv) + jnp.einsum('bqhe,bke->bhqk', q_rope, k_rope)
    causal = jnp.arange(T)[None, :] <= jnp.arange(T)[:, None]
    s_new = jnp.where(causal, s_new.astype(jnp.float32) * ATTN_SCALE, -jnp.inf)
    s = jnp.concatenate([s_past.astype(jnp.float32) * ATTN_SCALE, s_new], -1)
    p = jax.nn.softmax(s, axis=-1).astype(c_kv.dtype)
    o_lat = jnp.einsum('bhqk,bkr->bqhr', p[..., :past], ckv_past) + jnp.einsum('bhqk,bkr->bqhr', p[..., past:], c_kv)
    return jnp.einsum('bqhr,rhd->bqhd', o_lat, w_uv).reshape(DB, T, H * V_HEAD)

def pool_mix(ctx, start_pos, w_pool, pool_scale):
    B, L, D = ctx.shape
    n = L - POOL_CTX
    xf = ctx.astype(jnp.float32)
    csum = jnp.concatenate([jnp.zeros((B, 1, D), jnp.float32), jnp.cumsum(xf, axis=1)], axis=1)
    pos = start_pos + jnp.arange(n)
    end = csum[:, POOL_CTX + 1:]
    means = []
    for g, w in enumerate(POOL_WINDOWS):
        c0, c1 = g * POOL_GROUP_WIDTH, (g + 1) * POOL_GROUP_WIDTH
        begin = csum[:, POOL_CTX + 1 - w: POOL_CTX + 1 - w + n, c0:c1]
        cnt = jnp.minimum(pos + 1, w).astype(jnp.float32)[None, :, None]
        means.append((end[..., c0:c1] - begin) / cnt)
    pooled = (jnp.concatenate(means, -1) - xf[:, POOL_CTX:]).astype(ctx.dtype)
    pooled = pooled.reshape(B, n, N_POOL_GROUPS, POOL_GROUP_WIDTH)
    y = jnp.einsum('bsgc,gcd->bsgd', pooled, w_pool).reshape(B, n, D)
    return y * pool_scale

def route(t, w_router, router_bias):
    s = jax.nn.sigmoid((t @ w_router).astype(jnp.float32))
    biased = (s + router_bias.astype(jnp.float32)).reshape(-1, N_EXPERT_GROUPS, EXPERTS_PER_GROUP)
    group_score = lax.top_k(biased, TOP_K)[0].sum(-1)
    best = jnp.argmax(group_score, -1)
    in_group = jnp.arange(N_EXPERT_GROUPS)[None, :] == best[:, None]
    masked = jnp.where(in_group[..., None], biased, -jnp.inf).reshape(-1, N_EXPERTS)
    _, idx = lax.top_k(masked, TOP_K)
    w = jnp.take_along_axis(s, idx, -1)
    w = w / w.sum(-1, keepdims=True)
    return (jax.nn.one_hot(idx, N_EXPERTS, dtype=jnp.float32) * w[..., None]).sum(1)

def moe(x, w_router, router_bias, w_gate, w_up, w_down):
    B, S, D = x.shape
    t = x.reshape(B * S, D)
    combine = route(t, w_router, router_bias).astype(x.dtype)
    h = jax.nn.silu(jnp.einsum('td,edf->tef', t, w_gate)) * jnp.einsum('td,edf->tef', t, w_up)
    y = jnp.einsum('tef,efd->td', h * combine[:, :, None], w_down)
    return y.reshape(B, S, D)

def setup_inputs(seed: int = 0) -> dict:
    key = jax.random.key(seed)
    ks = jax.random.split(key, 26)
    f32 = jnp.float32
    n_pages = PAST_LEN // PAGE_SIZE
    used = DEC_BATCH * n_pages
    n_phys = used + max(1, used // 4)

    def nrm(k, shape, fan_in, gain=1.0):
        return jax.random.normal(k, shape, f32) * (gain * fan_in ** -0.5)

    def gain(k, shape):
        return 1.0 + 0.02 * jax.random.normal(k, shape, f32)

    page_table = jax.random.permutation(ks[5], n_phys)[:used].reshape(DEC_BATCH, n_pages).astype(jnp.int32)
    return {
        'x_prompt': jax.random.normal(ks[0], (BATCH, SEQ, D_MODEL), f32),
        'x_sample': jax.random.normal(ks[1], (DEC_BATCH, DEC_SEQ, D_MODEL), f32),
        'cache_ckv': jax.random.normal(ks[2], (N_MLA_LAYERS, n_phys, PAGE_SIZE, KV_LORA), f32),
        'cache_krope': jax.random.normal(ks[3], (N_MLA_LAYERS, n_phys, PAGE_SIZE, QK_ROPE), f32),
        'state_pool': jax.random.normal(ks[4], (N_POOL_LAYERS, DEC_BATCH, POOL_CTX, D_MODEL), f32),
        'page_table': page_table,
        'w_dq': nrm(ks[6], (N_MLA_LAYERS, D_MODEL, Q_LORA), D_MODEL),
        'g_q': gain(ks[7], (N_MLA_LAYERS, Q_LORA)),
        'w_uq': nrm(ks[8], (N_MLA_LAYERS, Q_LORA, N_HEADS * (QK_NOPE + QK_ROPE)), Q_LORA),
        'w_dkv': nrm(ks[9], (N_MLA_LAYERS, D_MODEL, KV_LORA + QK_ROPE), D_MODEL),
        'g_kv': gain(ks[10], (N_MLA_LAYERS, KV_LORA)),
        'w_uk': nrm(ks[11], (N_MLA_LAYERS, KV_LORA, N_HEADS, QK_NOPE), KV_LORA),
        'w_uv': nrm(ks[12], (N_MLA_LAYERS, KV_LORA, N_HEADS, V_HEAD), KV_LORA, BETA),
        'w_o': nrm(ks[13], (N_MLA_LAYERS, N_HEADS * V_HEAD, D_MODEL), N_HEADS * V_HEAD, BETA),
        'w_pool': nrm(ks[14], (N_POOL_LAYERS, N_POOL_GROUPS, POOL_GROUP_WIDTH, POOL_GROUP_WIDTH), POOL_GROUP_WIDTH, BETA),
        'pool_scale': gain(ks[15], (N_POOL_LAYERS, D_MODEL)),
        'w_router': nrm(ks[16], (D_MODEL, N_EXPERTS), D_MODEL),
        'router_bias': 0.01 * jax.random.normal(ks[17], (N_EXPERTS,), f32),
        'w_gate': nrm(ks[18], (DEPTH, N_EXPERTS, D_MODEL, D_EXPERT), D_MODEL),
        'w_up': nrm(ks[19], (DEPTH, N_EXPERTS, D_MODEL, D_EXPERT), D_MODEL, BETA),
        'w_down': nrm(ks[20], (DEPTH, N_EXPERTS, D_EXPERT, D_MODEL), D_EXPERT, BETA),
        'ln1_g': gain(ks[21], (DEPTH, D_MODEL)),
        'ln1_b': 0.02 * jax.random.normal(ks[22], (DEPTH, D_MODEL), f32),
        'ln2_g': gain(ks[23], (DEPTH, D_MODEL)),
        'ln2_b': 0.02 * jax.random.normal(ks[24], (DEPTH, D_MODEL), f32),
    }

def reference(x_prompt, x_sample, cache_ckv, cache_krope, state_pool, page_table,
              w_dq, g_q, w_uq, w_dkv, g_kv, w_uk, w_uv, w_o, w_pool, pool_scale,
              w_router, router_bias, w_gate, w_up, w_down, ln1_g, ln1_b, ln2_g, ln2_b):
    B, S, _ = x_prompt.shape
    DB, T, _ = x_sample.shape
    past_len = page_table.shape[1] * cache_ckv.shape[2]
    pos_p = jnp.arange(S)
    pos_s = past_len + jnp.arange(T)
    xp, xs = x_prompt, x_sample
    ckv_p, kr_p, pool_p, ckv_s, kr_s, pool_s = [], [], [], [], [], []
    for i in range(DEPTH):
        j = i // N_MIXERS
        if i % N_MIXERS == 0:
            qn, qr, c, k = mla_project(xp, pos_p, w_dq[j], g_q[j], w_uq[j], w_dkv[j], g_kv[j])
            mix_p = mla_attend_prompt(qn, qr, c, k, w_uk[j], w_uv[j]) @ w_o[j]
            ckv_p.append(c)
            kr_p.append(k)
            qn, qr, c, k = mla_project(xs, pos_s, w_dq[j], g_q[j], w_uq[j], w_dkv[j], g_kv[j])
            mix_s = mla_attend_sample(qn, qr, c, k, cache_ckv[j], cache_krope[j], page_table, w_uk[j], w_uv[j]) @ w_o[j]
            ckv_s.append(c)
            kr_s.append(k)
        else:
            ctx_p = jnp.concatenate([jnp.zeros((B, POOL_CTX, D_MODEL), xp.dtype), xp], axis=1)
            ctx_s = jnp.concatenate([state_pool[j].astype(xs.dtype), xs], axis=1)
            mix_p = pool_mix(ctx_p, 0, w_pool[j], pool_scale[j])
            mix_s = pool_mix(ctx_s, past_len, w_pool[j], pool_scale[j])
            pool_p.append(ctx_p[:, -POOL_CTX:])
            pool_s.append(ctx_s[:, -POOL_CTX:])
        xp = layer_norm(ALPHA * xp + mix_p, ln1_g[i], ln1_b[i])
        xs = layer_norm(ALPHA * xs + mix_s, ln1_g[i], ln1_b[i])
        xp = layer_norm(ALPHA * xp + moe(xp, w_router, router_bias, w_gate[i], w_up[i], w_down[i]), ln2_g[i], ln2_b[i])
        xs = layer_norm(ALPHA * xs + moe(xs, w_router, router_bias, w_gate[i], w_up[i], w_down[i]), ln2_g[i], ln2_b[i])
    return (xp, xs, jnp.stack(ckv_p), jnp.stack(kr_p), jnp.stack(pool_p), jnp.stack(ckv_s), jnp.stack(kr_s), jnp.stack(pool_s))


_drawn_inputs = setup_inputs


def setup_inputs(seed=0):
    import zlib

    import numpy as np

    out = dict(_drawn_inputs(seed))
    spreads = {}
    factors = {'cache_ckv': 6.429, 'cache_krope': 8.0, 'g_q': 8.0, 'pool_scale': 16.481}
    for name, (base, spread) in spreads.items():
        noise = np.random.default_rng([zlib.crc32(name.encode()), seed]).standard_normal(out[name].shape)
        drawn = base * np.exp(spread * noise) if base else spread * noise
        out[name] = __import__('jax').numpy.asarray(drawn.astype(out[name].dtype))
    for name, factor in factors.items():
        out[name] = (out[name] * factor).astype(out[name].dtype)
    return out
```

```python
from contextlib import ExitStack

import numpy as np

import concourse.bass as bass
from concourse import mybir

D = 1024
SEQ = 512
DB = 8
TOK = SEQ + DB
P = 128
NT = SEQ // P + 1
KD = D // P
H, NOPE, ROPE, VH = 16, 64, 32, 64
PAIRS = H // 2
QL, KVL = 384, 256
MQ, MKV = QL // P, KVL // P
HQ = NOPE + ROPE
PAGE, NPAGES, NPHYS = 128, 8, 80
PAST = PAGE * NPAGES
E, GROUPS, EPG, F = 16, 4, 4, 512
KF = F // P
CTX = 15
WINDOWS = (2, 4, 8, 16)
ALPHA = 4.0 ** 0.25
SCALE = HQ ** -0.5
LN_EPS, RMS_EPS = 1e-5, 1e-6
BIG = 1e30
HALF = TOK // 2
CAP = 96
KOV = (TOK - 1) // CAP
NOV = 10
TILES = E + NOV
BAND = P + CTX

F32 = mybir.dt.float32
I32 = mybir.dt.int32
ALU = mybir.AluOpType
ACT = mybir.ActivationFunctionType
AXX = mybir.AxisListType.X


def rows_of(i):
    return P if i < NT - 1 else DB


def constants():
    parts, place, at = [], {}, 0

    def put(name, a, *dims):
        nonlocal at
        full = np.zeros((P, int(np.prod(a.shape[1:]))), np.float32)
        full[:a.shape[0]] = a.reshape(a.shape[0], -1)
        parts.append(full)
        place[name] = (at, dims or a.shape[1:])
        at += full.shape[1]

    def rowwise(v):
        return np.broadcast_to(np.asarray(v, np.float32).reshape(1, -1), (P, np.size(v)))

    i = np.arange(P)
    put("ident", np.eye(P))
    put("ones", np.ones((P, P)))
    put("before", (i[:, None] < i[None, :]))
    half = ROPE // 2
    inv = (np.float32(10000.0) ** (np.float32(-2.0) * np.arange(half, dtype=np.float32) / np.float32(ROPE)))
    pos = np.concatenate([np.arange(SEQ), np.full(DB, PAST)]).astype(np.float32)
    ang = pos[:, None] * inv[None, :].astype(np.float32)
    cos, sin = np.cos(ang).astype(np.float32), np.sin(ang).astype(np.float32)
    rot = np.concatenate([cos.T, cos.T, -sin.T, sin.T])
    one = np.ones((NOPE, TOK))
    put("rope_q", -SCALE * np.stack([np.concatenate([one, rot]), np.concatenate([rot, one])], 1))
    def natural(t):
        out = np.zeros((P, NT, half), np.float32)
        for j in range(NT):
            out[:rows_of(j), j] = t[P * j:P * j + rows_of(j)]
        return out
    put("cos_k", natural(cos))
    put("sin_k", natural(sin))
    put("causal", np.concatenate([np.zeros((P, SEQ - P)), np.where(i[None, :] > i[:, None], BIG, 0.0)], 1))
    put("own_sample", np.broadcast_to(np.where(np.eye(DB) > 0, 0.0, BIG)[None], (H, DB, DB)))
    band = np.zeros((P, 2, 4, BAND), np.float32)
    band_s = np.zeros((DB * CTX, 4, DB), np.float32)
    own_s = np.zeros((DB, 4, DB), np.float32)
    for g, w in enumerate(WINDOWS):
        for c in range(BAND):
            for r in range(max(0, c - w + 1), min(P, c + 1)):
                band[r, 0, g, c] = 1.0 / min(c + 1, w)
                band[r, 1, g, c] = 1.0 / w
            if c < P:
                band[c, :, g, c] -= 1.0
        for b in range(DB):
            band_s[b * CTX + CTX - w + 1:(b + 1) * CTX, g, b] = 1.0 / w
            own_s[b, g, b] = 1.0 / w - 1.0
    put("band", band)
    put("band_s", band_s)
    put("own_s", own_s)
    e = np.arange(E)
    put("slot0", rowwise(e * CAP))
    put("slot_over", rowwise((E - 1) * CAP - e * CAP))
    put("steps", rowwise(CAP * np.arange(1, KOV + 1)))
    put("before_e", rowwise(e[None, :] < e[:, None]), E, E)
    j = np.arange(EPG)
    put("earlier", rowwise(j[None, :] < j[:, None]), EPG, EPG)
    put("prefer", rowwise(GROUPS - np.arange(GROUPS)))
    put("real_row", (i < DB).astype(np.float32)[:, None])
    put("over_k", rowwise(np.arange(NOV)))
    put("even_k", rowwise(np.arange(0, NOV, 2)))
    put("expert", rowwise(e))
    put("ln_eps", np.full((P, 1), LN_EPS))
    put("rms_eps", np.full((P, 1), RMS_EPS))
    return np.concatenate(parts, 1).astype(np.float32), place


def build(nc, t, consts_shape, place):
    ctx = ExitStack()
    with ctx:
        def sem(name):
            return ctx.enter_context(nc.semaphore(name))

        def sb(name, shape, dt=F32):
            return ctx.enter_context(nc.sbuf_tensor(name, shape, dt))

        ring = [sb("ring0", [P, 12288]), sb("ring1", [P, 12288])]
        X = sb("X", [P, NT, D])
        gb = sb("gb", [P, 4, D])
        C = sb("C", list(consts_shape))
        wr = sb("wr", [P, KD, E])
        small = sb("small", [P, 272])
        ids = sb("ids", [P, 128], I32)
        arena = sb("arena", [P, 15152])
        PS = ctx.enter_context(nc.psum_tensor("PS", [P, 4096], F32))

        def view(buf, off, *dims):
            n = int(np.prod(dims))
            ap = buf[:, off:off + n]
            if len(dims) == 2:
                return ap.rearrange("p (a b) -> p a b", a=dims[0])
            if len(dims) == 3:
                return ap.rearrange("p (a b c) -> p a b c", a=dims[0], b=dims[1])
            return ap

        def const(name):
            off, dims = place[name]
            if len(dims) == 3:
                n = int(np.prod(dims))
                return C[:, off:off + n].rearrange("p (a b c) -> p a b c", a=dims[0], b=dims[1])
            return view(C, off, *dims)

        def bank(b, *dims, off=0):
            return view(PS, 512 * b + off, *(dims or (512,)))

        ident, ones, before = const("ident"), const("ones"), const("before")
        rope_q, cos_k, sin_k = const("rope_q"), const("cos_k"), const("sin_k")
        causal, own_sample = const("causal"), const("own_sample")
        band, band_s, own_s = const("band"), const("band_s"), const("own_s")
        slot0, slot_over, steps = const("slot0"), const("slot_over"), const("steps")
        before_e, earlier, prefer = const("before_e"), const("earlier"), const("prefer")
        real_row, over_k, even_k, expert = (const(n) for n in ("real_row", "over_k", "even_k", "expert"))
        ln_eps, rms_eps = const("ln_eps"), const("rms_eps")

        wg = [view(r, 0, KD, F) for r in ring]
        wu = [view(r, 4096, KD, F) for r in ring]
        wd = [view(r, 8192, KF, D) for r in ring]
        R0, R1 = ring
        wo = view(R0, 0, KD, D)
        V = view(R0, 8192, 4, D)
        kraw = view(R0, 8192, NT, ROPE)
        krot = view(R0, 8192 + 160, NT, ROPE)
        gkv = view(R0, 8192 + 320, KVL)
        rtmp = view(R0, 8192 + 576, 4, 80)
        rq = view(R0, 8192 + 900, TOK)
        sqj = view(R0, 8192 + 1420, KVL)
        kdup = view(R0, 8192 + 1680, NT, 4, ROPE)
        wdq = view(R1, 0, KD, QL)
        wdkv = view(R1, 3072, KD, KVL + ROPE)
        sq = view(R1, 5376, MQ, TOK)
        prob = view(R1, 0, 4, 512)
        probT = view(R1, 2048, 2, 512)
        wqn = view(R1, 6936, MQ, 2 * HQ)
        wuq = view(R1, 7512, MQ, 256)
        wuk = view(R1, 8280, MKV, P)
        qT = [view(R1, 8536, TOK), view(R1, 9056, TOK)]
        kT = [view(R1, 9576, SEQ), view(R1, 10088, SEQ)]
        osb = view(R1, 10600, 4, P)
        ckp = [view(R1, 2048 * s, NPAGES, KVL) for s in range(2)]
        krp = [view(R1, 4096 + 1024 * s, NPAGES, 4, ROPE) for s in range(2)]
        kpT = [view(R1, 6144 + 3072 * s, 3, PAST) for s in range(2)]
        oT = view(arena, 0, PAIRS, TOK)
        ckv = view(arena, 4160, NT, KVL)
        ckT = view(arena, 5440, 3, TOK)
        XT = view(arena, 7168, KD, TOK)
        wukT = view(arena, 7168, PAIRS, KVL)
        qlat = view(arena, 9216, MKV, DB, H)
        olat = view(arena, 9472, MKV, DB, H)
        ps_s = view(arena, 9728, PAST + DB)
        psT_s = view(arena, 10760, NPAGES + 1, H)
        wuv = view(arena, 11328, MKV, D)
        cq = view(arena, 13376, MQ, TOK)
        qs = view(arena, 7000, PAIRS, 16)
        qr = view(arena, 14936, DB, H)
        xe = [view(arena, 1024 * s, D) for s in range(2)]
        xeT = [view(arena, 2048 + 768 * s, KD, CAP) for s in range(2)]
        sg = [view(arena, 3584 + 384 * s, KF, CAP) for s in range(2)]
        h = [view(arena, 4352 + 384 * s, KF, CAP) for s in range(2)]
        ys = [view(arena, 5120 + 1024 * s, D) for s in range(2)]
        ya = [view(arena, 7168 + 1024 * s, D) for s in range(2)]
        yb = [view(arena, 9216 + 1024 * s, D) for s in range(2)]
        state = view(arena, 0, D)
        pscale = view(arena, 1024, D)
        poolT = view(arena, 2048, KD, TOK)
        wpool = view(arena, 13104, KD, 256)
        RT = 11328

        def rt(n, *dims):
            nonlocal RT
            v = view(arena, RT, *(dims or (n,)))
            RT += n
            return v

        r_exp, r_s, r_bias, r_rank, r_sel, r_comb, r_slot = (rt(80) for _ in range(7))
        r_big = rt(320)
        r_gs, r_gp, r_gsel = (rt(20) for _ in range(3))
        r_m, r_den, r_a, r_b, r_all = (rt(5) for _ in range(5))
        r_nt, r_ex, r_ovb, r_end, r_diff = (rt(E) for _ in range(5))
        r_tab = rt(32)
        r_nh = rt(8)
        r_k = rt(160)
        r_nov = rt(1)
        assert RT <= 13104
        bias_row = view(small, 0, E)
        gq = view(small, 16, MQ)
        ss = view(small, 20, NT)
        kstd = view(small, 25, NT)
        krs = view(small, 30, NT)
        mneg = view(small, 36, 8)
        rsum = view(small, 44, 8)
        rinv = view(small, 52, 8)
        s_mneg, s_sum, s_inv = view(small, 60, 2), view(small, 62, 2), view(small, 64, 2)
        bn = view(small, 66, NT, 12)
        mv = view(small, 126, NT, 2)
        std, rstd, nmr = view(small, 136, NT), view(small, 141, NT), view(small, 146, NT)
        ca, cb = view(small, 152, NT), view(small, 158, NT)
        qb = [view(small, 168 + 48 * s, 3, H) for s in range(2)]
        zero_src = view(arena, 0, D)
        page_ids = ids[:, 0:64]
        idx_a, idx_b = ids[:, 64:69], ids[:, 72:77]
        tile_ids, n_half = ids[:, 80:112], ids[:, 120:121]

        xs = nc.dram_tensor("expert_rows", ((TILES + 1) * CAP, D), F32).ap()
        yd = nc.dram_tensor("expert_out", (TILES * CAP, D), F32).ap()

        c_ld, wdq_ld, wdkv_ld, gain_ld, wuv_ld, router_ld, wo_ld = (
            sem(n) for n in ("c_ld", "wdq_ld", "wdkv_ld", "gain_ld", "wuv_ld", "router_ld", "wo_ld"))
        x_ld = [sem(f"x_ld{i}") for i in range(NT)]
        pt_ld, wqn_ld, wuk_ld, zero_set, zero_st = (
            sem(n) for n in ("pt_ld", "wqn_ld", "wuk_ld", "zero_set", "zero_st"))
        page_ld = [sem("page_ld0"), sem("page_ld1")]
        kr_dup = sem("kr_dup")
        gb_ld = [[sem(f"gb{w + 1}_ld_{L}") for w in range(2)] for L in range(2)]
        wp_ld, st_ld, wp_ready = sem("wp_ld"), sem("st_ld"), sem("wp_ready")
        out_st = sem("out_st")
        latent_st = sem("latent_st")
        passed = sem("passed")
        pool_out = sem("pool_out")
        xt_ps = sem("xt_ps")
        xt_ev = [sem("xt_ev_dve"), sem("xt_ev_act")]
        cq_ps, cq_copied, cq_squared, cq_sum, rq_std, cq_done = (
            sem(n) for n in ("cq_ps", "cq_copied", "cq_squared", "cq_sum", "rq_std", "cq_done"))
        kraw_zero, kv_ps, kv_ss, kv_std, kv_ready, kr_ready, ck_ps, ck_ev, krope_set = (
            sem(n) for n in ("kraw_zero", "kv_ps", "kv_ss", "kv_std", "kv_ready", "kr_ready",
                             "ck_ps", "ck_ev", "krope_set"))
        dve_step = sem("dve_step")
        wq_even, wq_odd, q_ps, q_ev, for_act, act_ev = (
            sem(n) for n in ("wq_even", "wq_odd", "q_ps", "q_ev", "for_act", "act_ev"))
        s_ps, min_set, exp_set, t_ps, o_ps, rinv_set, o_ev = (
            sem(n) for n in ("s_ps", "min_set", "exp_set", "t_ps", "o_ps", "rinv_set", "o_ev"))
        pt_ev = [sem("pt_ev_dve"), sem("pt_ev_act")]
        qpad_zero = sem("qpad_zero")
        ql_ps, ql_ev, qb_set, tp_ps, sc_ps, new_masked, smin_set, sexp_set, sinv_set, sp_ready = (
            sem(n) for n in ("ql_ps", "ql_ev", "qb_set", "tp_ps", "sc_ps", "new_masked", "smin_set",
                             "sexp_set", "sinv_set", "sp_ready"))
        tp_ev = [sem("tp_ev_dve"), sem("tp_ev_act")]
        spT_ps, spT_ev, spv_ps, ol_ev, uv_ps, uv_ev = (
            sem(n) for n in ("spT_ps", "spT_ev", "spv_ps", "ol_ev", "uv_ps", "uv_ev"))
        mix_ps = sem("mix_ps")
        ln_z, ln_agg, ln_std, ln_rstd, ln_nrm, ln_gam, ln_out = (
            [sem(f"{n}_{L}") for L in range(2)]
            for n in ("ln_z", "ln_agg", "ln_std", "ln_rstd", "ln_nrm", "ln_gam", "ln_out"))
        turn_ps, turn_ev = sem("turn_ps"), sem("turn_ev")
        lg_zero, lg_ps, lg_exp, sel_set, cnt_ps, idx_set, tab_set, scat, xscaled = (
            sem(n) for n in ("lg_zero", "lg_ps", "lg_exp", "sel_set", "cnt_ps", "idx_set", "tab_set",
                             "scat", "xscaled"))
        gath = [sem("gath0"), sem("gath1")]
        def expert_sems(L):
            two = ("wg_ld", "wu_ld", "wd_ld", "xe_ld", "y_st", "gate_ps", "up_ps", "down_ps")
            one = ("tr_ps", "xeT_set", "sg_set", "h_set", "y_set")
            return {n: [sem(f"{n}{s}_{L}") for s in range(2)] for n in two} | {n: sem(f"{n}_{L}") for n in one}

        S = [expert_sems(0), expert_sems(1)]
        block = ctx.enter_context(nc.Block())

        def bcast(row, n=P):
            return row.unsqueeze(0).to_broadcast([n] + list(row.shape))

        turn_bank = [4, 5, 7]

        def score(i):
            return bank((2, 2, 1, 0)[i], P * (i + 1), off=256 if i == 0 else 0)

        def scored(i):
            return min(4 - i, 4) if i > 1 else 4

        def hold(eng, s, value):
            eng.wait_ge(s, value)
            if not isinstance(value, int):
                eng.sem_inc(passed, 1)

        @block.sync
        def _(sp):
            sp.dma_start(C[:, :], t["consts"]).then_inc(c_ld, 16)
            for i in range(4):
                sp.dma_start(X[:, i, :], t["x_prompt"][0, P * i:P * (i + 1), :]).then_inc(x_ld[i], 16)
            sp.dma_start(X[0:DB, 4, :], t["x_sample"][:, 0, :]).then_inc(x_ld[4], 16)
            sp.dma_start(wdq, t["w_dq"][0].rearrange("(k p) n -> p k n", p=P)).then_inc(wdq_ld, 16)
            with nc.allow_non_contiguous_dma(reason="384 words"):
                sp.dma_start(gq, t["g_q"][0].rearrange("(m p) -> p m", p=P)).then_inc(gain_ld, 16)
            sp.dma_start(wdkv, t["w_dkv"][0].rearrange("(k p) n -> p k n", p=P)).then_inc(wdkv_ld, 16)
            sp.dma_start(gkv, bcast(t["g_kv"][0])).then_inc(gain_ld, 16)
            sp.dma_start(page_ids[0:1, :], t["page_table"].rearrange("b n -> (b n)").unsqueeze(0)).then_inc(pt_ld, 16)

            def load_pair(j):
                sp.dma_start(wqn, t["w_uq"][0].rearrange("(m p) n -> p m n", p=P)[:, :, bass.ds(2 * HQ * j, 2 * HQ)]
                             ).then_inc(wqn_ld, 16)
                sp.dma_start(wuk, t["w_uk"][0].rearrange("(m p) h d -> p m (h d)", p=P)[:, :, bass.ds(P * j, P)]
                             ).then_inc(wuk_ld, 16)

            load_pair(0)
            sp.dma_start(wuv, t["w_uv"][0].rearrange("(m p) h d -> p m (h d)", p=P)).then_inc(wuv_ld, 16)
            sp.dma_start(wr[:, :, :], t["w_router"].rearrange("(k p) n -> p k n", p=P)).then_inc(router_ld, 16)
            sp.dma_start(bias_row, bcast(t["router_bias"])).then_inc(router_ld, 16)
            sp.dma_start(gb[:, 0, :], bcast(t["ln1_g"][0])).then_inc(gb_ld[0][0], 16)
            sp.dma_start(gb[:, 1, :], bcast(t["ln1_b"][0])).then_inc(gb_ld[0][0], 16)
            sp.dma_start(gb[:, 2, :], bcast(t["ln2_g"][0])).then_inc(gb_ld[0][1], 16)
            sp.dma_start(gb[:, 3, :], bcast(t["ln2_b"][0])).then_inc(gb_ld[0][1], 16)
            sp.dma_start(wo, t["w_o"][0].rearrange("(k p) n -> p k n", p=P)).then_inc(wo_ld, 16)
            sp.wait_ge(zero_set, 1)
            sp.dma_start(xs.rearrange("(a p) d -> p a d", p=CAP),
                         zero_src[0:CAP, :].unsqueeze(1).to_broadcast([CAP, TILES + 1, D])).then_inc(zero_st, 16)
            sp.dma_start(yd[E * CAP:, :].rearrange("(a p) d -> p a d", p=CAP),
                         zero_src[0:CAP, :].unsqueeze(1).to_broadcast([CAP, NOV, D])).then_inc(zero_st, 16)
            sp.wait_ge(kv_ready, NT)
            sp.wait_ge(kr_ready, 1)
            for i in range(4):
                sp.dma_start(t["o_ckv_p"][0, 0, P * i:P * (i + 1), :], ckv[:, i, :]).then_inc(latent_st, 16)
                sp.dma_start(t["o_kr_p"][0, 0, P * i:P * (i + 1), :], krot[:, i, :]).then_inc(latent_st, 16)
            sp.dma_start(t["o_ckv_s"][0, :, 0, :], ckv[0:DB, 4, :]).then_inc(latent_st, 16)
            sp.dma_start(t["o_kr_s"][0, :, 0, :], krot[0:DB, 4, :]).then_inc(latent_st, 16)
            sp.dma_start(t["o_pool_s"][0, :, 0:CTX - 1, :], t["state_pool"][0, :, 1:CTX, :]).then_inc(out_st, 16)
            sp.wait_ge(wq_odd, 1)
            sp.wait_ge(for_act, 3)
            load_pair(1)
            with sp.Fori(2, PAIRS) as j:
                sp.wait_ge(wq_odd, j)
                sp.wait_ge(for_act, 4 * j - 2)
                load_pair(j)

            def load_pages(b, s):
                for n in range(NPAGES):
                    page = sp.value_load(page_ids[0:1, bass.ds(b * NPAGES + n, 1)], min_val=0, max_val=NPHYS - 1)
                    sp.dma_start(ckp[s][:, n, :], t["cache_ckv"][0, bass.ds(page, 1), :, :].rearrange("a p d -> (a p) d")
                                 ).then_inc(page_ld[s], 16)
                    sp.dma_start(krp[s][:, n, 0, :], t["cache_krope"][0, bass.ds(page, 1), :, :].rearrange("a p d -> (a p) d")
                                 ).then_inc(page_ld[s], 16)

            sp.wait_ge(pt_ld, 16)
            sp.wait_ge(act_ev, 4 * PAIRS)
            load_pages(0, 0)
            load_pages(1, 1)
            with sp.Fori(1, DB // 2) as u:
                for s in range(2):
                    sp.wait_ge(spv_ps, 2 * u + s - 1)
                    load_pages(2 * u + s, s)

            def load_expert(L, e, s, gate_free=None, up_free=None, down_free=None):
                q = S[L]
                if gate_free:
                    sp.wait_ge(*gate_free)
                sp.dma_start(wg[s], t["w_gate"][L, bass.ds(e, 1), :, :].rearrange("a (k p) f -> p (a k) f", p=P)
                             ).then_inc(q["wg_ld"][s], 16)
                if up_free:
                    sp.wait_ge(*up_free)
                sp.dma_start(wu[s], t["w_up"][L, bass.ds(e, 1), :, :].rearrange("a (k p) f -> p (a k) f", p=P)
                             ).then_inc(q["wu_ld"][s], 16)
                if down_free:
                    sp.wait_ge(*down_free)
                sp.dma_start(wd[s], t["w_down"][L, bass.ds(e, 1), :, :].rearrange("a (k p) d -> p (a k) d", p=P)
                             ).then_inc(q["wd_ld"][s], 16)

            for L in range(2):
                q = S[L]
                if L == 0:
                    load_expert(0, 0, 1, gate_free=(spv_ps, DB))
                    load_expert(0, 1, 0, gate_free=(mix_ps, NT))
                else:
                    load_expert(1, 0, 1, (S[0]["gate_ps"][0], nh), (S[0]["up_ps"][0], nh), (S[0]["down_ps"][0], nh))
                    load_expert(1, 1, 0, (S[0]["gate_ps"][1], nh), (S[0]["up_ps"][1], nh), (S[0]["down_ps"][1], nh))
                    sp.wait_ge(ln_out[0], 2 * NT)
                    sp.dma_start(t["o_pool_p"][0, 0, :, :], X[P - CTX:P, 3, :]).then_inc(pool_out, 16)
                    sp.dma_start(t["o_pool_s"][0, :, CTX - 1, :], X[0:DB, 4, :]).then_inc(pool_out, 16)
                sp.wait_ge(tab_set, 2 * L + 2)
                nh = sp.value_load(n_half[0:1, 0:1], min_val=E // 2, max_val=TILES // 2)
                with sp.Fori(1, nh) as u:
                    for s in range(2):
                        ex = sp.value_load(tile_ids[0:1, bass.ds(2 * u + s, 1)], min_val=0, max_val=E - 1)
                        load_expert(L, ex, 1 - s, (q["gate_ps"][s], u), (q["up_ps"][s], u), (q["down_ps"][s], u))
            for i in range(4):
                sp.wait_ge(ln_out[1], NT + i + 1)
                sp.dma_start(t["o_y_p"][0, P * i:P * (i + 1), :], X[:, i, :]).then_inc(out_st, 16)
            sp.wait_ge(ln_out[1], 2 * NT)
            sp.dma_start(t["o_y_s"][:, 0, :], X[0:DB, 4, :]).then_inc(out_st, 16)
            sp.wait_ge(out_st, 16 * (1 + 5))
            sp.wait_ge(pool_out, 32)

        @block.tensor
        def _(pe):
            turns = [0]

            def turn():
                n = turns[0]
                turns[0] += 1
                if n >= 3:
                    pe.wait_ge(turn_ev, n - 2)
                return turn_bank[n % 3]

            def transpose_x(i, g, b):
                n = rows_of(i)
                for kk in range(4):
                    last = nc.tensor.transpose(bank(b, 4, P)[:, kk, 0:n], X[0:n, i, P * (4 * g + kk):P * (4 * g + kk + 1)],
                                               ident[0:n, 0:n])
                return last

            pe.wait_ge(c_ld, 16)
            for i in range(NT):
                pe.wait_ge(x_ld[i], 16)
                for g in range(2):
                    n = 2 * i + g
                    if n >= 4:
                        pe.wait_ge(xt_ev[g], (n - 4) // 2 + 1)
                    transpose_x(i, g, n % 4).then_inc(xt_ps, 1)
            pe.wait_ge(wdq_ld, 16)
            for g in range(2):
                pe.wait_ge(xt_ev[g], NT)
            for m in range(MQ):
                for hf in range(2):
                    n = 2 * m + hf
                    if n >= 4:
                        pe.wait_ge(cq_copied, n - 3)
                    for k in range(KD):
                        last = nc.tensor.matmul(bank(n % 4, HALF), wdq[:, k, P * m:P * (m + 1)],
                                                XT[:, k, HALF * hf:HALF * (hf + 1)], start=(k == 0), stop=(k == KD - 1))
                    last.then_inc(cq_ps, 1)
            pe.wait_ge(wdkv_ld, 16)
            for i in range(NT):
                n = rows_of(i)
                if i >= 2:
                    pe.wait_ge(kv_ready, i - 1)
                for k in range(KD):
                    last = nc.tensor.matmul(bank(4 + i % 2, KVL + ROPE)[0:n, :], XT[:, k, P * i:P * i + n], wdkv[:, k, :],
                                            start=(k == 0), stop=(k == KD - 1))
                last.then_inc(kv_ps, 1)
            pe.wait_ge(cq_squared, 2 * MQ)
            pe.wait_ge(cq_copied, 2 * MQ)
            for hf in range(2):
                for m in range(MQ):
                    last = nc.tensor.matmul(bank(hf, HALF), ones, sq[:, m, HALF * hf:HALF * (hf + 1)],
                                            start=(m == 0), stop=(m == MQ - 1))
                last.then_inc(cq_sum, 1)
            for i in range(NT):
                n = rows_of(i)
                if i == 0:
                    pe.wait_ge(kv_ready, NT)
                    pe.wait_ge(kr_ready, 2)
                if i >= 2:
                    pe.wait_ge(ck_ev, i - 1)
                out = bank(6 + i % 2, 3, P)
                for c in range(MKV):
                    nc.tensor.transpose(out[:, c, 0:n], ckv[0:n, i, P * c:P * (c + 1)], ident[0:n, 0:n])
                nc.tensor.transpose(out[:, 2, 0:n], kdup[0:n, i, :, :].rearrange("p a b -> p (a b)"), ident[0:n, 0:n]
                                    ).then_inc(ck_ps, 1)

            def project_q(parity, hf, b):
                for m in range(MQ):
                    last = nc.tensor.matmul(bank(b, HALF), wuq[:, m, P * parity:P * (parity + 1)],
                                            cq[:, m, HALF * hf:HALF * (hf + 1)], start=(m == 0), stop=(m == MQ - 1))
                last.then_inc(q_ps, 1)

            def project_even(j, first):
                pe.wait_ge(wq_even, j + 1)
                if not first:
                    pe.wait_ge(act_ev, 4 * j - 1)
                project_q(0, 0, 4)
                project_q(0, 1, 7)
                pe.wait_ge(q_ev, 4 * j + 1)
                for i in range(4):
                    for c in range(MKV):
                        last = nc.tensor.matmul(bank(4, 4, P)[:, i, :], ckT[:, c, P * i:P * (i + 1)],
                                                wuv[:, c, bass.ds(P * j, P)], start=(c == 0), stop=(c == MKV - 1))
                last.then_inc(for_act, 1)

            def project_odd(j, first):
                pe.wait_ge(wq_odd, j + 1)
                pe.wait_ge(q_ev, 4 * j + 2)
                project_q(1, 0, 7)
                pe.wait_ge(act_ev, 1 if first else 4 * j)
                project_q(1, 1, 4)
                pe.wait_ge(q_ev, 4 * j + 3)
                pe.wait_ge(wuk_ld, 16 * (j + 1))
                for c in range(MKV):
                    last = nc.tensor.matmul(bank(7), wuk[:, c, :], ckT[:, c, 0:SEQ], start=(c == 0), stop=(c == MKV - 1))
                last.then_inc(for_act, 1)
                pe.wait_ge(q_ev, 4 * j + 4)
                for c in range(MKV):
                    last = nc.tensor.transpose(bank(4, MKV, P)[:, c, :], wuk[:, c, :], ident)
                last.then_inc(for_act, 1)

            def scores(par):
                for i in (3, 2, 1, 0):
                    nc.tensor.matmul(score(i), qT[par][:, P * i:P * (i + 1)], kT[par][:, 0:P * (i + 1)],
                                     start=True, stop=True).then_inc(s_ps, 1)

            def attend(p, par):
                def turned(i):
                    hold(pe, exp_set, 8 * p + 4 * par + 4 - i)
                    for k in range(i + 1):
                        last = nc.tensor.transpose(bank(5 + i % 2, 4, P)[:, k, :], prob[:, i, P * k:P * (k + 1)], ident)
                    last.then_inc(t_ps, 1)

                def weighed(i):
                    hold(pe, pt_ev[i % 2], 4 * p + 2 * par + (3 - i) // 2 + 1)
                    for k in range(i + 1):
                        last = nc.tensor.matmul(bank(3, 4, VH, off=256 * par)[:, i, :], probT[:, i % 2, P * k:P * (k + 1)],
                                                V[:, k, bass.ds(P * p + VH * par, VH)], start=(k == 0), stop=(k == i))
                    return last

                turned(3)
                turned(2)
                if par:
                    pe.wait_ge(o_ev, 2 * p + 1)
                weighed(3)
                turned(1)
                weighed(2)
                turned(0)
                weighed(1)
                weighed(0).then_inc(o_ps, 1)

            def turn_heads(p):
                pe.wait_ge(o_ev, 2 * p + 2)
                for i in range(4):
                    last = nc.tensor.transpose(bank(7, 4, P)[:, i, :], osb[:, i, :], ident)
                last.then_inc(for_act, 1)

            def pair(p, more):
                pe.wait_ge(q_ev, 4 * p + 4)
                pe.wait_ge(act_ev, 4 * p + 2)
                for par, project in ((0, project_even), (1, project_odd)):
                    scores(par)
                    if more:
                        project(p + 1, False)
                    attend(p, par)
                if more:
                    pe.wait_ge(act_ev, 4 * p + 5)
                turn_heads(p)

            pe.wait_ge(cq_done, 1)
            pe.wait_ge(ck_ev, NT)
            pe.wait_ge(wuv_ld, 16)
            pe.wait_ge(krope_set, 1)
            project_even(0, True)
            project_odd(0, True)
            with pe.Fori(0, PAIRS - 1) as p:
                pair(p, True)
            pe.wait_ge(act_ev, 4 * PAIRS - 1)
            pair(PAIRS - 1, False)

            for j in range(PAIRS):
                for c in range(MKV):
                    last = nc.tensor.matmul(bank(3, MKV, PAIRS, 16)[:, c, j, :], wukT[:, j, P * c:P * (c + 1)], qs[:, j, :],
                                            start=True, stop=True)
            last.then_inc(ql_ps, 1)

            def turn_pages(b, s, first=False):
                pe.wait_ge(page_ld[s], 256 * ((b + 2 - s) // 2) if isinstance(b, int) else 128 * (b + 2 - s))
                n = 0
                for c in range(3):
                    if c == MKV:
                        pe.wait_ge(kr_dup, b + 1)
                    for hf in range(2):
                        if not first or n >= 2:
                            pe.wait_ge(tp_ev[n % 2], 3 * b + n // 2)
                        for a in range(4):
                            pg = 4 * hf + a
                            src = (ckp[s][:, pg, P * c:P * (c + 1)] if c < MKV
                                   else krp[s][:, pg, :, :].rearrange("p a b -> p (a b)"))
                            last = nc.tensor.transpose(bank(4 + n % 2, 4, P)[:, a, :], src, ident)
                        last.then_inc(tp_ps, 1)
                        n += 1

            def sample(b, s, more):
                pe.wait_ge(tp_ev[0], 3 * b + 3)
                pe.wait_ge(tp_ev[1], 3 * b + 3)
                pe.wait_ge(qb_set, b + 1)
                for hf in range(2):
                    for c in range(3):
                        nc.tensor.matmul(bank(hf)[0:H, :], qb[s][:, c, :], kpT[s][:, c, 512 * hf:512 * (hf + 1)],
                                         start=(c == 0), stop=(c == 2))
                for c in range(3):
                    last = nc.tensor.matmul(bank(2, DB)[0:H, :], qb[s][:, c, :], ckT[:, c, SEQ:TOK], start=(c == 0), stop=(c == 2))
                last.then_inc(sc_ps, 1)
                if more:
                    turn_pages(b + 1, 1 - s)
                hold(pe, sp_ready, b + 1)
                for n in range(NPAGES):
                    nc.tensor.transpose(bank(6, NPAGES + 1, H)[:, n, :], ps_s[0:H, P * n:P * (n + 1)], ident[0:H, 0:H])
                nc.tensor.transpose(bank(6, NPAGES + 1, H)[0:DB, NPAGES, :], ps_s[0:H, PAST:PAST + DB], ident[0:H, 0:H]
                                    ).then_inc(spT_ps, 1)
                pe.wait_ge(spT_ev, b + 1)
                for c in range(MKV):
                    for n in range(NPAGES):
                        nc.tensor.matmul(bank(7, MKV, H)[:, c, :], ckp[s][:, n, P * c:P * (c + 1)], psT_s[:, n, :],
                                         start=(n == 0), stop=False)
                    last = nc.tensor.matmul(bank(7, MKV, H)[:, c, :], ckv[0:DB, 4, P * c:P * (c + 1)], psT_s[0:DB, NPAGES, :],
                                            start=False, stop=True)
                last.then_inc(spv_ps, 1)

            turn_pages(0, 0, first=True)
            with pe.Fori(0, DB // 2 - 1) as u:
                sample(2 * u, 0, True)
                sample(2 * u + 1, 1, True)
            sample(DB - 2, 0, True)
            sample(DB - 1, 1, False)
            pe.wait_ge(ol_ev, DB)
            for j in range(PAIRS):
                for c in range(MKV):
                    last = nc.tensor.matmul(bank(3, PAIRS, DB, 2)[:, j, :, :], wuv[:, c, P * j:P * (j + 1)],
                                            olat[:, c, :, 2 * j:2 * j + 2], start=(c == 0), stop=(c == MKV - 1))
            last.then_inc(uv_ps, 1)

            def mix(L, i):
                n, b0 = rows_of(i), 2 * (i % 2)
                if i >= 2:
                    pe.wait_ge(ln_z[L], i - 1)
                if L == 0:
                    for hf in range(2):
                        for k in range(KD):
                            last = nc.tensor.matmul(bank(b0 + hf)[0:n, :], oT[:, k, P * i:P * i + n],
                                                    wo[:, k, 512 * hf:512 * (hf + 1)], start=(k == 0), stop=(k == KD - 1))
                else:
                    for g in range(4):
                        for kk in range(2):
                            last = nc.tensor.matmul(view(PS, 512 * b0 + 256 * g, 256)[0:n, :],
                                                    poolT[:, 2 * g + kk, P * i:P * i + n], wpool[:, 2 * g + kk, :],
                                                    start=(kk == 0), stop=(kk == 1))
                last.then_inc(mix_ps, 1)

            def pool(i):
                pe.wait_ge(ln_out[0], NT + i + 1)
                if i < 4:
                    for g in range(2):
                        b = turn()
                        for c in range(4):
                            k = 4 * g + c
                            out = bank(b, 4, P)[:, c, :]
                            last = nc.tensor.matmul(out, X[:, i, P * k:P * (k + 1)], band[:, min(i, 1), k // 2, 0:P],
                                                    start=True, stop=(i == 0))
                            if i:
                                last = nc.tensor.matmul(out[:, 0:CTX], X[:, i - 1, P * k:P * (k + 1)], band[:, 1, k // 2, P:BAND],
                                                        start=False, stop=True)
                        last.then_inc(turn_ps, 1)
                else:
                    b = turn()
                    pe.wait_ge(st_ld, 32)
                    for k in range(KD):
                        out = bank(b, KD, DB)[:, k, :]
                        nc.tensor.matmul(out, state[0:DB * CTX, P * k:P * (k + 1)], band_s[0:DB * CTX, k // 2, :],
                                         start=True, stop=False)
                        last = nc.tensor.matmul(out, X[0:DB, 4, P * k:P * (k + 1)], own_s[0:DB, k // 2, :],
                                                start=False, stop=True)
                    last.then_inc(turn_ps, 1)

            def router(L, i):
                n = rows_of(i)
                pe.wait_ge(ln_out[L], i + 1)
                for g in range(2):
                    transpose_x(i, g, turn()).then_inc(turn_ps, 1)
                pe.wait_ge(turn_ev, turns[0])
                if i == 0:
                    pe.wait_ge(lg_zero, L + 1)
                for k in range(KD):
                    last = nc.tensor.matmul(bank(6, NT, E)[0:n, i, :], XT[:, k, P * i:P * i + n], wr[:, k, :],
                                            start=(k == 0), stop=(k == KD - 1))
                if i == NT - 1:
                    last.then_inc(lg_ps, 1)

            def counts(L):
                pe.wait_ge(sel_set, L + 1)
                cum = bank(6, NT, E, off=128)
                selt = r_sel.rearrange("p (a b) -> p a b", a=NT)
                nc.tensor.matmul(cum, before, selt, start=True, stop=False)
                for j in range(NT - 1):
                    nc.tensor.matmul(cum[:, j + 1:NT, :], ones, selt[:, j:j + 1, :].to_broadcast([P, NT - 1 - j, E]),
                                     start=False, stop=(j == NT - 2))
                for j in range(NT):
                    last = nc.tensor.matmul(bank(6, E, off=256), ones, selt[:, j, :], start=(j == 0), stop=(j == NT - 1))
                last.then_inc(cnt_ps, 1)

            def experts(L):
                q = S[L]

                def turn_rows(tl, s):
                    for g in range(2):
                        for c in range(4):
                            k = 4 * g + c
                            last = nc.tensor.transpose(bank(6 + g, 4, CAP)[:, c, :], xe[s][0:CAP, P * k:P * (k + 1)],
                                                       ident[0:CAP, 0:CAP])
                        last.then_inc(q["tr_ps"], 1)

                def tile(u, s):
                    tl = 2 * u + s
                    w = 1 - s
                    pe.wait_ge(q["xeT_set"], 2 * tl + 2)
                    pe.wait_ge(q["wg_ld"][w], 16 * (u + 1))
                    for f in range(KF):
                        for k in range(KD):
                            last = nc.tensor.matmul(bank(s, KF, CAP)[:, f, :], wg[w][:, k, P * f:P * (f + 1)], xeT[s][:, k, :],
                                                    start=(k == 0), stop=(k == KD - 1))
                    last.then_inc(q["gate_ps"][s], 1)
                    pe.wait_ge(q["wu_ld"][w], 16 * (u + 1))
                    for f in range(KF):
                        for k in range(KD):
                            last = nc.tensor.matmul(bank(2 + s, KF, CAP)[:, f, :], wu[w][:, k, P * f:P * (f + 1)], xeT[s][:, k, :],
                                                    start=(k == 0), stop=(k == KD - 1))
                    last.then_inc(q["up_ps"][s], 1)
                    pe.wait_ge(q["xe_ld"][1 - s], 16 * (u + 1 + s))
                    turn_rows(tl + 1, 1 - s)
                    pe.wait_ge(q["h_set"], tl + 1)
                    pe.wait_ge(q["wd_ld"][w], 16 * (u + 1))
                    pe.wait_ge(q["y_set"], 2 * tl + 2)
                    for hf in range(2):
                        for f in range(KF):
                            last = nc.tensor.matmul(bank(4 + hf)[0:CAP, :], h[s][:, f, :], wd[w][:, f, 512 * hf:512 * (hf + 1)],
                                                    start=(f == 0), stop=(f == KF - 1))
                    last.then_inc(q["down_ps"][s], 1)

                pe.wait_ge(tab_set, 2 * L + 2)
                nh = pe.value_load(n_half[0:1, 0:1], min_val=E // 2, max_val=TILES // 2)
                pe.wait_ge(turn_ev, turns[0])
                pe.wait_ge(q["xe_ld"][0], 16)
                turn_rows(0, 0)
                with pe.Fori(0, nh) as u:
                    for s in range(2):
                        tile(u, s)

            pe.wait_ge(wo_ld, 16)
            pe.wait_ge(act_ev, 4 * PAIRS)
            pe.wait_ge(router_ld, 32)
            pe.wait_ge(uv_ev, 1)
            for step in range(NT + 1):
                if step < NT:
                    mix(0, step)
                if step >= 1:
                    router(0, step - 1)
            counts(0)
            experts(0)
            for step in range(NT + 2):
                if step < NT:
                    pool(step)
                if 1 <= step <= NT:
                    pe.wait_ge(turn_ev, turns[0] - (0 if step == NT else 1 if step == NT - 1 else 2))
                    if step == 1:
                        pe.wait_ge(wp_ready, 1)
                    mix(1, step - 1)
                if step >= 2:
                    router(1, step - 2)
            counts(1)
            experts(1)

        @block.gpsimd
        def _(pool_e):
            nc.gpsimd.memset(zero_src, 0.0).then_inc(zero_set, 1)

            def copy_even():
                nc.gpsimd.tensor_copy(wuq[:, :, 0:HQ], wqn[:, :, 0:HQ])
                nc.gpsimd.tensor_copy(wuq[:, :, 96:112], wqn[:, :, 80:96])
                nc.gpsimd.tensor_copy(wuq[:, :, 112:128], wqn[:, :, 64:80]).then_inc(wq_even, 1)

            def copy_odd():
                nc.gpsimd.tensor_copy(wuq[:, :, 128:160], wqn[:, :, 160:192])
                nc.gpsimd.tensor_copy(wuq[:, :, 160:176], wqn[:, :, 176:192])
                nc.gpsimd.tensor_copy(wuq[:, :, 176:192], wqn[:, :, 160:176])
                nc.gpsimd.tensor_copy(wuq[:, :, 192:256], wqn[:, :, 96:160]).then_inc(wq_odd, 1)

            hold(pool_e, wqn_ld, 16)
            copy_even()
            copy_odd()
            with pool_e.Fori(1, PAIRS) as j:
                hold(pool_e, wqn_ld, 16 * (j + 1))
                hold(pool_e, q_ps, 4 * j - 2)
                copy_even()
                hold(pool_e, q_ps, 4 * j)
                copy_odd()
            def repeat_keys(b, s):
                hold(pool_e, page_ld[s], 256 if isinstance(b, int) else 128 * (b + 2 - s))
                nc.gpsimd.tensor_copy(krp[s][:, :, 1:4, :], krp[s][:, :, 0:1, :].to_broadcast([P, NPAGES, 3, ROPE])
                                      ).then_inc(kr_dup, 1)

            repeat_keys(0, 0)
            repeat_keys(1, 1)
            with pool_e.Fori(1, DB // 2) as u:
                repeat_keys(2 * u, 0)
                repeat_keys(2 * u + 1, 1)
            hold(pool_e, uv_ps, 1)
            pool_e.dma_start(wpool, t["w_pool"][0].rearrange("g (k p) d -> p (g k) d", p=P)).then_inc(wp_ld, 16)

            def shift(L, which, i):
                n = rows_of(i)
                if i == 0:
                    hold(pool_e, gb_ld[L][which], 32)
                hold(pool_e, ln_gam[L], NT * which + i + 1)
                nc.gpsimd.tensor_tensor(X[0:n, i, :], X[0:n, i, :], gb[0:n, 2 * which + 1, :], ALU.add).then_inc(ln_out[L], 1)

            for L in range(2):
                q = S[L]
                if L == 0:
                    for i in range(NT):
                        shift(0, 0, i)
                hold(pool_e, idx_set, 2 * (L + 1))
                hold(pool_e, zero_st, 32)
                hold(pool_e, ln_out[L], NT)
                for i in range(NT):
                    for idx in (idx_a, idx_b):
                        pool_e.indirect_dma_start(
                            xs[:, :], bass.IndirectOffsetOnAxis(ap=idx[0:rows_of(i), i:i + 1], axis=0),
                            X[0:rows_of(i), i, :], None).then_inc(scat, 16)
                if L == 0:
                    pool_e.dma_start(gb[:, 0, :], bcast(t["ln1_g"][1])).then_inc(gb_ld[1][0], 16)
                    pool_e.dma_start(gb[:, 1, :], bcast(t["ln1_b"][1])).then_inc(gb_ld[1][0], 16)
                hold(pool_e, scat, 160 * (L + 1))
                hold(pool_e, tab_set, 2 * L + 2)
                nh = pool_e.value_load(n_half[0:1, 0:1], min_val=E // 2, max_val=TILES // 2)
                hold(pool_e, turn_ev, 10 if L == 0 else 29)
                pool_e.dma_start(xe[0][0:CAP, :], xs[0:CAP, :]).then_inc(q["xe_ld"][0], 16)
                with pool_e.Fori(0, nh) as u:
                    for s in range(2):
                        tl = 2 * u + s
                        hold(pool_e, q["tr_ps"], 2 * tl + 2)
                        pool_e.dma_start(xe[1 - s][0:CAP, :], xs[bass.ds(CAP * (tl + 1), CAP), :]).then_inc(q["xe_ld"][1 - s], 16)
                        hold(pool_e, q["y_set"], 2 * tl + 4)
                        pool_e.dma_start(yd[bass.ds(CAP * tl, CAP), :], ys[s][0:CAP, :]).then_inc(q["y_st"][s], 16)
                for s in range(2):
                    hold(pool_e, q["y_st"][s], 16 * nh)

                def gather(i):
                    n, s = rows_of(i), i % 2
                    if i >= 2:
                        hold(pool_e, ln_z[L], NT + i - 1)
                    for idx, y in ((idx_a, ya), (idx_b, yb)):
                        pool_e.indirect_dma_start(y[s][0:n, :], None, yd[:, :],
                                                  bass.IndirectOffsetOnAxis(ap=idx[0:n, i:i + 1], axis=0)).then_inc(gath[s], 16)

                gather(0)
                gather(1)
                if L == 0:
                    hold(pool_e, q["tr_ps"], 4 * nh + 2)
                    pool_e.dma_start(pscale, bcast(t["pool_scale"][0])).then_inc(st_ld, 16)
                    pool_e.dma_start(state[0:DB * CTX, :], t["state_pool"][0].rearrange("b c d -> (b c) d")).then_inc(st_ld, 16)
                for step in range(NT if L else NT + 2):
                    if step + 2 < NT:
                        gather(step + 2)
                    if step < NT:
                        shift(L, 1, step)
                    if L == 0 and step >= 2:
                        shift(1, 0, step - 2)
                if L == 0:
                    hold(pool_e, ln_out[0], 2 * NT)
                    pool_e.dma_start(gb[:, 2, :], bcast(t["ln2_g"][1])).then_inc(gb_ld[1][1], 16)
                    pool_e.dma_start(gb[:, 3, :], bcast(t["ln2_b"][1])).then_inc(gb_ld[1][1], 16)

        @block.scalar
        def _(act):
            act.wait_ge(kraw_zero, 1)
            for i in range(NT):
                act.wait_ge(xt_ps, 2 * i + 2)
                nc.scalar.activation(XT[:, 4:8, P * i:P * i + rows_of(i)], bank((2 * i + 1) % 4, 4, P)[:, :, 0:rows_of(i)],
                                     ACT.Copy).then_inc(xt_ev[1], 1)
            for n in range(2 * MQ):
                act.wait_ge(cq_copied, n + 1)
                part = (slice(None), n // 2, slice(HALF * (n % 2), HALF * (n % 2 + 1)))
                nc.scalar.activation(sq[part], cq[part], ACT.Square).then_inc(cq_squared, 1)
            act.wait_ge(c_ld, 16)
            for i in range(NT):
                n = rows_of(i)
                raw = bank(4 + i % 2, KVL + ROPE)[0:n, :]
                act.wait_ge(kv_ps, i + 1)
                nc.scalar.activation(kraw[0:n, i, :], raw[:, KVL:], ACT.Copy)
                nc.scalar.activation(sqj[0:n, :], raw[:, 0:KVL], ACT.Square, accum_out=ss[0:n, i:i + 1]).then_inc(kv_ss, 1)
                act.wait_ge(kv_ss, i + 1)
                nc.scalar.activation(kstd[0:n, i:i + 1], ss[0:n, i:i + 1], ACT.Sqrt, scale=1.0 / KVL, bias=rms_eps[0:n, :]
                                     ).then_inc(kv_std, 1)
            for hf in range(2):
                act.wait_ge(cq_sum, hf + 1)
                nc.scalar.activation(rq[:, HALF * hf:HALF * (hf + 1)], bank(hf, HALF), ACT.Sqrt, scale=1.0 / QL,
                                     bias=rms_eps).then_inc(rq_std, 1)
            for i in range(NT):
                n = rows_of(i)
                act.wait_ge(ck_ps, i + 1)
                nc.scalar.activation(ckT[:, :, P * i:P * i + n], bank(6 + i % 2, 3, P)[:, :, 0:n], ACT.Copy).then_inc(ck_ev, 1)

            def take_v(j, n):
                act.wait_ge(for_act, n)
                nc.scalar.activation(V[:, :, bass.ds(P * j, P)], bank(4, 4, P), ACT.Copy).then_inc(act_ev, 1)

            def take_k(j, n):
                act.wait_ge(for_act, n)
                nc.scalar.activation(kT[0][0:64, :], bank(7)[0:64, :], ACT.Copy)
                nc.scalar.activation(kT[1][64:128, :], bank(7)[64:128, :], ACT.Copy).then_inc(act_ev, 1)
                act.wait_ge(for_act, n + 1)
                nc.scalar.activation(wukT[:, bass.ds(j, 1), :], bank(4, 1, KVL), ACT.Copy).then_inc(act_ev, 1)

            def exps(p, par):
                for i in (3, 2, 1, 0):
                    act.wait_ge(min_set, 8 * p + 4 * par + scored(i))
                    c = 4 * par + i
                    nc.scalar.activation(prob[:, i, 0:P * (i + 1)], score(i), ACT.Exp, scale=-1.0,
                                         bias=mneg[:, c:c + 1], accum_out=rsum[:, c:c + 1]).then_inc(exp_set, 1)

            def take_probs(p, par):
                for i in (3, 1):
                    act.wait_ge(t_ps, 8 * p + 4 * par + 4 - i)
                    nc.scalar.activation(probT[:, 1, 0:P * (i + 1)], bank(6, P * (i + 1)), ACT.Copy).then_inc(pt_ev[1], 1)

            def pair(p, more):
                exps(p, 0)
                if more:
                    take_v(p + 1, 4 * p + 4)
                take_probs(p, 0)
                exps(p, 1)
                if more:
                    take_k(p + 1, 4 * p + 5)
                take_probs(p, 1)
                act.wait_ge(for_act, 4 * p + 7 if more else 4 * PAIRS)
                nc.scalar.activation(oT[:, bass.ds(p, 1), 0:SEQ], bank(7, 1, SEQ), ACT.Copy).then_inc(act_ev, 1)

            act.wait_ge(rq_std, 2)
            act.wait_ge(cq_done, 1)
            act.wait_ge(latent_st, 16 * 10)
            take_v(0, 1)
            take_k(0, 2)
            act.wait_ge(zero_st, 32)
            with act.Fori(0, PAIRS - 1) as p:
                pair(p, True)
            pair(PAIRS - 1, False)

            def take_pages(b, s):
                for n in (1, 3, 5):
                    act.wait_ge(tp_ps, 6 * b + n + 1)
                    nc.scalar.activation(kpT[s][:, n // 2, 512:1024], bank(5), ACT.Copy).then_inc(tp_ev[1], 1)

            def sample(b, s, more):
                act.wait_ge(smin_set, b + 1)
                nc.scalar.activation(ps_s[0:H, :], view(PS, 0, PAST + DB)[0:H, :], ACT.Exp, scale=-1.0,
                                     bias=s_mneg[0:H, s:s + 1], accum_out=s_sum[0:H, s:s + 1]).then_inc(sexp_set, 1)
                if more:
                    take_pages(b + 1, 1 - s)
                act.wait_ge(spv_ps, b + 1)
                nc.scalar.activation(olat[:, :, bass.ds(b, 1), :], bank(7, MKV, 1, H), ACT.Copy).then_inc(ol_ev, 1)

            take_pages(0, 0)
            with act.Fori(0, DB // 2 - 1) as u:
                sample(2 * u, 0, True)
                sample(2 * u + 1, 1, True)
            sample(DB - 2, 0, True)
            sample(DB - 1, 1, False)

            turns = [0]

            def take_turn(dst, src_dims, cols=None):
                n = turns[0]
                turns[0] += 1
                act.wait_ge(turn_ps, n + 1)
                src = bank(turn_bank[n % 3], *src_dims)
                nc.scalar.activation(dst, src if cols is None else src[:, :, 0:cols], ACT.Copy).then_inc(turn_ev, 1)

            def normalise(L, which, i):
                n = rows_of(i)
                k = NT * which + i + 1
                act.wait_ge(ln_agg[L], k)
                nc.scalar.activation(std[0:n, i:i + 1], mv[0:n, i, 1:2], ACT.Sqrt, bias=ln_eps[0:n, :]).then_inc(ln_std[L], 1)
                act.wait_ge(ln_rstd[L], k)
                nc.scalar.activation(X[0:n, i, :], X[0:n, i, :], ACT.Identity, scale=rstd[0:n, i:i + 1],
                                     bias=nmr[0:n, i:i + 1]).then_inc(ln_nrm[L], 1)

            def take_rows(i):
                for g in range(2):
                    take_turn(XT[:, 4 * g:4 * g + 4, P * i:P * i + rows_of(i)], (4, P), rows_of(i))

            def experts(L):
                q = S[L]
                act.wait_ge(lg_ps, L + 1)
                nc.scalar.activation(r_exp, bank(6, NT * E), ACT.Exp, scale=-1.0).then_inc(lg_exp, 1)
                act.wait_ge(scat, 160 * (L + 1))
                for i in range(NT):
                    n = rows_of(i)
                    nc.scalar.activation(X[0:n, i, :], X[0:n, i, :], ACT.Copy, scale=ALPHA).then_inc(xscaled, 1)
                act.wait_ge(tab_set, 2 * L + 2)
                nh = act.value_load(n_half[0:1, 0:1], min_val=E // 2, max_val=TILES // 2)
                act.sem_inc(q["y_set"], 1)
                act.wait_ge(q["tr_ps"], 1)
                nc.scalar.activation(xeT[0][:, 0:4, :], bank(6, 4, CAP), ACT.Copy).then_inc(q["xeT_set"], 1)

                def tile(u, s, stored):
                    tl = 2 * u + s
                    act.wait_ge(q["gate_ps"][s], u + 1)
                    nc.scalar.activation(sg[s], bank(s, KF, CAP), ACT.Silu).then_inc(q["sg_set"], 1)
                    act.wait_ge(q["tr_ps"], 2 * tl + 3)
                    nc.scalar.activation(xeT[1 - s][:, 0:4, :], bank(6, 4, CAP), ACT.Copy).then_inc(q["xeT_set"], 1)
                    act.wait_ge(q["down_ps"][s], u + 1)
                    if stored:
                        act.wait_ge(q["y_st"][s], 16 * u)
                    nc.scalar.activation(ys[s][0:CAP, 0:512], bank(4)[0:CAP, :], ACT.Copy).then_inc(q["y_set"], 1)

                tile(0, 0, False)
                tile(0, 1, False)
                with act.Fori(1, nh) as u:
                    tile(u, 0, True)
                    tile(u, 1, True)

            for step in range(NT + 1):
                if step < NT:
                    normalise(0, 0, step)
                if step:
                    take_rows(step - 1)
            experts(0)
            for step in range(2 * NT):
                if step < NT:
                    normalise(0, 1, step)
                if 1 <= step <= NT:
                    i = step - 1
                    if i < 4:
                        for g in range(2):
                            take_turn(poolT[:, 4 * g:4 * g + 4, P * i:P * (i + 1)], (4, P))
                    else:
                        take_turn(poolT[:, :, SEQ:TOK], (KD, DB))
                if 2 <= step <= NT + 1:
                    normalise(1, 0, step - 2)
                if step == 3:
                    act.wait_ge(ln_z[0], 2 * NT)
                if 3 <= step <= NT + 2:
                    take_rows(step - 3)
            experts(1)
            for i in range(NT):
                normalise(1, 1, i)

        @block.vector
        def _(dve):
            chain = [0]

            def link(ins):
                chain[0] += 1
                ins.then_inc(dve_step, 1)
                dve.wait_ge(dve_step, chain[0])

            v = nc.vector
            v.memset(kraw[:, 4, :], 0.0).then_inc(kraw_zero, 1)
            v.memset(qs, 0.0)
            link(v.memset(qr, 0.0))
            for i in range(NT):
                dve.wait_ge(xt_ps, 2 * i + 1)
                v.tensor_copy(XT[:, 0:4, P * i:P * i + rows_of(i)], bank((2 * i) % 4, 4, P)[:, :, 0:rows_of(i)]).then_inc(xt_ev[0], 1)
            for n in range(2 * MQ):
                dve.wait_ge(cq_ps, n + 1)
                v.tensor_copy(cq[:, n // 2, HALF * (n % 2):HALF * (n % 2 + 1)], bank(n % 4, HALF)).then_inc(cq_copied, 1)
            dve.wait_ge(gain_ld, 32)
            dve.wait_ge(c_ld, 16)
            for i in range(NT):
                n = rows_of(i)
                dve.wait_ge(kv_std, i + 1)
                link(v.reciprocal(krs[0:n, i:i + 1], kstd[0:n, i:i + 1]))
                v.scalar_tensor_tensor(out=ckv[0:n, i, :], in0=bank(4 + i % 2, KVL)[0:n, :], scalar=krs[0:n, i:i + 1],
                                       in1=gkv[0:n, :], op0=ALU.mult, op1=ALU.mult).then_inc(kv_ready, 1)
            half = ROPE // 2
            x1, x2 = kraw[:, :, 0:half], kraw[:, :, half:ROPE]
            tmp = [rtmp[:, a, :].rearrange("p (a b) -> p a b", a=NT) for a in range(4)]
            v.tensor_tensor(tmp[0], x1, cos_k, ALU.mult)
            v.tensor_tensor(tmp[1], x2, sin_k, ALU.mult)
            v.tensor_tensor(tmp[2], x1, sin_k, ALU.mult)
            link(v.tensor_tensor(tmp[3], x2, cos_k, ALU.mult))
            v.tensor_tensor(krot[:, :, 0:half], tmp[0], tmp[1], ALU.subtract)
            v.tensor_tensor(krot[:, :, half:ROPE], tmp[2], tmp[3], ALU.add).then_inc(kr_ready, 1)
            dve.wait_ge(kr_ready, 1)
            v.tensor_copy(kdup, krot.unsqueeze(2).to_broadcast([P, NT, 4, ROPE])).then_inc(kr_ready, 1)
            dve.wait_ge(rq_std, 2)
            link(v.reciprocal(rq, rq))
            for m in range(MQ):
                ins = v.scalar_tensor_tensor(out=cq[:, m, :], in0=cq[:, m, :], scalar=gq[:, m:m + 1], in1=rq, op0=ALU.mult,
                                             op1=ALU.mult)
            ins.then_inc(cq_done, 1)
            dve.wait_ge(ck_ev, 4)
            v.tensor_copy(kT[0][64:128, :], ckT[64:128, 2, 0:SEQ])
            v.tensor_copy(kT[1][0:64, :], ckT[0:64, 2, 0:SEQ]).then_inc(krope_set, 1)

            def take_q(j, parity, hf, n):
                b = 7 if (parity + hf) == 1 else 4
                ps = bank(b, HALF)
                tab = rope_q[:, parity, HALF * hf:HALF * (hf + 1)]
                dve.wait_ge(q_ps, n)
                ins = v.tensor_tensor(qT[parity][:, HALF * hf:HALF * (hf + 1)], ps, tab, ALU.mult)
                if hf:
                    lo, hi = (slice(0, 64), slice(64, 128)) if parity == 0 else (slice(64, 128), slice(0, 64))
                    c = slice(HALF - DB, HALF)
                    v.tensor_tensor(qs[lo, bass.ds(j, 1), DB * parity:DB * (parity + 1)], ps[lo, c].unsqueeze(1),
                                    tab[lo, c].unsqueeze(1), ALU.mult)
                    ins = v.tensor_tensor(qr[hi, :, bass.ds(2 * j + parity, 1)], ps[hi, c].unsqueeze(2),
                                          tab[hi, c].unsqueeze(2), ALU.mult)
                ins.then_inc(q_ev, 1)

            def mins(p, par):
                for i in (3, 2, 1, 0):
                    hold(dve, s_ps, 8 * p + 4 * par + scored(i))
                    w = P * (i + 1)
                    sc = score(i)
                    v.tensor_tensor_reduce(sc, sc, causal[:, SEQ - w:SEQ], 1.0, BIG, ALU.add, ALU.min,
                                           mneg[:, 4 * par + i:4 * par + i + 1]).then_inc(min_set, 1)

            def take_probs(p, par):
                for i in (2, 0):
                    dve.wait_ge(t_ps, 8 * p + 4 * par + 4 - i)
                    v.tensor_copy(probT[:, 0, 0:P * (i + 1)], bank(5, P * (i + 1))).then_inc(pt_ev[0], 1)

            def head_out(p, par):
                dve.wait_ge(exp_set, 8 * p + 4 * par + 4)
                v.reciprocal(rinv[:, 4 * par:4 * par + 4], rsum[:, 4 * par:4 * par + 4]).then_inc(rinv_set, 1)
                dve.wait_ge(rinv_set, 2 * p + par + 1)
                dve.wait_ge(o_ps, 2 * p + par + 1)
                v.tensor_tensor(osb[:, :, VH * par:VH * (par + 1)], bank(3, 4, VH, off=256 * par),
                                rinv[:, 4 * par:4 * par + 4].unsqueeze(2).to_broadcast([P, 4, VH]), ALU.mult).then_inc(o_ev, 1)

            def pair(p, more):
                for par in range(2):
                    mins(p, par)
                    if more:
                        take_q(p + 1, par, 0, 4 * p + 5 + 2 * par)
                        take_q(p + 1, par, 1, 4 * p + 6 + 2 * par)
                    take_probs(p, par)
                    head_out(p, par)

            for par in range(2):
                for hf in range(2):
                    take_q(0, par, hf, 2 * par + hf + 1)
            with dve.Fori(0, PAIRS - 1) as p:
                pair(p, True)
            pair(PAIRS - 1, False)

            dve.wait_ge(ql_ps, 1)
            for c in range(MKV):
                ins = v.tensor_copy(qlat[:, c, :, :].rearrange("p b (j e) -> p j e b", e=2),
                                    bank(3, MKV, PAIRS, 16)[:, c, :, :].rearrange("p j (e b) -> p j e b", e=2))
            ins.then_inc(ql_ev, 1)
            dve.wait_ge(ql_ev, 1)

            def set_qb(b, s):
                v.tensor_copy(qb[s][:, 0:MKV, :].unsqueeze(2), qlat[:, :, bass.ds(b, 1), :])
                v.tensor_copy(qb[s][:, MKV:MKV + 1, :], qr[:, bass.ds(b, 1), :]).then_inc(qb_set, 1)

            def take_pages(b, s):
                for n in (0, 2, 4):
                    dve.wait_ge(tp_ps, 6 * b + n + 1)
                    v.tensor_copy(kpT[s][:, n // 2, 0:512], bank(4)).then_inc(tp_ev[0], 1)

            def sample(b, s, more):
                if more:
                    set_qb(b + 1, 1 - s)
                dve.wait_ge(sc_ps, b + 1)
                v.tensor_tensor(bank(2, 1, DB)[0:H, :, :], bank(2, 1, DB)[0:H, :, :], own_sample[0:H, bass.ds(b, 1), :], ALU.add
                                ).then_inc(new_masked, 1)
                dve.wait_ge(new_masked, b + 1)
                v.tensor_reduce(s_mneg[0:H, s:s + 1], view(PS, 0, PAST + DB)[0:H, :], AXX, ALU.min).then_inc(smin_set, 1)
                if more:
                    take_pages(b + 1, 1 - s)
                dve.wait_ge(sexp_set, b + 1)
                v.reciprocal(s_inv[0:H, s:s + 1], s_sum[0:H, s:s + 1]).then_inc(sinv_set, 1)
                dve.wait_ge(sinv_set, b + 1)
                v.tensor_scalar(ps_s[0:H, :], ps_s[0:H, :], s_inv[0:H, s:s + 1], None, ALU.mult).then_inc(sp_ready, 1)
                dve.wait_ge(spT_ps, b + 1)
                v.tensor_copy(psT_s[:, 0:NPAGES, :], bank(6, NPAGES, H))
                v.tensor_copy(psT_s[0:DB, NPAGES, :], bank(6, NPAGES + 1, H)[0:DB, NPAGES, :]).then_inc(spT_ev, 1)

            set_qb(0, 0)
            take_pages(0, 0)
            with dve.Fori(0, DB // 2 - 1) as u:
                sample(2 * u, 0, True)
                sample(2 * u + 1, 1, True)
            sample(DB - 2, 0, True)
            sample(DB - 1, 1, False)
            dve.wait_ge(uv_ps, 1)
            for e in range(2):
                r = slice(64 * e, 64 * e + 64)
                ins = v.tensor_copy(oT[r, :, SEQ:TOK].unsqueeze(3), bank(3, PAIRS, DB, 2)[r, :, :, e:e + 1])
            ins.then_inc(uv_ev, 1)

            def stats(L, which, i):
                n = rows_of(i)
                k = NT * which + i + 1
                x = X[0:n, i, :]
                if which == 0:
                    dve.wait_ge(mix_ps, NT * L + i + 1)
                    v.scalar_tensor_tensor(out=x, in0=x, scalar=ALPHA, in1=view(PS, 1024 * (i % 2), D)[0:n, :],
                                           op0=ALU.mult, op1=ALU.add).then_inc(ln_z[L], 1)
                else:
                    s = i % 2
                    dve.wait_ge(gath[s], 32 * ((3 * L if s == 0 else 2 * L) + i // 2 + 1))
                    dve.wait_ge(xscaled, NT * L + i + 1)
                    link(v.scalar_tensor_tensor(out=x, in0=ya[s][0:n, :], scalar=ca[0:n, i:i + 1], in1=x,
                                                op0=ALU.mult, op1=ALU.add))
                    v.scalar_tensor_tensor(out=x, in0=yb[s][0:n, :], scalar=cb[0:n, i:i + 1], in1=x,
                                           op0=ALU.mult, op1=ALU.add).then_inc(ln_z[L], 1)
                dve.wait_ge(ln_z[L], k)
                for c in range(2):
                    ins = v.bn_stats(bn[0:n, i, 6 * c:6 * c + 6], X[0:n, i, 512 * c:512 * (c + 1)])
                link(ins)
                v.bn_aggr(mv[0:n, i, :], bn[0:n, i, :]).then_inc(ln_agg[L], 1)

            def spread(L, which, i):
                n = rows_of(i)
                k = NT * which + i + 1
                dve.wait_ge(ln_std[L], k)
                link(v.reciprocal(rstd[0:n, i:i + 1], std[0:n, i:i + 1]))
                v.tensor_scalar(nmr[0:n, i:i + 1], mv[0:n, i, 0:1], rstd[0:n, i:i + 1], -1.0, ALU.mult, ALU.mult).then_inc(ln_rstd[L], 1)

            def gain(L, which, i):
                n = rows_of(i)
                dve.wait_ge(ln_nrm[L], NT * which + i + 1)
                if i == 0:
                    dve.wait_ge(gb_ld[L][which], 32)
                v.tensor_tensor(X[0:n, i, :], X[0:n, i, :], gb[0:n, 2 * which, :], ALU.mult).then_inc(ln_gam[L], 1)

            def layer_norm(L, which):
                for i in range(NT + 1):
                    if i < NT:
                        stats(L, which, i)
                        spread(L, which, i)
                    if i:
                        gain(L, which, i - 1)

            def route(L):
                def five(a):
                    return a.rearrange("p (a b) -> p a b", a=NT)

                def by_group(a):
                    return a.rearrange("p (a b) -> p a b", b=EPG)

                over = [P, NT, E]
                dve.wait_ge(lg_exp, L + 1)
                link(v.tensor_scalar_add(r_exp, r_exp, 1.0))
                link(v.reciprocal(r_s, r_exp))
                if L == 0:
                    dve.wait_ge(router_ld, 32)
                link(v.tensor_tensor(five(r_bias), five(r_s), bias_row.unsqueeze(1).to_broadcast(over), ALU.add))
                b4 = by_group(r_bias)
                sums = r_big[:, 0:120].rearrange("p (a b) -> p a b", b=6)
                v.tensor_tensor(sums[:, :, 0:3], b4[:, :, 0:3], b4[:, :, 1:4], ALU.add)
                v.tensor_tensor(sums[:, :, 3:5], b4[:, :, 0:2], b4[:, :, 2:4], ALU.add)
                link(v.tensor_tensor(sums[:, :, 5:6], b4[:, :, 0:1], b4[:, :, 3:4], ALU.add))
                link(v.tensor_reduce(r_gs, sums, AXX, ALU.max))
                gs, gp, gsel = (a.rearrange("p (a b) -> p a b", a=NT) for a in (r_gs, r_gp, r_gsel))
                link(v.tensor_reduce(r_m, gs, AXX, ALU.max))
                link(v.tensor_tensor(gp, gs, r_m.unsqueeze(2).to_broadcast([P, NT, GROUPS]), ALU.is_equal))
                link(v.tensor_tensor(gp, gp, prefer.unsqueeze(1).to_broadcast([P, NT, GROUPS]), ALU.mult))
                link(v.tensor_reduce(r_m, gp, AXX, ALU.max))
                link(v.tensor_tensor(gsel, gp, r_m.unsqueeze(2).to_broadcast([P, NT, GROUPS]), ALU.is_equal))
                cmp = r_big.rearrange("p (a j i) -> p a j i", j=EPG, i=EPG)
                wide = [P, NT * GROUPS, EPG, EPG]
                bi, bj = b4.unsqueeze(2).to_broadcast(wide), b4.unsqueeze(3).to_broadcast(wide)
                link(v.tensor_tensor(cmp, bi, bj, ALU.is_equal))
                link(v.tensor_tensor(cmp, cmp, earlier.unsqueeze(1).to_broadcast(wide), ALU.mult))
                link(v.tensor_reduce(by_group(r_rank), cmp, AXX, ALU.add))
                link(v.tensor_tensor(cmp, bi, bj, ALU.is_gt))
                link(v.tensor_reduce(by_group(r_comb), cmp, AXX, ALU.add))
                link(v.tensor_tensor(r_rank, r_rank, r_comb, ALU.add))
                link(v.scalar_tensor_tensor(out=by_group(r_sel), in0=by_group(r_rank), scalar=float(2),
                                            in1=r_gsel.unsqueeze(2).to_broadcast([P, NT * GROUPS, EPG]),
                                            op0=ALU.is_lt, op1=ALU.mult))
                link(v.tensor_tensor(r_comb, r_s, r_sel, ALU.mult))
                link(v.tensor_reduce(r_den, five(r_comb), AXX, ALU.add))
                link(v.reciprocal(r_den, r_den))
                link(v.tensor_tensor(five(r_comb), five(r_comb), r_den.unsqueeze(2).to_broadcast(over), ALU.mult))
                v.tensor_scalar(r_sel[:, 64:80], r_sel[:, 64:80], real_row, None, ALU.mult).then_inc(sel_set, 1)
                dve.wait_ge(cnt_ps, L + 1)
                cum = bank(6, NT, E, off=128)
                link(v.tensor_copy(r_nt, bank(6, E, off=256)))
                k5 = r_k[:, 0:E * KOV].rearrange("p (a b) -> p a b", a=E)
                link(v.tensor_tensor(k5, r_nt.unsqueeze(2).to_broadcast([P, E, KOV]),
                                     steps.unsqueeze(1).to_broadcast([P, E, KOV]), ALU.is_gt))
                link(v.tensor_reduce(r_ex, k5, AXX, ALU.add))
                tri = r_big[:, 0:E * E].rearrange("p (a b) -> p a b", a=E)
                link(v.tensor_tensor(tri, r_ex.unsqueeze(1).to_broadcast([P, E, E]), before_e, ALU.mult))
                link(v.tensor_reduce(r_ovb, tri, AXX, ALU.add))
                link(v.scalar_tensor_tensor(out=r_diff, in0=r_ovb, scalar=float(CAP), in1=slot_over, op0=ALU.mult, op1=ALU.add))
                link(v.tensor_scalar(five(r_slot), cum, float(CAP), None, ALU.is_ge))
                link(v.tensor_tensor(five(r_slot), five(r_slot), r_diff.unsqueeze(1).to_broadcast(over), ALU.mult))
                link(v.tensor_tensor(five(r_slot), five(r_slot), cum, ALU.add))
                link(v.tensor_tensor(five(r_slot), five(r_slot), slot0.unsqueeze(1).to_broadcast(over), ALU.add))
                link(v.scalar_tensor_tensor(out=r_slot, in0=r_slot, scalar=1.0, in1=r_sel, op0=ALU.add, op1=ALU.mult))
                v.tensor_reduce(r_all, five(r_slot), AXX, ALU.add)
                link(v.tensor_reduce(r_a, five(r_slot), AXX, ALU.max))
                v.tensor_scalar(idx_a, r_a, -1.0, None, ALU.add).then_inc(idx_set, 1)
                link(v.tensor_tensor(r_b, r_all, r_a, ALU.subtract))
                v.tensor_scalar(idx_b, r_b, -1.0, None, ALU.add).then_inc(idx_set, 1)
                link(v.tensor_tensor(five(r_bias), five(r_slot), r_a.unsqueeze(2).to_broadcast(over), ALU.is_equal))
                link(v.tensor_tensor(r_bias, r_bias, r_comb, ALU.mult))
                v.tensor_reduce(ca, five(r_bias), AXX, ALU.add)
                link(v.tensor_tensor(r_comb, r_comb, r_bias, ALU.subtract))
                v.tensor_reduce(cb, five(r_comb), AXX, ALU.add)
                one = slice(0, 1)
                v.tensor_copy(r_tab[one, 0:E], expert[one, :])
                link(v.tensor_tensor(r_end[one, :], r_ovb[one, :], r_ex[one, :], ALU.add))
                ke = r_k[one, 0:NOV * E].rearrange("p (a b) -> p a b", a=NOV)
                ks = r_big[one, 0:NOV * E].rearrange("p (a b) -> p a b", a=NOV)
                kk = over_k[one, :].unsqueeze(2).to_broadcast([1, NOV, E])
                v.tensor_tensor(ke, kk, r_ovb[one, :].unsqueeze(1).to_broadcast([1, NOV, E]), ALU.is_ge)
                link(v.tensor_tensor(ks, kk, r_end[one, :].unsqueeze(1).to_broadcast([1, NOV, E]), ALU.is_lt))
                link(v.tensor_tensor(ke, ke, ks, ALU.mult))
                link(v.tensor_tensor(ke, ke, expert[one, :].unsqueeze(1).to_broadcast([1, NOV, E]), ALU.mult))
                link(v.tensor_reduce(r_tab[one, E:TILES], ke, AXX, ALU.add))
                v.tensor_copy(tile_ids[one, 0:TILES], r_tab[one, 0:TILES]).then_inc(tab_set, 1)
                link(v.tensor_reduce(r_nov[one, :], r_ex[one, :], AXX, ALU.add))
                link(v.tensor_scalar(r_nh[one, 0:NOV // 2], even_k[one, :], r_nov[one, :], None, ALU.is_lt))
                link(v.tensor_reduce(r_nov[one, :], r_nh[one, 0:NOV // 2], AXX, ALU.add))
                v.tensor_scalar(n_half[one, :], r_nov[one, :], float(E // 2), None, ALU.add).then_inc(tab_set, 1)

            def experts(L):
                q = S[L]
                dve.wait_ge(tab_set, 2 * L + 2)
                nh = dve.value_load(n_half[0:1, 0:1], min_val=E // 2, max_val=TILES // 2)
                dve.sem_inc(q["y_set"], 1)
                dve.wait_ge(q["tr_ps"], 2)
                v.tensor_copy(xeT[0][:, 4:8, :], bank(7, 4, CAP)).then_inc(q["xeT_set"], 1)

                def tile(u, s, stored):
                    tl = 2 * u + s
                    dve.wait_ge(q["sg_set"], tl + 1)
                    dve.wait_ge(q["up_ps"][s], u + 1)
                    v.tensor_tensor(h[s], sg[s], bank(2 + s, KF, CAP), ALU.mult).then_inc(q["h_set"], 1)
                    dve.wait_ge(q["tr_ps"], 2 * tl + 4)
                    v.tensor_copy(xeT[1 - s][:, 4:8, :], bank(7, 4, CAP)).then_inc(q["xeT_set"], 1)
                    dve.wait_ge(q["down_ps"][s], u + 1)
                    if stored:
                        dve.wait_ge(q["y_st"][s], 16 * u)
                    v.tensor_copy(ys[s][0:CAP, 512:D], bank(5)[0:CAP, :]).then_inc(q["y_set"], 1)

                tile(0, 0, False)
                tile(0, 1, False)
                with dve.Fori(1, nh) as u:
                    tile(u, 0, True)
                    tile(u, 1, True)

            v.memset(bank(6, NT * E), 0.0).then_inc(lg_zero, 1)
            layer_norm(0, 0)
            route(0)
            experts(0)
            dve.wait_ge(wp_ld, 16)
            dve.wait_ge(st_ld, 32)
            wp4 = wpool.rearrange("p (g k) d -> p g k d", g=4)
            v.tensor_tensor(wp4, wp4, pscale.rearrange("p (g d) -> p g d", g=4).unsqueeze(2).to_broadcast([P, 4, 2, 256]),
                            ALU.mult).then_inc(wp_ready, 1)
            v.memset(bank(6, NT * E), 0.0).then_inc(lg_zero, 1)
            for step in range(NT + 3):
                if step < NT:
                    stats(0, 1, step)
                    spread(0, 1, step)
                    gain(0, 1, step)
                if 2 <= step <= NT + 1:
                    i = step - 2
                    if i == 3:
                        dve.wait_ge(pool_out, 32)
                    stats(1, 0, i)
                    spread(1, 0, i)
                    gain(1, 0, i)
            route(1)
            experts(1)
            layer_norm(1, 1)


_INS = ["x_prompt", "x_sample", "cache_ckv", "cache_krope", "state_pool", "page_table", "w_dq", "g_q", "w_uq", "w_dkv",
        "g_kv", "w_uk", "w_uv", "w_o", "w_pool", "pool_scale", "w_router", "router_bias", "w_gate", "w_up", "w_down",
        "ln1_g", "ln1_b", "ln2_g", "ln2_b"]
_OUTS = [("o_y_p", (1, SEQ, D)), ("o_y_s", (DB, 1, D)), ("o_ckv_p", (1, 1, SEQ, KVL)), ("o_kr_p", (1, 1, SEQ, ROPE)),
         ("o_pool_p", (1, 1, CTX, D)), ("o_ckv_s", (1, DB, 1, KVL)), ("o_kr_s", (1, DB, 1, ROPE)),
         ("o_pool_s", (1, DB, CTX, D))]


def kernel(**inputs):
    import concourse.bacc as _bacc
    from concourse.bass_utils import run_bass_kernel_spmd as _run

    nc = _bacc.Bacc("TRN2", target_bir_lowering=False, num_devices=1)
    consts, place = constants()
    arrays, t = {"consts": consts}, {}
    for name in _INS:
        arrays[name] = np.ascontiguousarray(inputs[name])
    for name, a in arrays.items():
        t[name] = nc.dram_tensor(name, a.shape, mybir.dt.from_np(a.dtype), kind="ExternalInput").ap()
    for name, shape in _OUTS:
        t[name] = nc.dram_tensor(name, shape, F32, kind="ExternalOutput").ap()
    build(nc, t, consts.shape, place)
    r = _run(nc, [arrays], core_ids=[0])
    return tuple(r.results[0][name] for name, _ in _OUTS)
```

```python
from contextlib import ExitStack

import numpy as np

import concourse.bass as bass
from concourse import mybir

D = 1024
SEQ = 512
DB = 8
TOK = SEQ + DB
P = 128
NT = SEQ // P + 1
KD = D // P
H, NOPE, ROPE, VH = 16, 64, 32, 64
PAIRS = H // 2
QL, KVL = 384, 256
MQ, MKV = QL // P, KVL // P
HQ = NOPE + ROPE
PAGE, NPAGES, NPHYS = 128, 8, 80
PAST = PAGE * NPAGES
E, GROUPS, EPG, F = 16, 4, 4, 512
KF = F // P
CTX = 15
WINDOWS = (2, 4, 8, 16)
ALPHA = 4.0 ** 0.25
SCALE = HQ ** -0.5
LN_EPS, RMS_EPS = 1e-5, 1e-6
BIG = 1e30
HALF = TOK // 2
CAP = 96
KOV = (TOK - 1) // CAP
NOV = 10
TILES = E + NOV
BAND = P + CTX

F32 = mybir.dt.float32
I32 = mybir.dt.int32
ALU = mybir.AluOpType
ACT = mybir.ActivationFunctionType
AXX = mybir.AxisListType.X


def rows_of(i):
    return P if i < NT - 1 else DB


def constants():
    parts, place, at = [], {}, 0

    def put(name, a, *dims):
        nonlocal at
        full = np.zeros((P, int(np.prod(a.shape[1:]))), np.float32)
        full[:a.shape[0]] = a.reshape(a.shape[0], -1)
        parts.append(full)
        place[name] = (at, dims or a.shape[1:])
        at += full.shape[1]

    def rowwise(v):
        return np.broadcast_to(np.asarray(v, np.float32).reshape(1, -1), (P, np.size(v)))

    i = np.arange(P)
    put("ident", np.eye(P))
    put("ones", np.ones((P, P)))
    put("before", (i[:, None] < i[None, :]))
    half = ROPE // 2
    inv = (np.float32(10000.0) ** (np.float32(-2.0) * np.arange(half, dtype=np.float32) / np.float32(ROPE)))
    pos = np.concatenate([np.arange(SEQ), np.full(DB, PAST)]).astype(np.float32)
    ang = pos[:, None] * inv[None, :].astype(np.float32)
    cos, sin = np.cos(ang).astype(np.float32), np.sin(ang).astype(np.float32)
    rot = np.concatenate([cos.T, cos.T, -sin.T, sin.T])
    one = np.ones((NOPE, TOK))
    put("rope_q", -SCALE * np.stack([np.concatenate([one, rot]), np.concatenate([rot, one])], 1))
    def natural(t):
        out = np.zeros((P, NT, half), np.float32)
        for j in range(NT):
            out[:rows_of(j), j] = t[P * j:P * j + rows_of(j)]
        return out
    put("cos_k", natural(cos))
    put("sin_k", natural(sin))
    put("causal", np.concatenate([np.zeros((P, SEQ - P)), np.where(i[None, :] > i[:, None], BIG, 0.0)], 1))
    put("own_sample", np.broadcast_to(np.where(np.eye(DB) > 0, 0.0, BIG)[None], (H, DB, DB)))
    band = np.zeros((P, 2, 4, BAND), np.float32)
    band_s = np.zeros((DB * CTX, 4, DB), np.float32)
    own_s = np.zeros((DB, 4, DB), np.float32)
    for g, w in enumerate(WINDOWS):
        for c in range(BAND):
            for r in range(max(0, c - w + 1), min(P, c + 1)):
                band[r, 0, g, c] = 1.0 / min(c + 1, w)
                band[r, 1, g, c] = 1.0 / w
            if c < P:
                band[c, :, g, c] -= 1.0
        for b in range(DB):
            band_s[b * CTX + CTX - w + 1:(b + 1) * CTX, g, b] = 1.0 / w
            own_s[b, g, b] = 1.0 / w - 1.0
    put("band", band)
    put("band_s", band_s)
    put("own_s", own_s)
    e = np.arange(E)
    put("slot0", rowwise(e * CAP))
    put("slot_over", rowwise((E - 1) * CAP - e * CAP))
    put("steps", rowwise(CAP * np.arange(1, KOV + 1)))
    put("before_e", rowwise(e[None, :] < e[:, None]), E, E)
    j = np.arange(EPG)
    put("earlier", rowwise(j[None, :] < j[:, None]), EPG, EPG)
    put("prefer", rowwise(GROUPS - np.arange(GROUPS)))
    put("real_row", (i < DB).astype(np.float32)[:, None])
    put("over_k", rowwise(np.arange(NOV)))
    put("even_k", rowwise(np.arange(0, NOV, 2)))
    put("expert", rowwise(e))
    put("ln_eps", np.full((P, 1), LN_EPS))
    put("rms_eps", np.full((P, 1), RMS_EPS))
    return np.concatenate(parts, 1).astype(np.float32), place


def build(nc, t, consts_shape, place):
    ctx = ExitStack()
    with ctx:
        def sem(name):
            return ctx.enter_context(nc.semaphore(name))

        def sb(name, shape, dt=F32):
            return ctx.enter_context(nc.sbuf_tensor(name, shape, dt))

        ring = [sb("ring0", [P, 12288]), sb("ring1", [P, 12288])]
        X = sb("X", [P, NT, D])
        gb = sb("gb", [P, 4, D])
        C = sb("C", list(consts_shape))
        wr = sb("wr", [P, KD, E])
        small = sb("small", [P, 272])
        ids = sb("ids", [P, 128], I32)
        arena = sb("arena", [P, 15152])
        PS = ctx.enter_context(nc.psum_tensor("PS", [P, 4096], F32))

        def view(buf, off, *dims):
            n = int(np.prod(dims))
            ap = buf[:, off:off + n]
            if len(dims) == 2:
                return ap.rearrange("p (a b) -> p a b", a=dims[0])
            if len(dims) == 3:
                return ap.rearrange("p (a b c) -> p a b c", a=dims[0], b=dims[1])
            return ap

        def const(name):
            off, dims = place[name]
            if len(dims) == 3:
                n = int(np.prod(dims))
                return C[:, off:off + n].rearrange("p (a b c) -> p a b c", a=dims[0], b=dims[1])
            return view(C, off, *dims)

        def bank(b, *dims, off=0):
            return view(PS, 512 * b + off, *(dims or (512,)))

        ident, ones, before = const("ident"), const("ones"), const("before")
        rope_q, cos_k, sin_k = const("rope_q"), const("cos_k"), const("sin_k")
        causal, own_sample = const("causal"), const("own_sample")
        band, band_s, own_s = const("band"), const("band_s"), const("own_s")
        slot0, slot_over, steps = const("slot0"), const("slot_over"), const("steps")
        before_e, earlier, prefer = const("before_e"), const("earlier"), const("prefer")
        real_row, over_k, even_k, expert = (const(n) for n in ("real_row", "over_k", "even_k", "expert"))
        ln_eps, rms_eps = const("ln_eps"), const("rms_eps")

        wg = [view(r, 0, KD, F) for r in ring]
        wu = [view(r, 4096, KD, F) for r in ring]
        wd = [view(r, 8192, KF, D) for r in ring]
        R0, R1 = ring
        wo = view(R0, 0, KD, D)
        V = view(R0, 8192, 4, D)
        kraw = view(R0, 8192, NT, ROPE)
        krot = view(R0, 8192 + 160, NT, ROPE)
        gkv = view(R0, 8192 + 320, KVL)
        rtmp = view(R0, 8192 + 576, 4, 80)
        rq = view(R0, 8192 + 900, TOK)
        sqj = view(R0, 8192 + 1420, KVL)
        kdup = view(R0, 8192 + 1680, NT, 4, ROPE)
        wdq = view(R1, 0, KD, QL)
        wdkv = view(R1, 3072, KD, KVL + ROPE)
        sq = view(R1, 5376, MQ, TOK)
        prob = view(R1, 0, 4, 512)
        probT = view(R1, 2048, 2, 512)
        wqn = view(R1, 6936, MQ, 2 * HQ)
        wuq = view(R1, 7512, MQ, 256)
        wuk = view(R1, 8280, MKV, P)
        qT = [view(R1, 8536, TOK), view(R1, 9056, TOK)]
        kT = [view(R1, 9576, SEQ), view(R1, 10088, SEQ)]
        osb = view(R1, 10600, 4, P)
        ckp = [view(R1, at, NPAGES, KVL) for at in (3072, 0, 6144)]
        krp = [view(R1, at, NPAGES, 4, ROPE) for at in (5120, 2048, 8192)]
        kpT = view(R1, 9216, 3, PAST)
        zero_src = view(R1, 11264, D)
        oT = view(arena, 0, PAIRS, TOK)
        ckv = view(arena, 4160, NT, KVL)
        ckT = view(arena, 5440, 3, TOK)
        XT = view(arena, 7168, KD, TOK)
        xr = [[view(R0, 8192 + 1024 * s, KD, P) for s in range(2)], [view(arena, 7168 + 1024 * s, KD, P) for s in range(2)]]
        wukT = view(arena, 7168, PAIRS, KVL)
        qlat = view(arena, 9216, MKV, DB, H)
        olat = view(arena, 9472, MKV, DB, H)
        ps_s = view(arena, 9728, PAST + DB)
        psT_s = view(arena, 10760, NPAGES + 1, H)
        wuv = view(arena, 11328, MKV, D)
        cq = view(arena, 13376, MQ, TOK)
        qs = view(arena, 7000, PAIRS, 16)
        qr = view(arena, 14936, DB, H)
        xe = [view(arena, 1024 * s, D) for s in range(2)]
        xeT = [view(arena, 2048 + 768 * s, KD, CAP) for s in range(2)]
        sg = [view(arena, 3584 + 384 * s, KF, CAP) for s in range(2)]
        h = [view(arena, 4352 + 384 * s, KF, CAP) for s in range(2)]
        ys = [view(arena, 5120 + 1024 * s, D) for s in range(2)]
        ya = [view(arena, 7168 + 1024 * s, D) for s in range(2)]
        yb = [view(arena, 9216 + 1024 * s, D) for s in range(2)]
        state = view(arena, 0, D)
        pscale = view(arena, 1024, D)
        poolT = view(arena, 2048, KD, TOK)
        wpool = view(arena, 13104, KD, 256)
        RT = 11328

        def rt(n, *dims):
            nonlocal RT
            v = view(arena, RT, *(dims or (n,)))
            RT += n
            return v

        r_exp, r_s, r_bias, r_rank, r_sel, r_comb, r_slot = (rt(80) for _ in range(7))
        r_big = rt(320)
        r_gs, r_gp, r_gsel = (rt(20) for _ in range(3))
        r_m, r_den, r_a, r_b, r_all = (rt(5) for _ in range(5))
        r_nt, r_ex, r_ovb, r_end, r_diff = (rt(E) for _ in range(5))
        r_tab = rt(32)
        r_nh = rt(8)
        r_k = rt(160)
        r_nov = rt(1)
        assert RT <= 13104
        bias_row = view(small, 0, E)
        gq = view(small, 16, MQ)
        ss = view(small, 20, NT)
        kstd = view(small, 25, NT)
        krs = view(small, 30, NT)
        mneg = view(small, 36, 8)
        rsum = view(small, 44, 8)
        rinv = view(small, 52, 8)
        s_mneg, s_sum, s_inv = view(small, 60, 1), view(small, 61, 1), view(small, 62, 1)
        bn = view(small, 66, NT, 12)
        mv = view(small, 126, NT, 2)
        std, rstd, nmr = view(small, 136, NT), view(small, 141, NT), view(small, 146, NT)
        ca, cb = view(small, 152, NT), view(small, 158, NT)
        qb = [view(arena, 10904 + 48 * s, 3, H) for s in range(3)]
        onat = view(arena, 13376, KVL)
        page_ids = ids[:, 0:64]
        idx_a, idx_b = ids[:, 64:69], ids[:, 72:77]
        tile_ids, n_half = ids[:, 80:112], ids[:, 120:121]

        ZSTEP = -(-(TILES + 1) // (PAIRS - 2))
        xs = nc.dram_tensor("expert_rows", (ZSTEP * (PAIRS - 2) * CAP, D), F32).ap()
        yd = nc.dram_tensor("expert_out", (TILES * CAP, D), F32).ap()

        ident_ld, c_ld, wdq_ld, wdkv_ld, gain_ld, wuv_ld, router_ld, wo_ld = (
            sem(n) for n in ("ident_ld", "c_ld", "wdq_ld", "wdkv_ld", "gain_ld", "wuv_ld", "router_ld", "wo_ld"))
        x_ld = [sem(f"x_ld{i}") for i in range(NT)]
        pt_ld, wqn_ld, wuk_ld, zero_set, zero_st = (
            sem(n) for n in ("pt_ld", "wqn_ld", "wuk_ld", "zero_set", "zero_st"))
        page_ld = [sem(f"page_ld{s}") for s in range(3)]
        kr_dup = sem("kr_dup")
        gb_ld = [[sem(f"gb{w + 1}_ld_{L}") for w in range(2)] for L in range(2)]
        wp_ld, st_ld, wp_ready = sem("wp_ld"), sem("st_ld"), sem("wp_ready")
        out_st = sem("out_st")
        latent_st = sem("latent_st")
        passed = sem("passed")
        pool_out = sem("pool_out")
        xt_ps = sem("xt_ps")
        xt_ev = [sem("xt_ev_dve"), sem("xt_ev_act")]
        cq_ps, cq_copied, cq_squared, cq_sum, rq_std, cq_done = (
            sem(n) for n in ("cq_ps", "cq_copied", "cq_squared", "cq_sum", "rq_std", "cq_done"))
        kraw_zero, kv_ps, kv_ss, kv_std, kv_ready, kr_ready, ck_ps, ck_ev, krope_set = (
            sem(n) for n in ("kraw_zero", "kv_ps", "kv_ss", "kv_std", "kv_ready", "kr_ready",
                             "ck_ps", "ck_ev", "krope_set"))
        dve_step = sem("dve_step")
        wq_even, wq_odd, q_ps, q_ev, for_act, act_ev = (
            sem(n) for n in ("wq_even", "wq_odd", "q_ps", "q_ev", "for_act", "act_ev"))
        s_ps, min_set, exp_set, t_ps, o_ps, rinv_set, o_ev = (
            sem(n) for n in ("s_ps", "min_set", "exp_set", "t_ps", "o_ps", "rinv_set", "o_ev"))
        pt_ev = [sem("pt_ev_dve"), sem("pt_ev_act")]
        qpad_zero = sem("qpad_zero")
        ql_ps, ql_ev, qb_set, tp_ps, sc_ps, new_masked, smin_set, sexp_set, sinv_set = (
            sem(n) for n in ("ql_ps", "ql_ev", "qb_set", "tp_ps", "sc_ps", "new_masked", "smin_set",
                             "sexp_set", "sinv_set"))
        tp_ev = [sem("tp_ev_dve"), sem("tp_ev_act")]
        spT_ps, spT_ev, pv_ps, onat_set, ol_ps, ol_ev, uv_ps, uv_ev = (
            sem(n) for n in ("spT_ps", "spT_ev", "pv_ps", "onat_set", "ol_ps", "ol_ev", "uv_ps", "uv_ev"))
        mix_ps = sem("mix_ps")
        ln_z, ln_agg, ln_std, ln_rstd, ln_nrm, ln_gam, ln_out = (
            [sem(f"{n}_{L}") for L in range(2)]
            for n in ("ln_z", "ln_agg", "ln_std", "ln_rstd", "ln_nrm", "ln_gam", "ln_out"))
        turn_ps, turn_ev = sem("turn_ps"), sem("turn_ev")
        lg_zero, lg_ps, lg_exp, sel_set, cnt_ps, idx_set, tab_set, scat, xscaled = (
            sem(n) for n in ("lg_zero", "lg_ps", "lg_exp", "sel_set", "cnt_ps", "idx_set", "tab_set",
                             "scat", "xscaled"))
        gath = [sem("gath0"), sem("gath1")]
        def expert_sems(L):
            two = ("wg_ld", "wu_ld", "wd_ld", "xe_ld", "y_st", "gate_ps", "up_ps", "down_ps")
            one = ("tr_ps", "xeT_set", "sg_set", "h_set", "y_set")
            return {n: [sem(f"{n}{s}_{L}") for s in range(2)] for n in two} | {n: sem(f"{n}_{L}") for n in one}

        S = [expert_sems(0), expert_sems(1)]
        block = ctx.enter_context(nc.Block())

        def bcast(row, n=P):
            return row.unsqueeze(0).to_broadcast([n] + list(row.shape))

        turn_bank = [4, 5, 7]

        def score(i):
            return bank((2, 2, 1, 0)[i], P * (i + 1), off=256 if i == 0 else 0)

        def scored(i):
            return min(4 - i, 4) if i > 1 else 4

        def hold(eng, s, value):
            eng.wait_ge(s, value)
            if not isinstance(value, int):
                eng.sem_inc(passed, 1)

        @block.sync
        def _(sp):
            sp.dma_start(C[:, 0:P], t["consts"][:, 0:P]).then_inc(ident_ld, 16)
            for i in range(4):
                sp.dma_start(X[:, i, :], t["x_prompt"][0, P * i:P * (i + 1), :]).then_inc(x_ld[i], 16)
            sp.dma_start(X[0:DB, 4, :], t["x_sample"][:, 0, :]).then_inc(x_ld[4], 16)
            sp.dma_start(wdq, t["w_dq"][0].rearrange("(k p) n -> p k n", p=P)).then_inc(wdq_ld, 16)
            sp.dma_start(C[:, P:], t["consts"][:, P:]).then_inc(c_ld, 16)
            with nc.allow_non_contiguous_dma(reason="384 words"):
                sp.dma_start(gq, t["g_q"][0].rearrange("(m p) -> p m", p=P)).then_inc(gain_ld, 16)
            sp.dma_start(wdkv, t["w_dkv"][0].rearrange("(k p) n -> p k n", p=P)).then_inc(wdkv_ld, 16)
            sp.dma_start(gkv, bcast(t["g_kv"][0])).then_inc(gain_ld, 16)
            sp.dma_start(page_ids[0:1, :], t["page_table"].rearrange("b n -> (b n)").unsqueeze(0)).then_inc(pt_ld, 16)

            def load_pair(j):
                sp.dma_start(wqn, t["w_uq"][0].rearrange("(m p) n -> p m n", p=P)[:, :, bass.ds(2 * HQ * j, 2 * HQ)]
                             ).then_inc(wqn_ld, 16)
                sp.dma_start(wuk, t["w_uk"][0].rearrange("(m p) h d -> p m (h d)", p=P)[:, :, bass.ds(P * j, P)]
                             ).then_inc(wuk_ld, 16)

            load_pair(0)
            sp.dma_start(wuv, t["w_uv"][0].rearrange("(m p) h d -> p m (h d)", p=P)).then_inc(wuv_ld, 16)
            sp.dma_start(wr[:, :, :], t["w_router"].rearrange("(k p) n -> p k n", p=P)).then_inc(router_ld, 16)
            sp.dma_start(bias_row, bcast(t["router_bias"])).then_inc(router_ld, 16)
            sp.dma_start(gb[:, 0, :], bcast(t["ln1_g"][0])).then_inc(gb_ld[0][0], 16)
            sp.dma_start(gb[:, 1, :], bcast(t["ln1_b"][0])).then_inc(gb_ld[0][0], 16)
            sp.dma_start(gb[:, 2, :], bcast(t["ln2_g"][0])).then_inc(gb_ld[0][1], 16)
            sp.dma_start(gb[:, 3, :], bcast(t["ln2_b"][0])).then_inc(gb_ld[0][1], 16)
            sp.dma_start(wo, t["w_o"][0].rearrange("(k p) n -> p k n", p=P)).then_inc(wo_ld, 16)
            sp.wait_ge(kv_ready, NT)
            sp.wait_ge(kr_ready, 1)
            for i in range(4):
                sp.dma_start(t["o_ckv_p"][0, 0, P * i:P * (i + 1), :], ckv[:, i, :]).then_inc(latent_st, 16)
                sp.dma_start(t["o_kr_p"][0, 0, P * i:P * (i + 1), :], krot[:, i, :]).then_inc(latent_st, 16)
            sp.dma_start(t["o_ckv_s"][0, :, 0, :], ckv[0:DB, 4, :]).then_inc(latent_st, 16)
            sp.dma_start(t["o_kr_s"][0, :, 0, :], krot[0:DB, 4, :]).then_inc(latent_st, 16)
            sp.dma_start(t["o_pool_s"][0, :, 0:CTX - 1, :], t["state_pool"][0, :, 1:CTX, :]).then_inc(out_st, 16)
            sp.wait_ge(wq_odd, 1)
            sp.wait_ge(for_act, 3)
            load_pair(1)

            def load_pages(b, s):
                for n in range(NPAGES):
                    page = sp.value_load(page_ids[0:1, bass.ds(b * NPAGES + n, 1)], min_val=0, max_val=NPHYS - 1)
                    sp.dma_start(ckp[s][:, n, :], t["cache_ckv"][0, bass.ds(page, 1), :, :].rearrange("a p d -> (a p) d")
                                 ).then_inc(page_ld[s], 16)
                    sp.dma_start(krp[s][:, n, 0, :], t["cache_krope"][0, bass.ds(page, 1), :, :].rearrange("a p d -> (a p) d")
                                 ).then_inc(page_ld[s], 16)

            sp.wait_ge(pt_ld, 16)
            sp.wait_ge(cq_sum, 2)
            load_pages(0, 0)
            sp.wait_ge(zero_set, 1)
            zeros = zero_src[0:CAP, :].unsqueeze(1)
            sp.dma_start(yd[E * CAP:, :].rearrange("(a p) d -> p a d", p=CAP), zeros.to_broadcast([CAP, NOV, D])
                         ).then_inc(zero_st, 16)
            with sp.Fori(2, PAIRS) as j:
                sp.wait_ge(wq_odd, j)
                sp.wait_ge(for_act, 4 * j - 2)
                load_pair(j)
                sp.dma_start(xs[bass.ds(ZSTEP * CAP * (j - 2), ZSTEP * CAP), :].rearrange("(a p) d -> p a d", p=CAP),
                             zeros.to_broadcast([CAP, ZSTEP, D])).then_inc(zero_st, 16)
            with sp.Fori(0, (DB - 2) // 3) as u:
                for d in (1, 2, 3):
                    sp.wait_ge(pv_ps, 3 * u + d)
                    load_pages(3 * u + d, d % 3)
            sp.wait_ge(pv_ps, DB - 1)
            load_pages(DB - 1, 1)

            def load_expert(L, e, s, gate_free=None, up_free=None, down_free=None):
                q = S[L]
                if gate_free:
                    sp.wait_ge(*gate_free)
                sp.dma_start(wg[s], t["w_gate"][L, bass.ds(e, 1), :, :].rearrange("a (k p) f -> p (a k) f", p=P)
                             ).then_inc(q["wg_ld"][s], 16)
                if up_free:
                    sp.wait_ge(*up_free)
                sp.dma_start(wu[s], t["w_up"][L, bass.ds(e, 1), :, :].rearrange("a (k p) f -> p (a k) f", p=P)
                             ).then_inc(q["wu_ld"][s], 16)
                if down_free:
                    sp.wait_ge(*down_free)
                sp.dma_start(wd[s], t["w_down"][L, bass.ds(e, 1), :, :].rearrange("a (k p) d -> p (a k) d", p=P)
                             ).then_inc(q["wd_ld"][s], 16)

            for L in range(2):
                q = S[L]
                if L == 0:
                    load_expert(0, 0, 1, gate_free=(pv_ps, DB + 2))
                    load_expert(0, 1, 0, gate_free=(mix_ps, NT), down_free=(lg_ps, 1))
                else:
                    load_expert(1, 0, 1, (S[0]["gate_ps"][0], nh), (S[0]["up_ps"][0], nh), (S[0]["down_ps"][0], nh))
                    sp.wait_ge(ln_out[0], 2 * NT)
                    sp.dma_start(t["o_pool_p"][0, 0, :, :], X[P - CTX:P, 3, :]).then_inc(pool_out, 16)
                    sp.dma_start(t["o_pool_s"][0, :, CTX - 1, :], X[0:DB, 4, :]).then_inc(pool_out, 16)
                    load_expert(1, 1, 0, (S[0]["gate_ps"][1], nh), (S[0]["up_ps"][1], nh), (S[0]["down_ps"][1], nh))
                sp.wait_ge(tab_set, 2 * L + 2)
                nh = sp.value_load(n_half[0:1, 0:1], min_val=E // 2, max_val=TILES // 2)
                with sp.Fori(1, nh) as u:
                    for s in range(2):
                        ex = sp.value_load(tile_ids[0:1, bass.ds(2 * u + s, 1)], min_val=0, max_val=E - 1)
                        load_expert(L, ex, 1 - s, (q["gate_ps"][s], u), (q["up_ps"][s], u), (q["down_ps"][s], u))
            for i in range(4):
                sp.wait_ge(ln_out[1], NT + i + 1)
                sp.dma_start(t["o_y_p"][0, P * i:P * (i + 1), :], X[:, i, :]).then_inc(out_st, 16)
            sp.wait_ge(ln_out[1], 2 * NT)
            sp.dma_start(t["o_y_s"][:, 0, :], X[0:DB, 4, :]).then_inc(out_st, 16)
            sp.wait_ge(out_st, 16 * (1 + 5))
            sp.wait_ge(pool_out, 32)

        @block.tensor
        def _(pe):
            turns = [0]

            def turn():
                n = turns[0]
                turns[0] += 1
                if n >= 3:
                    pe.wait_ge(turn_ev, n - 2)
                return turn_bank[n % 3]

            def transpose_x(i, g, b):
                n = rows_of(i)
                for kk in range(4):
                    last = nc.tensor.transpose(bank(b, 4, P)[:, kk, 0:n], X[0:n, i, P * (4 * g + kk):P * (4 * g + kk + 1)],
                                               ident[0:n, 0:n])
                return last

            pe.wait_ge(ident_ld, 16)
            for i in range(NT):
                pe.wait_ge(x_ld[i], 16)
                for g in range(2):
                    n = 2 * i + g
                    if n >= 4:
                        pe.wait_ge(xt_ev[g], (n - 4) // 2 + 1)
                    transpose_x(i, g, n % 4).then_inc(xt_ps, 1)
            pe.wait_ge(wdq_ld, 16)
            for g in range(2):
                pe.wait_ge(xt_ev[g], NT)
            for m in range(MQ):
                for hf in range(2):
                    n = 2 * m + hf
                    if n >= 4:
                        pe.wait_ge(cq_copied, n - 3)
                    for k in range(KD):
                        last = nc.tensor.matmul(bank(n % 4, HALF), wdq[:, k, P * m:P * (m + 1)],
                                                XT[:, k, HALF * hf:HALF * (hf + 1)], start=(k == 0), stop=(k == KD - 1))
                    last.then_inc(cq_ps, 1)
            pe.wait_ge(wdkv_ld, 16)
            for i in range(NT):
                n = rows_of(i)
                if i >= 2:
                    pe.wait_ge(kv_ready, i - 1)
                for k in range(KD):
                    last = nc.tensor.matmul(bank(4 + i % 2, KVL + ROPE)[0:n, :], XT[:, k, P * i:P * i + n], wdkv[:, k, :],
                                            start=(k == 0), stop=(k == KD - 1))
                last.then_inc(kv_ps, 1)
            pe.wait_ge(c_ld, 16)
            pe.wait_ge(cq_squared, 2 * MQ)
            pe.wait_ge(cq_copied, 2 * MQ)
            for hf in range(2):
                for m in range(MQ):
                    last = nc.tensor.matmul(bank(hf, HALF), ones, sq[:, m, HALF * hf:HALF * (hf + 1)],
                                            start=(m == 0), stop=(m == MQ - 1))
                last.then_inc(cq_sum, 1)
            for i in range(NT):
                n = rows_of(i)
                if i == 0:
                    pe.wait_ge(kv_ready, NT)
                    pe.wait_ge(kr_ready, 2)
                if i >= 2:
                    pe.wait_ge(ck_ev, i - 1)
                out = bank(6 + i % 2, 3, P)
                for c in range(MKV):
                    nc.tensor.transpose(out[:, c, 0:n], ckv[0:n, i, P * c:P * (c + 1)], ident[0:n, 0:n])
                nc.tensor.transpose(out[:, 2, 0:n], kdup[0:n, i, :, :].rearrange("p a b -> p (a b)"), ident[0:n, 0:n]
                                    ).then_inc(ck_ps, 1)

            def project_q(parity, hf, b):
                for m in range(MQ):
                    last = nc.tensor.matmul(bank(b, HALF), wuq[:, m, P * parity:P * (parity + 1)],
                                            cq[:, m, HALF * hf:HALF * (hf + 1)], start=(m == 0), stop=(m == MQ - 1))
                last.then_inc(q_ps, 1)

            def q_even(j, first):
                pe.wait_ge(wq_even, j + 1)
                if not first:
                    pe.wait_ge(act_ev, 3 if isinstance(j, int) and j == 1 else 4 * j - 2)
                project_q(0, 0, 4)
                if not first:
                    pe.wait_ge(act_ev, 4 * j - 1)
                project_q(0, 1, 7)

            def v_both(j):
                pe.wait_ge(q_ev, 4 * j + 1)
                for i in range(4):
                    for c in range(MKV):
                        last = nc.tensor.matmul(bank(4, 4, P)[:, i, :], ckT[:, c, P * i:P * (i + 1)],
                                                wuv[:, c, bass.ds(P * j, P)], start=(c == 0), stop=(c == MKV - 1))
                last.then_inc(for_act, 1)

            def q_odd(j, first):
                pe.wait_ge(wq_odd, j + 1)
                pe.wait_ge(q_ev, 4 * j + 2)
                project_q(1, 0, 7)
                pe.wait_ge(act_ev, 1 if first else 4 * j)
                project_q(1, 1, 4)

            def k_both(j):
                pe.wait_ge(q_ev, 4 * j + 3)
                pe.wait_ge(wuk_ld, 16 * (j + 1))
                for c in range(MKV):
                    last = nc.tensor.matmul(bank(7), wuk[:, c, :], ckT[:, c, 0:SEQ], start=(c == 0), stop=(c == MKV - 1))
                last.then_inc(for_act, 1)
                pe.wait_ge(q_ev, 4 * j + 4)
                for c in range(MKV):
                    last = nc.tensor.transpose(bank(4, MKV, P)[:, c, :], wuk[:, c, :], ident)
                last.then_inc(for_act, 1)

            def scores(par):
                for i in (3, 2, 1, 0):
                    nc.tensor.matmul(score(i), qT[par][:, P * i:P * (i + 1)], kT[par][:, 0:P * (i + 1)],
                                     start=True, stop=True).then_inc(s_ps, 1)

            def attend(p, par, meanwhile):
                def turned(i):
                    hold(pe, exp_set, 8 * p + 4 * par + 4 - i)
                    for k in range(i + 1):
                        last = nc.tensor.transpose(bank(5 + i % 2, 4, P)[:, k, :], prob[:, i, P * k:P * (k + 1)], ident)
                    last.then_inc(t_ps, 1)

                def weighed(i):
                    hold(pe, pt_ev[i % 2], 4 * p + 2 * par + (3 - i) // 2 + 1)
                    for k in range(i + 1):
                        last = nc.tensor.matmul(bank(3, 4, VH, off=256 * par)[:, i, :], probT[:, i % 2, P * k:P * (k + 1)],
                                                V[:, k, bass.ds(P * p + VH * par, VH)], start=(k == 0), stop=(k == i))
                    return last

                turned(3)
                turned(2)
                if meanwhile:
                    meanwhile(p + 1)
                if par:
                    pe.wait_ge(o_ev, 2 * p + 1)
                weighed(3)
                turned(1)
                weighed(2)
                turned(0)
                weighed(1)
                weighed(0).then_inc(o_ps, 1)

            def turn_heads(p):
                pe.wait_ge(o_ev, 2 * p + 2)
                for i in range(4):
                    last = nc.tensor.transpose(bank(7, 4, P)[:, i, :], osb[:, i, :], ident)
                last.then_inc(for_act, 1)

            def pair(p, after_one, more):
                pe.wait_ge(q_ev, 4 * p + 4)
                pe.wait_ge(act_ev, 4 * p + 2)
                scores(0)
                if after_one:
                    turn_heads(p - 1)
                if more:
                    q_even(p + 1, False)
                attend(p, 0, v_both if more else None)
                scores(1)
                if more:
                    q_odd(p + 1, False)
                attend(p, 1, k_both if more else None)

            pe.wait_ge(cq_done, 1)
            pe.wait_ge(ck_ev, NT)
            pe.wait_ge(wuv_ld, 16)
            pe.wait_ge(krope_set, 1)
            q_even(0, True)
            v_both(0)
            q_odd(0, True)
            k_both(0)
            pe.wait_ge(q_ev, 4)
            pair(0, False, True)
            with pe.Fori(1, PAIRS - 1) as p:
                pair(p, True, True)
            pair(PAIRS - 1, True, False)
            turn_heads(PAIRS - 1)

            def latent_q():
                pe.wait_ge(ln_z[0], 4)
                for j in range(PAIRS):
                    for c in range(MKV):
                        last = nc.tensor.matmul(bank(3, MKV, PAIRS, 16)[:, c, j, :], wukT[:, j, P * c:P * (c + 1)], qs[:, j, :],
                                                start=True, stop=True)
                last.then_inc(ql_ps, 1)

            def turn_pages(b, s, use):
                pe.wait_ge(page_ld[s], 256 * use)
                n = 0
                for c in range(3):
                    if c == MKV:
                        pe.wait_ge(kr_dup, b + 1)
                    for hf in range(2):
                        if not isinstance(b, int) or b > 0 or n >= 2:
                            pe.wait_ge(tp_ev[n % 2], 3 * b + n // 2)
                        for a in range(4):
                            pg = 4 * hf + a
                            src = (ckp[s][:, pg, P * c:P * (c + 1)] if c < MKV
                                   else krp[s][:, pg, :, :].rearrange("p a b -> p (a b)"))
                            last = nc.tensor.transpose(bank(4 + n % 2, 4, P)[:, a, :], src, ident)
                        last.then_inc(tp_ps, 1)
                        n += 1

            def turn_latent_out(b):
                hold(pe, onat_set, b + 1)
                for c in range(MKV):
                    last = nc.tensor.transpose(bank(3, MKV, H)[:, c, :], onat[0:H, P * c:P * (c + 1)], ident[0:H, 0:H])
                last.then_inc(ol_ps, 1)

            def sample(b, s, after_one, following):
                pe.wait_ge(tp_ev[0], 3 * b + 3)
                pe.wait_ge(tp_ev[1], 3 * b + 3)
                pe.wait_ge(qb_set, b + 1)
                for hf in range(2):
                    for c in range(3):
                        nc.tensor.matmul(bank(hf)[0:H, :], qb[s][:, c, :], kpT[:, c, 512 * hf:512 * (hf + 1)],
                                         start=(c == 0), stop=(c == 2))
                for c in range(3):
                    last = nc.tensor.matmul(bank(2, DB)[0:H, :], qb[s][:, c, :], ckT[:, c, SEQ:TOK], start=(c == 0), stop=(c == 2))
                last.then_inc(sc_ps, 1)
                if after_one:
                    turn_latent_out(b - 1)
                if following:
                    turn_pages(*following)
                if after_one:
                    pe.wait_ge(ol_ev, b)
                hold(pe, sexp_set, b + 1)
                turned = bank(6, NPAGES + 1, H, off=256)
                for n in range(NPAGES):
                    nc.tensor.transpose(turned[:, n, :], ps_s[0:H, P * n:P * (n + 1)], ident[0:H, 0:H])
                nc.tensor.transpose(turned[0:DB, NPAGES, :], ps_s[0:H, PAST:PAST + DB], ident[0:H, 0:H]).then_inc(spT_ps, 1)
                pe.wait_ge(spT_ev, b + 1)
                for n in range(NPAGES):
                    nc.tensor.matmul(bank(7, KVL)[0:H, :], psT_s[:, n, :], ckp[s][:, n, :], start=(n == 0), stop=False)
                nc.tensor.matmul(bank(7, KVL)[0:H, :], psT_s[0:DB, NPAGES, :], ckv[0:DB, 4, :], start=False, stop=True
                                 ).then_inc(pv_ps, 1)

            def samples():
                sample(0, 0, False, (1, 1, 1))
                with pe.Fori(0, (DB - 2) // 3) as u:
                    for d in (1, 2, 3):
                        sample(3 * u + d, d % 3, True, (3 * u + d + 1, (d + 1) % 3, u + 1 + (d + 1) // 3))
                sample(DB - 1, 1, True, None)
                turn_latent_out(DB - 1)
                pe.wait_ge(ol_ev, DB)
                for j in range(PAIRS):
                    for c in range(MKV):
                        last = nc.tensor.matmul(bank(3, PAIRS, DB, 2, off=256)[:, j, :, :], wuv[:, c, P * j:P * (j + 1)],
                                                olat[:, c, :, 2 * j:2 * j + 2], start=(c == 0), stop=(c == MKV - 1))
                last.then_inc(uv_ps, 1)

            def mix(L, i):
                n, b0 = rows_of(i), 2 * (i % 2)
                if i >= 2:
                    pe.wait_ge(ln_z[L], i - 1)
                if L == 0:
                    for hf in range(2):
                        for k in range(KD):
                            last = nc.tensor.matmul(bank(b0 + hf)[0:n, :], oT[:, k, P * i:P * i + n],
                                                    wo[:, k, 512 * hf:512 * (hf + 1)], start=(k == 0), stop=(k == KD - 1))
                else:
                    for g in range(4):
                        for kk in range(2):
                            last = nc.tensor.matmul(view(PS, 512 * b0 + 256 * g, 256)[0:n, :],
                                                    poolT[:, 2 * g + kk, P * i:P * i + n], wpool[:, 2 * g + kk, :],
                                                    start=(kk == 0), stop=(kk == 1))
                last.then_inc(mix_ps, 1)

            def pool(i):
                pe.wait_ge(ln_out[0], NT + i + 1)
                if i < 4:
                    for g in range(2):
                        b = turn()
                        for c in range(4):
                            k = 4 * g + c
                            out = bank(b, 4, P)[:, c, :]
                            last = nc.tensor.matmul(out, X[:, i, P * k:P * (k + 1)], band[:, min(i, 1), k // 2, 0:P],
                                                    start=True, stop=(i == 0))
                            if i:
                                last = nc.tensor.matmul(out[:, 0:CTX], X[:, i - 1, P * k:P * (k + 1)], band[:, 1, k // 2, P:BAND],
                                                        start=False, stop=True)
                        last.then_inc(turn_ps, 1)
                else:
                    b = turn()
                    pe.wait_ge(st_ld, 32)
                    for k in range(KD):
                        out = bank(b, KD, DB)[:, k, :]
                        nc.tensor.matmul(out, state[0:DB * CTX, P * k:P * (k + 1)], band_s[0:DB * CTX, k // 2, :],
                                         start=True, stop=False)
                        last = nc.tensor.matmul(out, X[0:DB, 4, P * k:P * (k + 1)], own_s[0:DB, k // 2, :],
                                                start=False, stop=True)
                    last.then_inc(turn_ps, 1)

            def router(L, i):
                n = rows_of(i)
                pe.wait_ge(ln_out[L], i + 1)
                for g in range(2):
                    transpose_x(i, g, turn()).then_inc(turn_ps, 1)
                pe.wait_ge(turn_ev, turns[0])
                if i == 0:
                    pe.wait_ge(lg_zero, L + 1)
                for k in range(KD):
                    last = nc.tensor.matmul(bank(6, NT, E)[0:n, i, :], xr[L][i % 2][:, k, 0:n], wr[:, k, :],
                                            start=(k == 0), stop=(k == KD - 1))
                if i == NT - 1:
                    last.then_inc(lg_ps, 1)

            def counts(L):
                pe.wait_ge(sel_set, L + 1)
                cum = bank(6, NT, E, off=128)
                selt = r_sel.rearrange("p (a b) -> p a b", a=NT)
                nc.tensor.matmul(cum, before, selt, start=True, stop=False)
                for j in range(NT - 1):
                    nc.tensor.matmul(cum[:, j + 1:NT, :], ones, selt[:, j:j + 1, :].to_broadcast([P, NT - 1 - j, E]),
                                     start=False, stop=(j == NT - 2))
                for j in range(NT):
                    last = nc.tensor.matmul(bank(6, E, off=256), ones, selt[:, j, :], start=(j == 0), stop=(j == NT - 1))
                last.then_inc(cnt_ps, 1)

            def experts(L):
                q = S[L]

                def turn_rows(tl, s):
                    for g in range(2):
                        for c in range(4):
                            k = 4 * g + c
                            last = nc.tensor.transpose(bank(6 + g, 4, CAP)[:, c, :], xe[s][0:CAP, P * k:P * (k + 1)],
                                                       ident[0:CAP, 0:CAP])
                        last.then_inc(q["tr_ps"], 1)

                def tile(u, s):
                    tl = 2 * u + s
                    w = 1 - s
                    pe.wait_ge(q["xeT_set"], 2 * tl + 2)
                    pe.wait_ge(q["wg_ld"][w], 16 * (u + 1))
                    for f in range(KF):
                        for k in range(KD):
                            last = nc.tensor.matmul(bank(s, KF, CAP)[:, f, :], wg[w][:, k, P * f:P * (f + 1)], xeT[s][:, k, :],
                                                    start=(k == 0), stop=(k == KD - 1))
                    last.then_inc(q["gate_ps"][s], 1)
                    pe.wait_ge(q["wu_ld"][w], 16 * (u + 1))
                    for f in range(KF):
                        for k in range(KD):
                            last = nc.tensor.matmul(bank(2 + s, KF, CAP)[:, f, :], wu[w][:, k, P * f:P * (f + 1)], xeT[s][:, k, :],
                                                    start=(k == 0), stop=(k == KD - 1))
                    last.then_inc(q["up_ps"][s], 1)
                    pe.wait_ge(q["xe_ld"][1 - s], 16 * (u + 1 + s))
                    turn_rows(tl + 1, 1 - s)
                    pe.wait_ge(q["h_set"], tl + 1)
                    pe.wait_ge(q["wd_ld"][w], 16 * (u + 1))
                    pe.wait_ge(q["y_set"], 2 * tl + 2)
                    for hf in range(2):
                        for f in range(KF):
                            last = nc.tensor.matmul(bank(4 + hf)[0:CAP, :], h[s][:, f, :], wd[w][:, f, 512 * hf:512 * (hf + 1)],
                                                    start=(f == 0), stop=(f == KF - 1))
                    last.then_inc(q["down_ps"][s], 1)

                pe.wait_ge(tab_set, 2 * L + 2)
                nh = pe.value_load(n_half[0:1, 0:1], min_val=E // 2, max_val=TILES // 2)
                pe.wait_ge(turn_ev, turns[0])
                pe.wait_ge(q["xe_ld"][0], 16)
                turn_rows(0, 0)
                with pe.Fori(0, nh) as u:
                    for s in range(2):
                        tile(u, s)

            pe.wait_ge(wo_ld, 16)
            pe.wait_ge(act_ev, 4 * PAIRS)
            pe.sem_inc(pv_ps, 2)
            pe.wait_ge(router_ld, 32)
            mix(0, 0)
            for i in range(1, 4):
                mix(0, i)
                router(0, i - 1)
            latent_q()
            turn_pages(0, 0, 1)
            pe.wait_ge(tp_ev[0], 3)
            pe.wait_ge(tp_ev[1], 3)
            router(0, 3)
            samples()
            pe.wait_ge(uv_ev, 1)
            mix(0, 4)
            router(0, 4)
            counts(0)
            experts(0)
            pool_turns = []

            def pool_then(i):
                pool(i)
                pool_turns.append(turns[0])

            def mix_pooled(i):
                pe.wait_ge(turn_ev, pool_turns[i])
                if i == 0:
                    pe.wait_ge(wp_ready, 1)
                mix(1, i)

            pool_then(0)
            for i in range(1, 5):
                pool_then(i)
                mix_pooled(i - 1)
            router(1, 0)
            mix_pooled(4)
            for i in range(1, NT):
                router(1, i)
            counts(1)
            experts(1)

        @block.gpsimd
        def _(pool_e):
            nc.gpsimd.memset(zero_src, 0.0).then_inc(zero_set, 1)

            def copy_even():
                nc.gpsimd.tensor_copy(wuq[:, :, 0:HQ], wqn[:, :, 0:HQ])
                nc.gpsimd.tensor_copy(wuq[:, :, 96:112], wqn[:, :, 80:96])
                nc.gpsimd.tensor_copy(wuq[:, :, 112:128], wqn[:, :, 64:80]).then_inc(wq_even, 1)

            def copy_odd():
                nc.gpsimd.tensor_copy(wuq[:, :, 128:160], wqn[:, :, 160:192])
                nc.gpsimd.tensor_copy(wuq[:, :, 160:176], wqn[:, :, 176:192])
                nc.gpsimd.tensor_copy(wuq[:, :, 176:192], wqn[:, :, 160:176])
                nc.gpsimd.tensor_copy(wuq[:, :, 192:256], wqn[:, :, 96:160]).then_inc(wq_odd, 1)

            hold(pool_e, wqn_ld, 16)
            copy_even()
            copy_odd()
            with pool_e.Fori(1, PAIRS) as j:
                hold(pool_e, wqn_ld, 16 * (j + 1))
                hold(pool_e, q_ps, 4 * j - 2)
                copy_even()
                hold(pool_e, q_ps, 4 * j)
                copy_odd()

            def repeat_keys(b, s, use):
                hold(pool_e, page_ld[s], 256 * use)
                nc.gpsimd.tensor_copy(krp[s][:, :, 1:4, :], krp[s][:, :, 0:1, :].to_broadcast([P, NPAGES, 3, ROPE])
                                      ).then_inc(kr_dup, 1)

            def shift(L, which, i):
                n = rows_of(i)
                if i == 0:
                    hold(pool_e, gb_ld[L][which], 32)
                hold(pool_e, ln_gam[L], NT * which + i + 1)
                nc.gpsimd.tensor_tensor(X[0:n, i, :], X[0:n, i, :], gb[0:n, 2 * which + 1, :], ALU.add).then_inc(ln_out[L], 1)

            repeat_keys(0, 0, 1)
            for i in range(4):
                shift(0, 0, i)
            with pool_e.Fori(0, (DB - 2) // 3) as u:
                for d in (1, 2, 3):
                    repeat_keys(3 * u + d, d % 3, u + 1 + d // 3)
            repeat_keys(DB - 1, 1, 3)
            hold(pool_e, uv_ps, 1)
            pool_e.dma_start(wpool, t["w_pool"][0].rearrange("g (k p) d -> p (g k) d", p=P)).then_inc(wp_ld, 16)

            for L in range(2):
                q = S[L]
                for i in ((4,) if L == 0 else range(NT)):
                    shift(L, 0, i)
                hold(pool_e, idx_set, 2 * (L + 1))
                hold(pool_e, zero_st, 16 * (PAIRS - 1))
                hold(pool_e, ln_out[L], NT)
                for i in range(NT):
                    for idx in (idx_a, idx_b):
                        pool_e.indirect_dma_start(
                            xs[:, :], bass.IndirectOffsetOnAxis(ap=idx[0:rows_of(i), i:i + 1], axis=0),
                            X[0:rows_of(i), i, :], None).then_inc(scat, 16)
                if L == 0:
                    pool_e.dma_start(gb[:, 0, :], bcast(t["ln1_g"][1])).then_inc(gb_ld[1][0], 16)
                    pool_e.dma_start(gb[:, 1, :], bcast(t["ln1_b"][1])).then_inc(gb_ld[1][0], 16)
                hold(pool_e, scat, 160 * (L + 1))
                hold(pool_e, tab_set, 2 * L + 2)
                nh = pool_e.value_load(n_half[0:1, 0:1], min_val=E // 2, max_val=TILES // 2)
                hold(pool_e, turn_ev, 10 if L == 0 else 29)
                pool_e.dma_start(xe[0][0:CAP, :], xs[0:CAP, :]).then_inc(q["xe_ld"][0], 16)
                with pool_e.Fori(0, nh) as u:
                    for s in range(2):
                        tl = 2 * u + s
                        hold(pool_e, q["tr_ps"], 2 * tl + 2)
                        pool_e.dma_start(xe[1 - s][0:CAP, :], xs[bass.ds(CAP * (tl + 1), CAP), :]).then_inc(q["xe_ld"][1 - s], 16)
                        hold(pool_e, q["y_set"], 2 * tl + 4)
                        pool_e.dma_start(yd[bass.ds(CAP * tl, CAP), :], ys[s][0:CAP, :]).then_inc(q["y_st"][s], 16)
                for s in range(2):
                    hold(pool_e, q["y_st"][s], 16 * nh)

                def gather(i):
                    n, s = rows_of(i), i % 2
                    if i >= 2:
                        hold(pool_e, ln_z[L], NT + i - 1)
                    for idx, y in ((idx_a, ya), (idx_b, yb)):
                        pool_e.indirect_dma_start(y[s][0:n, :], None, yd[:, :],
                                                  bass.IndirectOffsetOnAxis(ap=idx[0:n, i:i + 1], axis=0)).then_inc(gath[s], 16)

                gather(0)
                gather(1)
                if L == 0:
                    hold(pool_e, q["tr_ps"], 4 * nh + 2)
                    pool_e.dma_start(pscale, bcast(t["pool_scale"][0])).then_inc(st_ld, 16)
                    pool_e.dma_start(state[0:DB * CTX, :], t["state_pool"][0].rearrange("b c d -> (b c) d")).then_inc(st_ld, 16)
                for i in range(NT):
                    if i + 2 < NT:
                        gather(i + 2)
                    shift(L, 1, i)
                if L == 0:
                    hold(pool_e, ln_out[0], 2 * NT)
                    pool_e.dma_start(gb[:, 2, :], bcast(t["ln2_g"][1])).then_inc(gb_ld[1][1], 16)
                    pool_e.dma_start(gb[:, 3, :], bcast(t["ln2_b"][1])).then_inc(gb_ld[1][1], 16)

        @block.scalar
        def _(act):
            act.wait_ge(kraw_zero, 1)
            for i in range(NT):
                act.wait_ge(xt_ps, 2 * i + 2)
                nc.scalar.activation(XT[:, 4:8, P * i:P * i + rows_of(i)], bank((2 * i + 1) % 4, 4, P)[:, :, 0:rows_of(i)],
                                     ACT.Copy).then_inc(xt_ev[1], 1)
            for n in range(2 * MQ):
                act.wait_ge(cq_copied, n + 1)
                part = (slice(None), n // 2, slice(HALF * (n % 2), HALF * (n % 2 + 1)))
                nc.scalar.activation(sq[part], cq[part], ACT.Square).then_inc(cq_squared, 1)
            act.wait_ge(c_ld, 16)
            for i in range(NT):
                n = rows_of(i)
                raw = bank(4 + i % 2, KVL + ROPE)[0:n, :]
                act.wait_ge(kv_ps, i + 1)
                nc.scalar.activation(kraw[0:n, i, :], raw[:, KVL:], ACT.Copy)
                nc.scalar.activation(sqj[0:n, :], raw[:, 0:KVL], ACT.Square, accum_out=ss[0:n, i:i + 1]).then_inc(kv_ss, 1)
                act.wait_ge(kv_ss, i + 1)
                nc.scalar.activation(kstd[0:n, i:i + 1], ss[0:n, i:i + 1], ACT.Sqrt, scale=1.0 / KVL, bias=rms_eps[0:n, :]
                                     ).then_inc(kv_std, 1)
            for hf in range(2):
                act.wait_ge(cq_sum, hf + 1)
                nc.scalar.activation(rq[:, HALF * hf:HALF * (hf + 1)], bank(hf, HALF), ACT.Sqrt, scale=1.0 / QL,
                                     bias=rms_eps).then_inc(rq_std, 1)
            for i in range(NT):
                n = rows_of(i)
                act.wait_ge(ck_ps, i + 1)
                nc.scalar.activation(ckT[:, :, P * i:P * i + n], bank(6 + i % 2, 3, P)[:, :, 0:n], ACT.Copy).then_inc(ck_ev, 1)

            def take_v(j, n):
                act.wait_ge(for_act, n)
                nc.scalar.activation(V[:, :, bass.ds(P * j, P)], bank(4, 4, P), ACT.Copy).then_inc(act_ev, 1)

            def take_k(j, n):
                act.wait_ge(for_act, n)
                nc.scalar.activation(kT[0][0:64, :], bank(7)[0:64, :], ACT.Copy)
                nc.scalar.activation(kT[1][64:128, :], bank(7)[64:128, :], ACT.Copy).then_inc(act_ev, 1)
                act.wait_ge(for_act, n + 1)
                nc.scalar.activation(wukT[:, bass.ds(j, 1), :], bank(4, 1, KVL), ACT.Copy).then_inc(act_ev, 1)

            def exps(p, par):
                for i in (3, 2, 1, 0):
                    act.wait_ge(min_set, 8 * p + 4 * par + scored(i))
                    c = 4 * par + i
                    nc.scalar.activation(prob[:, i, 0:P * (i + 1)], score(i), ACT.Exp, scale=-1.0,
                                         bias=mneg[:, c:c + 1], accum_out=rsum[:, c:c + 1]).then_inc(exp_set, 1)

            def take_probs(p, par, i):
                act.wait_ge(t_ps, 8 * p + 4 * par + 4 - i)
                nc.scalar.activation(probT[:, 1, 0:P * (i + 1)], bank(6, P * (i + 1)), ACT.Copy).then_inc(pt_ev[1], 1)

            def take_heads(p, n):
                act.wait_ge(for_act, n)
                nc.scalar.activation(oT[:, bass.ds(p, 1), 0:SEQ], bank(7, 1, SEQ), ACT.Copy).then_inc(act_ev, 1)

            def pair(p, after_one, more):
                if after_one:
                    take_heads(p - 1, 4 * p + 3)
                exps(p, 0)
                take_probs(p, 0, 3)
                if more:
                    take_v(p + 1, 4 * p + 4)
                take_probs(p, 0, 1)
                exps(p, 1)
                take_probs(p, 1, 3)
                if more:
                    take_k(p + 1, 4 * p + 5)
                take_probs(p, 1, 1)

            act.wait_ge(rq_std, 2)
            act.wait_ge(cq_done, 1)
            act.wait_ge(latent_st, 16 * 10)
            take_v(0, 1)
            take_k(0, 2)
            pair(0, False, True)
            with act.Fori(1, PAIRS - 1) as p:
                pair(p, True, True)
            pair(PAIRS - 1, True, False)
            take_heads(PAIRS - 1, 4 * PAIRS)

            turns = [0]

            def take_turn(dst, src_dims, cols=None):
                n = turns[0]
                turns[0] += 1
                act.wait_ge(turn_ps, n + 1)
                src = bank(turn_bank[n % 3], *src_dims)
                nc.scalar.activation(dst, src if cols is None else src[:, :, 0:cols], ACT.Copy).then_inc(turn_ev, 1)

            def normalise(L, which, i):
                n = rows_of(i)
                k = NT * which + i + 1
                act.wait_ge(ln_agg[L], k)
                nc.scalar.activation(std[0:n, i:i + 1], mv[0:n, i, 1:2], ACT.Sqrt, bias=ln_eps[0:n, :]).then_inc(ln_std[L], 1)
                act.wait_ge(ln_rstd[L], k)
                nc.scalar.activation(X[0:n, i, :], X[0:n, i, :], ACT.Identity, scale=rstd[0:n, i:i + 1],
                                     bias=nmr[0:n, i:i + 1]).then_inc(ln_nrm[L], 1)

            def take_rows(L, i):
                for g in range(2):
                    take_turn(xr[L][i % 2][:, 4 * g:4 * g + 4, 0:rows_of(i)], (4, P), rows_of(i))

            def experts(L):
                q = S[L]
                act.wait_ge(lg_ps, L + 1)
                nc.scalar.activation(r_exp, bank(6, NT * E), ACT.Exp, scale=-1.0).then_inc(lg_exp, 1)
                act.wait_ge(tab_set, 2 * L + 2)
                nh = act.value_load(n_half[0:1, 0:1], min_val=E // 2, max_val=TILES // 2)
                act.sem_inc(q["y_set"], 1)
                act.wait_ge(q["tr_ps"], 1)
                nc.scalar.activation(xeT[0][:, 0:4, :], bank(6, 4, CAP), ACT.Copy).then_inc(q["xeT_set"], 1)
                act.wait_ge(scat, 160 * (L + 1))
                for i in range(NT):
                    n = rows_of(i)
                    nc.scalar.activation(X[0:n, i, :], X[0:n, i, :], ACT.Copy, scale=ALPHA).then_inc(xscaled, 1)

                def tile(u, s, stored):
                    tl = 2 * u + s
                    act.wait_ge(q["gate_ps"][s], u + 1)
                    nc.scalar.activation(sg[s], bank(s, KF, CAP), ACT.Silu).then_inc(q["sg_set"], 1)
                    act.wait_ge(q["tr_ps"], 2 * tl + 3)
                    nc.scalar.activation(xeT[1 - s][:, 0:4, :], bank(6, 4, CAP), ACT.Copy).then_inc(q["xeT_set"], 1)
                    act.wait_ge(q["down_ps"][s], u + 1)
                    if stored:
                        act.wait_ge(q["y_st"][s], 16 * u)
                    nc.scalar.activation(ys[s][0:CAP, 0:512], bank(4)[0:CAP, :], ACT.Copy).then_inc(q["y_set"], 1)

                tile(0, 0, False)
                tile(0, 1, False)
                with act.Fori(1, nh) as u:
                    tile(u, 0, True)
                    tile(u, 1, True)

            def take_pages(b):
                for n in (1, 3, 5):
                    act.wait_ge(tp_ps, 6 * b + n + 1)
                    nc.scalar.activation(kpT[:, n // 2, 512:1024], bank(5), ACT.Copy).then_inc(tp_ev[1], 1)

            def take_latent_out(b):
                act.wait_ge(ol_ps, b + 1)
                nc.scalar.activation(olat[:, :, bass.ds(b, 1), :], bank(3, MKV, 1, H), ACT.Copy).then_inc(ol_ev, 1)

            def sample(b, after_one, more):
                act.wait_ge(smin_set, b + 1)
                nc.scalar.activation(ps_s[0:H, :], view(PS, 0, PAST + DB)[0:H, :], ACT.Exp, scale=-1.0,
                                     bias=s_mneg[0:H, :], accum_out=s_sum[0:H, :]).then_inc(sexp_set, 1)
                if after_one:
                    take_latent_out(b - 1)
                if more:
                    take_pages(b + 1)

            def samples():
                sample(0, False, True)
                with act.Fori(1, DB - 1) as b:
                    sample(b, True, True)
                sample(DB - 1, True, False)
                take_latent_out(DB - 1)

            normalise(0, 0, 0)
            for i in range(1, 4):
                take_rows(0, i - 1)
                normalise(0, 0, i)
            act.wait_ge(zero_st, 16 * (PAIRS - 1))
            take_pages(0)
            take_rows(0, 3)
            samples()
            normalise(0, 0, 4)
            take_rows(0, 4)
            experts(0)
            for step in range(2 * NT + 1):
                if step < NT:
                    normalise(0, 1, step)
                if 2 <= step < NT + 2:
                    i = step - 2
                    if i < 4:
                        for g in range(2):
                            take_turn(poolT[:, 4 * g:4 * g + 4, P * i:P * (i + 1)], (4, P))
                    else:
                        take_turn(poolT[:, :, SEQ:TOK], (KD, DB))
                if 4 <= step < NT + 4:
                    normalise(1, 0, step - 4)
                if step == 6:
                    act.wait_ge(ln_z[0], 2 * NT)
                if step >= 6:
                    take_rows(1, step - 6)
            experts(1)
            for i in range(NT):
                normalise(1, 1, i)

        @block.vector
        def _(dve):
            chain = [0]

            def link(ins):
                chain[0] += 1
                ins.then_inc(dve_step, 1)
                dve.wait_ge(dve_step, chain[0])

            v = nc.vector
            v.memset(kraw[:, 4, :], 0.0).then_inc(kraw_zero, 1)
            v.memset(qs, 0.0)
            link(v.memset(qr, 0.0))
            for i in range(NT):
                dve.wait_ge(xt_ps, 2 * i + 1)
                v.tensor_copy(XT[:, 0:4, P * i:P * i + rows_of(i)], bank((2 * i) % 4, 4, P)[:, :, 0:rows_of(i)]).then_inc(xt_ev[0], 1)
            for n in range(2 * MQ):
                dve.wait_ge(cq_ps, n + 1)
                v.tensor_copy(cq[:, n // 2, HALF * (n % 2):HALF * (n % 2 + 1)], bank(n % 4, HALF)).then_inc(cq_copied, 1)
            dve.wait_ge(gain_ld, 32)
            dve.wait_ge(c_ld, 16)
            for i in range(NT):
                n = rows_of(i)
                dve.wait_ge(kv_std, i + 1)
                link(v.reciprocal(krs[0:n, i:i + 1], kstd[0:n, i:i + 1]))
                v.scalar_tensor_tensor(out=ckv[0:n, i, :], in0=bank(4 + i % 2, KVL)[0:n, :], scalar=krs[0:n, i:i + 1],
                                       in1=gkv[0:n, :], op0=ALU.mult, op1=ALU.mult).then_inc(kv_ready, 1)
            half = ROPE // 2
            x1, x2 = kraw[:, :, 0:half], kraw[:, :, half:ROPE]
            tmp = [rtmp[:, a, :].rearrange("p (a b) -> p a b", a=NT) for a in range(4)]
            v.tensor_tensor(tmp[0], x1, cos_k, ALU.mult)
            v.tensor_tensor(tmp[1], x2, sin_k, ALU.mult)
            v.tensor_tensor(tmp[2], x1, sin_k, ALU.mult)
            link(v.tensor_tensor(tmp[3], x2, cos_k, ALU.mult))
            v.tensor_tensor(krot[:, :, 0:half], tmp[0], tmp[1], ALU.subtract)
            v.tensor_tensor(krot[:, :, half:ROPE], tmp[2], tmp[3], ALU.add).then_inc(kr_ready, 1)
            dve.wait_ge(kr_ready, 1)
            v.tensor_copy(kdup, krot.unsqueeze(2).to_broadcast([P, NT, 4, ROPE])).then_inc(kr_ready, 1)
            dve.wait_ge(rq_std, 2)
            link(v.reciprocal(rq, rq))
            for m in range(MQ):
                ins = v.scalar_tensor_tensor(out=cq[:, m, :], in0=cq[:, m, :], scalar=gq[:, m:m + 1], in1=rq, op0=ALU.mult,
                                             op1=ALU.mult)
            ins.then_inc(cq_done, 1)
            dve.wait_ge(ck_ev, 4)
            v.tensor_copy(kT[0][64:128, :], ckT[64:128, 2, 0:SEQ])
            v.tensor_copy(kT[1][0:64, :], ckT[0:64, 2, 0:SEQ]).then_inc(krope_set, 1)

            def take_q(j, parity, hf, n):
                b = 7 if (parity + hf) == 1 else 4
                ps = bank(b, HALF)
                tab = rope_q[:, parity, HALF * hf:HALF * (hf + 1)]
                dve.wait_ge(q_ps, n)
                ins = v.tensor_tensor(qT[parity][:, HALF * hf:HALF * (hf + 1)], ps, tab, ALU.mult)
                if hf:
                    lo, hi = (slice(0, 64), slice(64, 128)) if parity == 0 else (slice(64, 128), slice(0, 64))
                    c = slice(HALF - DB, HALF)
                    v.tensor_tensor(qs[lo, bass.ds(j, 1), DB * parity:DB * (parity + 1)], ps[lo, c].unsqueeze(1),
                                    tab[lo, c].unsqueeze(1), ALU.mult)
                    ins = v.tensor_tensor(qr[hi, :, bass.ds(2 * j + parity, 1)], ps[hi, c].unsqueeze(2),
                                          tab[hi, c].unsqueeze(2), ALU.mult)
                ins.then_inc(q_ev, 1)

            def mins(p, par):
                for i in (3, 2, 1, 0):
                    hold(dve, s_ps, 8 * p + 4 * par + scored(i))
                    w = P * (i + 1)
                    sc = score(i)
                    v.tensor_tensor_reduce(sc, sc, causal[:, SEQ - w:SEQ], 1.0, BIG, ALU.add, ALU.min,
                                           mneg[:, 4 * par + i:4 * par + i + 1]).then_inc(min_set, 1)

            def take_probs(p, par):
                for i in (2, 0):
                    dve.wait_ge(t_ps, 8 * p + 4 * par + 4 - i)
                    v.tensor_copy(probT[:, 0, 0:P * (i + 1)], bank(5, P * (i + 1))).then_inc(pt_ev[0], 1)

            def head_out(p, par):
                dve.wait_ge(exp_set, 8 * p + 4 * par + 4)
                v.reciprocal(rinv[:, 4 * par:4 * par + 4], rsum[:, 4 * par:4 * par + 4]).then_inc(rinv_set, 1)
                dve.wait_ge(rinv_set, 2 * p + par + 1)
                dve.wait_ge(o_ps, 2 * p + par + 1)
                v.tensor_tensor(osb[:, :, VH * par:VH * (par + 1)], bank(3, 4, VH, off=256 * par),
                                rinv[:, 4 * par:4 * par + 4].unsqueeze(2).to_broadcast([P, 4, VH]), ALU.mult).then_inc(o_ev, 1)

            def pair(p, more):
                for par in range(2):
                    mins(p, par)
                    if more:
                        take_q(p + 1, par, 0, 4 * p + 5 + 2 * par)
                        take_q(p + 1, par, 1, 4 * p + 6 + 2 * par)
                    take_probs(p, par)
                    head_out(p, par)

            for par in range(2):
                for hf in range(2):
                    take_q(0, par, hf, 2 * par + hf + 1)
            with dve.Fori(0, PAIRS - 1) as p:
                pair(p, True)
            pair(PAIRS - 1, False)

            def set_qb(b, s):
                v.tensor_copy(qb[s][:, 0:MKV, :].unsqueeze(2), qlat[:, :, bass.ds(b, 1), :])
                v.tensor_copy(qb[s][:, MKV:MKV + 1, :], qr[:, bass.ds(b, 1), :]).then_inc(qb_set, 1)

            def take_pages(b):
                for n in (0, 2, 4):
                    dve.wait_ge(tp_ps, 6 * b + n + 1)
                    v.tensor_copy(kpT[:, n // 2, 0:512], bank(4)).then_inc(tp_ev[0], 1)

            def sample(b, more_in):
                if more_in is not None:
                    set_qb(b + 1, more_in)
                dve.wait_ge(sc_ps, b + 1)
                v.tensor_tensor(bank(2, 1, DB)[0:H, :, :], bank(2, 1, DB)[0:H, :, :], own_sample[0:H, bass.ds(b, 1), :], ALU.add
                                ).then_inc(new_masked, 1)
                dve.wait_ge(new_masked, b + 1)
                v.tensor_reduce(s_mneg[0:H, :], view(PS, 0, PAST + DB)[0:H, :], AXX, ALU.min).then_inc(smin_set, 1)
                if more_in is not None:
                    take_pages(b + 1)
                dve.wait_ge(spT_ps, b + 1)
                turned = bank(6, NPAGES + 1, H, off=256)
                v.tensor_copy(psT_s[:, 0:NPAGES, :], turned[:, 0:NPAGES, :])
                v.tensor_copy(psT_s[0:DB, NPAGES, :], turned[0:DB, NPAGES, :]).then_inc(spT_ev, 1)
                dve.wait_ge(sexp_set, b + 1)
                v.reciprocal(s_inv[0:H, :], s_sum[0:H, :]).then_inc(sinv_set, 1)
                dve.wait_ge(sinv_set, b + 1)
                dve.wait_ge(pv_ps, b + 3)
                v.tensor_scalar(onat[0:H, :], bank(7, KVL)[0:H, :], s_inv[0:H, :], None, ALU.mult).then_inc(onat_set, 1)

            def samples():
                dve.wait_ge(ql_ps, 1)
                for c in range(MKV):
                    ins = v.tensor_copy(qlat[:, c, :, :].rearrange("p b (j e) -> p j e b", e=2),
                                        bank(3, MKV, PAIRS, 16)[:, c, :, :].rearrange("p j (e b) -> p j e b", e=2))
                ins.then_inc(ql_ev, 1)
                dve.wait_ge(ql_ev, 1)
                set_qb(0, 0)
                dve.wait_ge(zero_st, 16 * (PAIRS - 1))
                take_pages(0)
                sample(0, 1)
                with dve.Fori(0, (DB - 2) // 3) as u:
                    for d in (1, 2, 3):
                        sample(3 * u + d, (d + 1) % 3)
                sample(DB - 1, None)
                dve.wait_ge(uv_ps, 1)
                for e in range(2):
                    part = slice(64 * e, 64 * e + 64)
                    ins = v.tensor_copy(oT[part, :, SEQ:TOK].unsqueeze(3), bank(3, PAIRS, DB, 2, off=256)[part, :, :, e:e + 1])
                ins.then_inc(uv_ev, 1)

            def stats(L, which, i):
                n = rows_of(i)
                k = NT * which + i + 1
                x = X[0:n, i, :]
                if which == 0:
                    dve.wait_ge(mix_ps, NT * L + i + 1)
                    v.scalar_tensor_tensor(out=x, in0=x, scalar=ALPHA, in1=view(PS, 1024 * (i % 2), D)[0:n, :],
                                           op0=ALU.mult, op1=ALU.add).then_inc(ln_z[L], 1)
                else:
                    s = i % 2
                    dve.wait_ge(gath[s], 32 * ((3 * L if s == 0 else 2 * L) + i // 2 + 1))
                    dve.wait_ge(xscaled, NT * L + i + 1)
                    link(v.scalar_tensor_tensor(out=x, in0=ya[s][0:n, :], scalar=ca[0:n, i:i + 1], in1=x,
                                                op0=ALU.mult, op1=ALU.add))
                    v.scalar_tensor_tensor(out=x, in0=yb[s][0:n, :], scalar=cb[0:n, i:i + 1], in1=x,
                                           op0=ALU.mult, op1=ALU.add).then_inc(ln_z[L], 1)
                dve.wait_ge(ln_z[L], k)
                for c in range(2):
                    ins = v.bn_stats(bn[0:n, i, 6 * c:6 * c + 6], X[0:n, i, 512 * c:512 * (c + 1)])
                link(ins)
                v.bn_aggr(mv[0:n, i, :], bn[0:n, i, :]).then_inc(ln_agg[L], 1)

            def spread(L, which, i):
                n = rows_of(i)
                k = NT * which + i + 1
                dve.wait_ge(ln_std[L], k)
                link(v.reciprocal(rstd[0:n, i:i + 1], std[0:n, i:i + 1]))
                v.tensor_scalar(nmr[0:n, i:i + 1], mv[0:n, i, 0:1], rstd[0:n, i:i + 1], -1.0, ALU.mult, ALU.mult).then_inc(ln_rstd[L], 1)

            def gain(L, which, i):
                n = rows_of(i)
                dve.wait_ge(ln_nrm[L], NT * which + i + 1)
                if i == 0:
                    dve.wait_ge(gb_ld[L][which], 32)
                v.tensor_tensor(X[0:n, i, :], X[0:n, i, :], gb[0:n, 2 * which, :], ALU.mult).then_inc(ln_gam[L], 1)

            def norm(L, which, i):
                stats(L, which, i)
                spread(L, which, i)
                gain(L, which, i)

            def route(L):
                def five(a):
                    return a.rearrange("p (a b) -> p a b", a=NT)

                def by_group(a):
                    return a.rearrange("p (a b) -> p a b", b=EPG)

                over = [P, NT, E]
                dve.wait_ge(lg_exp, L + 1)
                link(v.tensor_scalar_add(r_exp, r_exp, 1.0))
                link(v.reciprocal(r_s, r_exp))
                if L == 0:
                    dve.wait_ge(router_ld, 32)
                link(v.tensor_tensor(five(r_bias), five(r_s), bias_row.unsqueeze(1).to_broadcast(over), ALU.add))
                b4 = by_group(r_bias)
                sums = r_big[:, 0:120].rearrange("p (a b) -> p a b", b=6)
                v.tensor_tensor(sums[:, :, 0:3], b4[:, :, 0:3], b4[:, :, 1:4], ALU.add)
                v.tensor_tensor(sums[:, :, 3:5], b4[:, :, 0:2], b4[:, :, 2:4], ALU.add)
                link(v.tensor_tensor(sums[:, :, 5:6], b4[:, :, 0:1], b4[:, :, 3:4], ALU.add))
                link(v.tensor_reduce(r_gs, sums, AXX, ALU.max))
                gs, gp, gsel = (a.rearrange("p (a b) -> p a b", a=NT) for a in (r_gs, r_gp, r_gsel))
                link(v.tensor_reduce(r_m, gs, AXX, ALU.max))
                link(v.tensor_tensor(gp, gs, r_m.unsqueeze(2).to_broadcast([P, NT, GROUPS]), ALU.is_equal))
                link(v.tensor_tensor(gp, gp, prefer.unsqueeze(1).to_broadcast([P, NT, GROUPS]), ALU.mult))
                link(v.tensor_reduce(r_m, gp, AXX, ALU.max))
                link(v.tensor_tensor(gsel, gp, r_m.unsqueeze(2).to_broadcast([P, NT, GROUPS]), ALU.is_equal))
                cmp = r_big.rearrange("p (a j i) -> p a j i", j=EPG, i=EPG)
                wide = [P, NT * GROUPS, EPG, EPG]
                bi, bj = b4.unsqueeze(2).to_broadcast(wide), b4.unsqueeze(3).to_broadcast(wide)
                link(v.tensor_tensor(cmp, bi, bj, ALU.is_equal))
                link(v.tensor_tensor(cmp, cmp, earlier.unsqueeze(1).to_broadcast(wide), ALU.mult))
                link(v.tensor_reduce(by_group(r_rank), cmp, AXX, ALU.add))
                link(v.tensor_tensor(cmp, bi, bj, ALU.is_gt))
                link(v.tensor_reduce(by_group(r_comb), cmp, AXX, ALU.add))
                link(v.tensor_tensor(r_rank, r_rank, r_comb, ALU.add))
                link(v.scalar_tensor_tensor(out=by_group(r_sel), in0=by_group(r_rank), scalar=float(2),
                                            in1=r_gsel.unsqueeze(2).to_broadcast([P, NT * GROUPS, EPG]),
                                            op0=ALU.is_lt, op1=ALU.mult))
                link(v.tensor_tensor(r_comb, r_s, r_sel, ALU.mult))
                link(v.tensor_reduce(r_den, five(r_comb), AXX, ALU.add))
                link(v.reciprocal(r_den, r_den))
                link(v.tensor_tensor(five(r_comb), five(r_comb), r_den.unsqueeze(2).to_broadcast(over), ALU.mult))
                v.tensor_scalar(r_sel[:, 64:80], r_sel[:, 64:80], real_row, None, ALU.mult).then_inc(sel_set, 1)
                dve.wait_ge(cnt_ps, L + 1)
                cum = bank(6, NT, E, off=128)
                link(v.tensor_copy(r_nt, bank(6, E, off=256)))
                k5 = r_k[:, 0:E * KOV].rearrange("p (a b) -> p a b", a=E)
                link(v.tensor_tensor(k5, r_nt.unsqueeze(2).to_broadcast([P, E, KOV]),
                                     steps.unsqueeze(1).to_broadcast([P, E, KOV]), ALU.is_gt))
                link(v.tensor_reduce(r_ex, k5, AXX, ALU.add))
                tri = r_big[:, 0:E * E].rearrange("p (a b) -> p a b", a=E)
                link(v.tensor_tensor(tri, r_ex.unsqueeze(1).to_broadcast([P, E, E]), before_e, ALU.mult))
                link(v.tensor_reduce(r_ovb, tri, AXX, ALU.add))
                link(v.scalar_tensor_tensor(out=r_diff, in0=r_ovb, scalar=float(CAP), in1=slot_over, op0=ALU.mult, op1=ALU.add))
                link(v.tensor_scalar(five(r_slot), cum, float(CAP), None, ALU.is_ge))
                link(v.tensor_tensor(five(r_slot), five(r_slot), r_diff.unsqueeze(1).to_broadcast(over), ALU.mult))
                link(v.tensor_tensor(five(r_slot), five(r_slot), cum, ALU.add))
                link(v.tensor_tensor(five(r_slot), five(r_slot), slot0.unsqueeze(1).to_broadcast(over), ALU.add))
                link(v.scalar_tensor_tensor(out=r_slot, in0=r_slot, scalar=1.0, in1=r_sel, op0=ALU.add, op1=ALU.mult))
                v.tensor_reduce(r_all, five(r_slot), AXX, ALU.add)
                link(v.tensor_reduce(r_a, five(r_slot), AXX, ALU.max))
                v.tensor_scalar(idx_a, r_a, -1.0, None, ALU.add).then_inc(idx_set, 1)
                link(v.tensor_tensor(r_b, r_all, r_a, ALU.subtract))
                v.tensor_scalar(idx_b, r_b, -1.0, None, ALU.add).then_inc(idx_set, 1)
                link(v.tensor_tensor(five(r_bias), five(r_slot), r_a.unsqueeze(2).to_broadcast(over), ALU.is_equal))
                link(v.tensor_tensor(r_bias, r_bias, r_comb, ALU.mult))
                v.tensor_reduce(ca, five(r_bias), AXX, ALU.add)
                link(v.tensor_tensor(r_comb, r_comb, r_bias, ALU.subtract))
                v.tensor_reduce(cb, five(r_comb), AXX, ALU.add)
                one = slice(0, 1)
                v.tensor_copy(r_tab[one, 0:E], expert[one, :])
                link(v.tensor_tensor(r_end[one, :], r_ovb[one, :], r_ex[one, :], ALU.add))
                ke = r_k[one, 0:NOV * E].rearrange("p (a b) -> p a b", a=NOV)
                ks = r_big[one, 0:NOV * E].rearrange("p (a b) -> p a b", a=NOV)
                kk = over_k[one, :].unsqueeze(2).to_broadcast([1, NOV, E])
                v.tensor_tensor(ke, kk, r_ovb[one, :].unsqueeze(1).to_broadcast([1, NOV, E]), ALU.is_ge)
                link(v.tensor_tensor(ks, kk, r_end[one, :].unsqueeze(1).to_broadcast([1, NOV, E]), ALU.is_lt))
                link(v.tensor_tensor(ke, ke, ks, ALU.mult))
                link(v.tensor_tensor(ke, ke, expert[one, :].unsqueeze(1).to_broadcast([1, NOV, E]), ALU.mult))
                link(v.tensor_reduce(r_tab[one, E:TILES], ke, AXX, ALU.add))
                v.tensor_copy(tile_ids[one, 0:TILES], r_tab[one, 0:TILES]).then_inc(tab_set, 1)
                link(v.tensor_reduce(r_nov[one, :], r_ex[one, :], AXX, ALU.add))
                link(v.tensor_scalar(r_nh[one, 0:NOV // 2], even_k[one, :], r_nov[one, :], None, ALU.is_lt))
                link(v.tensor_reduce(r_nov[one, :], r_nh[one, 0:NOV // 2], AXX, ALU.add))
                v.tensor_scalar(n_half[one, :], r_nov[one, :], float(E // 2), None, ALU.add).then_inc(tab_set, 1)

            def experts(L):
                q = S[L]
                dve.wait_ge(tab_set, 2 * L + 2)
                nh = dve.value_load(n_half[0:1, 0:1], min_val=E // 2, max_val=TILES // 2)
                dve.sem_inc(q["y_set"], 1)
                dve.wait_ge(q["tr_ps"], 2)
                v.tensor_copy(xeT[0][:, 4:8, :], bank(7, 4, CAP)).then_inc(q["xeT_set"], 1)

                def tile(u, s, stored):
                    tl = 2 * u + s
                    dve.wait_ge(q["sg_set"], tl + 1)
                    dve.wait_ge(q["up_ps"][s], u + 1)
                    v.tensor_tensor(h[s], sg[s], bank(2 + s, KF, CAP), ALU.mult).then_inc(q["h_set"], 1)
                    dve.wait_ge(q["tr_ps"], 2 * tl + 4)
                    v.tensor_copy(xeT[1 - s][:, 4:8, :], bank(7, 4, CAP)).then_inc(q["xeT_set"], 1)
                    dve.wait_ge(q["down_ps"][s], u + 1)
                    if stored:
                        dve.wait_ge(q["y_st"][s], 16 * u)
                    v.tensor_copy(ys[s][0:CAP, 512:D], bank(5)[0:CAP, :]).then_inc(q["y_set"], 1)

                tile(0, 0, False)
                tile(0, 1, False)
                with dve.Fori(1, nh) as u:
                    tile(u, 0, True)
                    tile(u, 1, True)

            dve.wait_ge(act_ev, 4 * PAIRS)
            v.memset(bank(6, NT * E), 0.0).then_inc(lg_zero, 1)
            for i in range(4):
                norm(0, 0, i)
            samples()
            norm(0, 0, 4)
            route(0)
            experts(0)
            for step in range(NT + 5):
                if step == 2:
                    v.memset(bank(6, NT * E), 0.0).then_inc(lg_zero, 1)
                    dve.wait_ge(wp_ld, 16)
                    dve.wait_ge(st_ld, 32)
                    wp4 = wpool.rearrange("p (g k) d -> p g k d", g=4)
                    v.tensor_tensor(wp4, wp4, pscale.rearrange("p (g d) -> p g d", g=4).unsqueeze(2).to_broadcast([P, 4, 2, 256]),
                                    ALU.mult).then_inc(wp_ready, 1)
                for L, which, i in ((0, 1, step), (1, 0, step - 4)):
                    if i == 3 and L == 1:
                        dve.wait_ge(pool_out, 32)
                    if 0 <= i < NT:
                        stats(L, which, i)
                    if 1 <= i <= NT:
                        gain(L, which, i - 1)
                    if 0 <= i < NT:
                        spread(L, which, i)
            route(1)
            experts(1)
            for i in range(NT + 1):
                if i < NT:
                    stats(1, 1, i)
                if i:
                    gain(1, 1, i - 1)
                if i < NT:
                    spread(1, 1, i)


_INS = ["x_prompt", "x_sample", "cache_ckv", "cache_krope", "state_pool", "page_table", "w_dq", "g_q", "w_uq", "w_dkv",
        "g_kv", "w_uk", "w_uv", "w_o", "w_pool", "pool_scale", "w_router", "router_bias", "w_gate", "w_up", "w_down",
        "ln1_g", "ln1_b", "ln2_g", "ln2_b"]
_OUTS = [("o_y_p", (1, SEQ, D)), ("o_y_s", (DB, 1, D)), ("o_ckv_p", (1, 1, SEQ, KVL)), ("o_kr_p", (1, 1, SEQ, ROPE)),
         ("o_pool_p", (1, 1, CTX, D)), ("o_ckv_s", (1, DB, 1, KVL)), ("o_kr_s", (1, DB, 1, ROPE)),
         ("o_pool_s", (1, DB, CTX, D))]


def kernel(**inputs):
    import concourse.bacc as _bacc
    from concourse.bass_utils import run_bass_kernel_spmd as _run

    nc = _bacc.Bacc("TRN2", target_bir_lowering=False, num_devices=1)
    consts, place = constants()
    arrays, t = {"consts": consts}, {}
    for name in _INS:
        arrays[name] = np.ascontiguousarray(inputs[name])
    for name, a in arrays.items():
        t[name] = nc.dram_tensor(name, a.shape, mybir.dt.from_np(a.dtype), kind="ExternalInput").ap()
    for name, shape in _OUTS:
        t[name] = nc.dram_tensor(name, shape, F32, kind="ExternalOutput").ap()
    build(nc, t, consts.shape, place)
    r = _run(nc, [arrays], core_ids=[0])
    return tuple(r.results[0][name] for name, _ in _OUTS)
```

```python
from contextlib import ExitStack

import numpy as np

import concourse.bass as bass
from concourse import mybir

D = 1024
SEQ = 512
DB = 8
TOK = SEQ + DB
P = 128
NT = SEQ // P + 1
KD = D // P
H, NOPE, ROPE, VH = 16, 64, 32, 64
PAIRS = H // 2
QL, KVL = 384, 256
MQ, MKV = QL // P, KVL // P
HQ = NOPE + ROPE
PAGE, NPAGES, NPHYS = 128, 8, 80
PAST = PAGE * NPAGES
E, GROUPS, EPG, F = 16, 4, 4, 512
KF = F // P
CTX = 15
WINDOWS = (2, 4, 8, 16)
ALPHA = 4.0 ** 0.25
SCALE = HQ ** -0.5
LN_EPS, RMS_EPS = 1e-5, 1e-6
BIG = 1e30
HALF = TOK // 2
CAP = 96
KOV = (TOK - 1) // CAP
NOV = 10
TILES = E + NOV
BAND = P + CTX

F32 = mybir.dt.float32
I32 = mybir.dt.int32
ALU = mybir.AluOpType
ACT = mybir.ActivationFunctionType
AXX = mybir.AxisListType.X


def rows_of(i):
    return P if i < NT - 1 else DB


def constants():
    parts, place, at = [], {}, 0

    def put(name, a, *dims):
        nonlocal at
        full = np.zeros((P, int(np.prod(a.shape[1:]))), np.float32)
        full[:a.shape[0]] = a.reshape(a.shape[0], -1)
        parts.append(full)
        place[name] = (at, dims or a.shape[1:])
        at += full.shape[1]

    def rowwise(v):
        return np.broadcast_to(np.asarray(v, np.float32).reshape(1, -1), (P, np.size(v)))

    i = np.arange(P)
    put("ident", np.eye(P))
    put("ones", np.ones((P, P)))
    put("before", (i[:, None] < i[None, :]))
    half = ROPE // 2
    inv = (np.float32(10000.0) ** (np.float32(-2.0) * np.arange(half, dtype=np.float32) / np.float32(ROPE)))
    pos = np.concatenate([np.arange(SEQ), np.full(DB, PAST)]).astype(np.float32)
    ang = pos[:, None] * inv[None, :].astype(np.float32)
    cos, sin = np.cos(ang).astype(np.float32), np.sin(ang).astype(np.float32)
    rot = np.concatenate([cos.T, cos.T, -sin.T, sin.T])
    one = np.ones((NOPE, TOK))
    put("rope_q", -SCALE * np.stack([np.concatenate([one, rot]), np.concatenate([rot, one])], 1))
    def natural(t):
        out = np.zeros((P, NT, half), np.float32)
        for j in range(NT):
            out[:rows_of(j), j] = t[P * j:P * j + rows_of(j)]
        return out
    put("cos_k", natural(cos))
    put("sin_k", natural(sin))
    put("causal", np.concatenate([np.zeros((P, SEQ - P)), np.where(i[None, :] > i[:, None], BIG, 0.0)], 1))
    put("own_sample", np.broadcast_to(np.where(np.eye(DB) > 0, 0.0, BIG)[None], (H, DB, DB)))
    band = np.zeros((P, 2, 4, BAND), np.float32)
    band_s = np.zeros((DB * CTX, 4, DB), np.float32)
    own_s = np.zeros((DB, 4, DB), np.float32)
    for g, w in enumerate(WINDOWS):
        for c in range(BAND):
            for r in range(max(0, c - w + 1), min(P, c + 1)):
                band[r, 0, g, c] = 1.0 / min(c + 1, w)
                band[r, 1, g, c] = 1.0 / w
            if c < P:
                band[c, :, g, c] -= 1.0
        for b in range(DB):
            band_s[b * CTX + CTX - w + 1:(b + 1) * CTX, g, b] = 1.0 / w
            own_s[b, g, b] = 1.0 / w - 1.0
    put("band", band)
    put("band_s", band_s)
    put("own_s", own_s)
    e = np.arange(E)
    put("slot0", rowwise(e * CAP))
    put("slot_over", rowwise((E - 1) * CAP - e * CAP))
    put("steps", rowwise(CAP * np.arange(1, KOV + 1)))
    put("before_e", rowwise(e[None, :] < e[:, None]), E, E)
    j = np.arange(EPG)
    put("earlier", rowwise(j[None, :] < j[:, None]), EPG, EPG)
    put("prefer", rowwise(GROUPS - np.arange(GROUPS)))
    put("real_row", (i < DB).astype(np.float32)[:, None])
    put("no_row", (i >= DB).astype(np.float32)[:, None])
    put("over_k", rowwise(np.arange(NOV)))
    put("even_k", rowwise(np.arange(0, NOV, 2)))
    put("expert", rowwise(e))
    put("ln_eps", np.full((P, 1), LN_EPS))
    put("rms_eps", np.full((P, 1), RMS_EPS))
    return np.concatenate(parts, 1).astype(np.float32), place


def build(nc, t, consts_shape, place):
    ctx = ExitStack()
    with ctx:
        def sem(name):
            return ctx.enter_context(nc.semaphore(name))

        def sb(name, shape, dt=F32):
            return ctx.enter_context(nc.sbuf_tensor(name, shape, dt))

        ring = [sb("ring0", [P, 12288]), sb("ring1", [P, 12288])]
        X = sb("X", [P, NT, D])
        gb = sb("gb", [P, 4, D])
        C = sb("C", list(consts_shape))
        wr = sb("wr", [P, KD, E])
        small = sb("small", [P, 272])
        ids = sb("ids", [P, 128], I32)
        arena = sb("arena", [P, 15152])
        PS = ctx.enter_context(nc.psum_tensor("PS", [P, 4096], F32))

        def view(buf, off, *dims):
            n = int(np.prod(dims))
            ap = buf[:, off:off + n]
            if len(dims) == 2:
                return ap.rearrange("p (a b) -> p a b", a=dims[0])
            if len(dims) == 3:
                return ap.rearrange("p (a b c) -> p a b c", a=dims[0], b=dims[1])
            return ap

        def const(name):
            off, dims = place[name]
            if len(dims) == 3:
                n = int(np.prod(dims))
                return C[:, off:off + n].rearrange("p (a b c) -> p a b c", a=dims[0], b=dims[1])
            return view(C, off, *dims)

        def bank(b, *dims, off=0):
            return view(PS, 512 * b + off, *(dims or (512,)))

        ident, ones, before = const("ident"), const("ones"), const("before")
        rope_q, cos_k, sin_k = const("rope_q"), const("cos_k"), const("sin_k")
        causal, own_sample = const("causal"), const("own_sample")
        band, band_s, own_s = const("band"), const("band_s"), const("own_s")
        slot0, slot_over, steps = const("slot0"), const("slot_over"), const("steps")
        before_e, earlier, prefer = const("before_e"), const("earlier"), const("prefer")
        no_row = const("no_row")
        real_row, over_k, even_k, expert = (const(n) for n in ("real_row", "over_k", "even_k", "expert"))
        ln_eps, rms_eps = const("ln_eps"), const("rms_eps")

        wg = [view(r, 0, KD, F) for r in ring]
        wu = [view(r, 4096, KD, F) for r in ring]
        wd = [view(r, 8192, KF, D) for r in ring]
        R0, R1 = ring
        wo = view(R0, 0, KD, D)
        V = view(R0, 8192, 4, D)
        kraw = view(R0, 8192, NT, ROPE)
        krot = view(R0, 8192 + 160, NT, ROPE)
        gkv = view(R0, 8192 + 320, KVL)
        rtmp = view(R0, 8192 + 576, 4, 80)
        rq = view(R0, 8192 + 900, TOK)
        sqj = view(R0, 8192 + 1420, KVL)
        kdup = view(R0, 8192 + 1680, NT, 4, ROPE)
        wdq = view(R1, 0, KD, QL)
        wdkv = view(R1, 3072, KD, KVL + ROPE)
        sq = view(R1, 5376, MQ, TOK)
        prob = view(R1, 0, 4, 512)
        probT = view(R1, 2048, 2, 512)
        wqn = view(R1, 6936, MQ, 2 * HQ)
        wuq = view(R1, 7512, MQ, 256)
        wuk = view(R1, 8280, MKV, P)
        qT = [view(R1, 8536, TOK), view(R1, 9056, TOK)]
        kT = [view(R1, 9576, SEQ), view(R1, 10088, SEQ)]
        osb = view(R1, 10600, 4, P)
        ckp = [view(R1, at, NPAGES, KVL) for at in (3072, 0, 6144)]
        krp = [view(R1, at, NPAGES, 4, ROPE) for at in (5120, 2048, 8192)]
        kpT = view(R1, 9216, 3, PAST)
        zero_src = view(R1, 11264, D)
        oT = view(arena, 0, PAIRS, TOK)
        ckv = view(arena, 4160, NT, KVL)
        ckT = view(arena, 5440, 3, TOK)
        XT = view(arena, 7168, KD, TOK)
        xr = [[view(R0, 8192 + 1024 * s, KD, P) for s in range(2)], [view(arena, 7168 + 1024 * s, KD, P) for s in range(2)]]
        wukT = view(arena, 7168, PAIRS, KVL)
        qlat = view(arena, 9216, MKV, DB, H)
        olat = view(arena, 9472, MKV, DB, H)
        ps_s = view(arena, 9728, PAST + DB)
        psT_s = view(arena, 10760, NPAGES + 1, H)
        wuv = view(arena, 11328, MKV, D)
        cq = view(arena, 13376, MQ, TOK)
        qs = view(arena, 7000, PAIRS, 16)
        qr = view(arena, 14936, DB, H)
        xe = [view(arena, 768 * s, CAP // 32, D // 4) for s in range(2)]
        xeT = [view(arena, 2048 + 768 * s, KD, CAP) for s in range(2)]
        sg = [view(arena, 3584 + 384 * s, KF, CAP) for s in range(2)]
        h = [view(arena, 4352 + 384 * s, KF, CAP) for s in range(2)]
        ys = [view(arena, 5120 + 1024 * s, D) for s in range(2)]
        ya = [view(arena, at, D) for at in (7168, 8192, 5120)]
        yb = [view(arena, at, D) for at in (9216, 10240, 6144)]
        state = view(arena, 0, D)
        pscale = view(arena, 1024, D)
        poolT = view(arena, 2048, KD, TOK)
        wpool = view(arena, 13104, KD, 256)
        RT = 11328

        def rt(n, *dims):
            nonlocal RT
            v = view(arena, RT, *(dims or (n,)))
            RT += n
            return v

        r_exp, r_s, r_bias, r_rank, r_sel, r_comb, r_slot = (rt(80) for _ in range(7))
        r_big = rt(640)
        r_gs, r_gp, r_gsel = (rt(20) for _ in range(3))
        r_m, r_den, r_a, r_b, r_all = (rt(5) for _ in range(5))
        r_nt, r_ex, r_ovb, r_end, r_diff = (rt(E) for _ in range(5))
        r_tab = rt(32)
        r_nh = rt(8)
        r_k = rt(160)
        r_nov = rt(1)
        r_m6 = rt(120)
        assert RT <= 13104
        bias_row = view(small, 0, E)
        gq = view(small, 16, MQ)
        ss = view(small, 20, NT)
        kstd = view(small, 25, NT)
        krs = view(small, 30, NT)
        mneg = view(small, 36, 8)
        rsum = view(small, 44, 8)
        rinv = view(small, 52, 8)
        s_mneg, s_sum, s_inv = view(small, 60, 1), view(small, 61, 1), view(small, 62, 1)
        bn = view(small, 66, NT, 12)
        mv = view(small, 126, NT, 2)
        std, rstd, nmr = view(small, 136, NT), view(small, 141, NT), view(small, 146, NT)
        ca, cb = view(small, 152, NT), view(small, 158, NT)
        qb = [view(arena, 10904 + 48 * s, 3, H) for s in range(3)]
        onat = view(arena, 13376, KVL)
        page_ids = ids[:, 0:64]
        idx_a, idx_b = ids[:, 64:69], ids[:, 72:77]
        tile_ids, n_half = ids[:, 80:112], ids[:, 120:121]

        ZSTEP = -(-(TILES + 2) // (PAIRS - 2))
        xs = nc.dram_tensor("expert_rows", (ZSTEP * (PAIRS - 2) * CAP, D), F32).ap()
        yd = nc.dram_tensor("expert_out", (TILES * CAP, D), F32).ap()

        c_ld, wdq_ld, wdkv_ld, gain_ld, wuv_ld, router_ld, wo_ld = (
            sem(n) for n in ("c_ld", "wdq_ld", "wdkv_ld", "gain_ld", "wuv_ld", "router_ld", "wo_ld"))
        x_ld = [sem(f"x_ld{i}") for i in range(NT)]
        pt_ld, wqn_ld, wuk_ld, zero_set, zero_st = (
            sem(n) for n in ("pt_ld", "wqn_ld", "wuk_ld", "zero_set", "zero_st"))
        page_ld = [sem(f"page_ld{s}") for s in range(3)]
        kr_ld, kr_dup = sem("kr_ld"), sem("kr_dup")
        gb_ld = [[sem(f"gb{w + 1}_ld_{L}") for w in range(2)] for L in range(2)]
        wp_ld, st_ld, wp_ready = sem("wp_ld"), sem("st_ld"), sem("wp_ready")
        out_st = sem("out_st")
        latent_st = sem("latent_st")
        passed = sem("passed")
        pool_out = sem("pool_out")
        xt_ps = sem("xt_ps")
        xt_ev = [sem("xt_ev_dve"), sem("xt_ev_act")]
        cq_ps, cq_copied, cq_squared, cq_sum, rq_std, cq_done = (
            sem(n) for n in ("cq_ps", "cq_copied", "cq_squared", "cq_sum", "rq_std", "cq_done"))
        kraw_zero, kv_ps, kv_ss, kv_std, kv_ready, kr_ready, ck_ps, ck_ev = (
            sem(n) for n in ("kraw_zero", "kv_ps", "kv_ss", "kv_std", "kv_ready", "kr_ready",
                             "ck_ps", "ck_ev"))
        dve_step = sem("dve_step")
        wq_even, wq_odd, q_ps, q_ev, for_act, act_ev = (
            sem(n) for n in ("wq_even", "wq_odd", "q_ps", "q_ev", "for_act", "act_ev"))
        s_ps, min_set, exp_set, t_ps, o_ps, rinv_set, o_ev = (
            sem(n) for n in ("s_ps", "min_set", "exp_set", "t_ps", "o_ps", "rinv_set", "o_ev"))
        pt_ev = [sem("pt_ev_dve"), sem("pt_ev_act")]
        qpad_zero = sem("qpad_zero")
        ql_ps, qb_set, tp_ps, sc_ps, new_masked, smin_set, sexp_set, sinv_set = (
            sem(n) for n in ("ql_ps", "qb_set", "tp_ps", "sc_ps", "new_masked", "smin_set",
                             "sexp_set", "sinv_set"))
        tp_ev = [sem("tp_ev_dve"), sem("tp_ev_act")]
        spT_ps, spT_ev, pv_ps, onat_set, ol_ps, ol_ev, uv_ps, uv_ev = (
            sem(n) for n in ("spT_ps", "spT_ev", "pv_ps", "onat_set", "ol_ps", "ol_ev", "uv_ps", "uv_ev"))
        mix_ps = sem("mix_ps")
        ln_z, ln_agg, ln_std, ln_rstd, ln_nrm, ln_gam, ln_out = (
            [sem(f"{n}_{L}") for L in range(2)]
            for n in ("ln_z", "ln_agg", "ln_std", "ln_rstd", "ln_nrm", "ln_gam", "ln_out"))
        turn_ps, turn_ev = sem("turn_ps"), sem("turn_ev")
        lg_zero, lg_ps, lg_exp, sel_set, cnt_ps, idx_set, tab_set, scat, xscaled = (
            sem(n) for n in ("lg_zero", "lg_ps", "lg_exp", "sel_set", "cnt_ps", "idx_set", "tab_set",
                             "scat", "xscaled"))
        gath = [sem(f"gath{s}") for s in range(3)]
        def expert_sems(L):
            two = ("wg_ld", "wu_ld", "wd_ld", "xe_ld", "y_st", "gate_ps", "up_ps", "down_ps")
            one = ("xeT_set", "sg_set", "h_set", "y_set")
            return {n: [sem(f"{n}{s}_{L}") for s in range(2)] for n in two} | {n: sem(f"{n}_{L}") for n in one}

        S = [expert_sems(0), expert_sems(1)]
        block = ctx.enter_context(nc.Block())

        def bcast(row, n=P):
            return row.unsqueeze(0).to_broadcast([n] + list(row.shape))

        turn_bank = [4, 5, 7]
        page_bank = [4, 5, 3]

        def score(i):
            return bank((2, 2, 1, 0)[i], P * (i + 1), off=256 if i == 0 else 0)

        def scored(i):
            return 4 - i if i > 1 else 4

        def hold(eng, s, value):
            eng.wait_ge(s, value)
            if not isinstance(value, int):
                eng.sem_inc(passed, 1)

        @block.sync
        def _(sp):
            sp.dma_start(C[:, 0:P], t["consts"][:, 0:P]).then_inc(x_ld[0], 16)
            for i in range(4):
                sp.dma_start(X[:, i, :], t["x_prompt"][0, P * i:P * (i + 1), :]).then_inc(x_ld[i], 16)
            sp.dma_start(X[0:DB, 4, :], t["x_sample"][:, 0, :]).then_inc(x_ld[4], 16)
            sp.dma_start(wdq, t["w_dq"][0].rearrange("(k p) n -> p k n", p=P)).then_inc(wdq_ld, 16)
            sp.dma_start(C[:, P:], t["consts"][:, P:]).then_inc(c_ld, 16)
            with nc.allow_non_contiguous_dma(reason="384 words"):
                sp.dma_start(gq, t["g_q"][0].rearrange("(m p) -> p m", p=P)).then_inc(gain_ld, 16)
            sp.dma_start(wdkv, t["w_dkv"][0].rearrange("(k p) n -> p k n", p=P)).then_inc(wdkv_ld, 16)
            sp.dma_start(gkv, bcast(t["g_kv"][0])).then_inc(gain_ld, 16)
            sp.dma_start(page_ids[0:1, :], t["page_table"].rearrange("b n -> (b n)").unsqueeze(0)).then_inc(pt_ld, 16)

            def load_pair(j):
                sp.dma_start(wqn, t["w_uq"][0].rearrange("(m p) n -> p m n", p=P)[:, :, bass.ds(2 * HQ * j, 2 * HQ)]
                             ).then_inc(wqn_ld, 16)
                sp.dma_start(wuk, t["w_uk"][0].rearrange("(m p) h d -> p m (h d)", p=P)[:, :, bass.ds(P * j, P)]
                             ).then_inc(wuk_ld, 16)

            load_pair(0)
            sp.dma_start(wuv, t["w_uv"][0].rearrange("(m p) h d -> p m (h d)", p=P)).then_inc(wuv_ld, 16)
            sp.dma_start(wr[:, :, :], t["w_router"].rearrange("(k p) n -> p k n", p=P)).then_inc(router_ld, 16)
            sp.dma_start(bias_row, bcast(t["router_bias"])).then_inc(router_ld, 16)
            sp.dma_start(gb[:, 0, :], bcast(t["ln1_g"][0])).then_inc(gb_ld[0][0], 16)
            sp.dma_start(gb[:, 1, :], bcast(t["ln1_b"][0])).then_inc(gb_ld[0][0], 16)
            sp.dma_start(gb[:, 2, :], bcast(t["ln2_g"][0])).then_inc(gb_ld[0][1], 16)
            sp.dma_start(gb[:, 3, :], bcast(t["ln2_b"][0])).then_inc(gb_ld[0][1], 16)
            sp.dma_start(wo, t["w_o"][0].rearrange("(k p) n -> p k n", p=P)).then_inc(wo_ld, 16)
            sp.wait_ge(kv_ready, NT)
            sp.wait_ge(kr_ready, 1)
            for i in range(4):
                sp.dma_start(t["o_ckv_p"][0, 0, P * i:P * (i + 1), :], ckv[:, i, :]).then_inc(latent_st, 16)
                sp.dma_start(t["o_kr_p"][0, 0, P * i:P * (i + 1), :], krot[:, i, :]).then_inc(latent_st, 16)
            sp.dma_start(t["o_ckv_s"][0, :, 0, :], ckv[0:DB, 4, :]).then_inc(latent_st, 16)
            sp.dma_start(t["o_kr_s"][0, :, 0, :], krot[0:DB, 4, :]).then_inc(latent_st, 16)
            sp.dma_start(t["o_pool_s"][0, :, 0:CTX - 1, :], t["state_pool"][0, :, 1:CTX, :]).then_inc(out_st, 16)
            sp.wait_ge(wq_odd, 1)
            sp.wait_ge(for_act, 3)
            load_pair(1)

            def load_pages(b, s):
                for n in range(NPAGES):
                    page = sp.value_load(page_ids[0:1, bass.ds(b * NPAGES + n, 1)], min_val=0, max_val=NPHYS - 1)
                    sp.dma_start(ckp[s][:, n, :], t["cache_ckv"][0, bass.ds(page, 1), :, :].rearrange("a p d -> (a p) d")
                                 ).then_inc(page_ld[s], 16)

            sp.wait_ge(pt_ld, 16)
            sp.wait_ge(cq_sum, 2)
            load_pages(0, 0)
            sp.wait_ge(zero_set, 1)
            zeros = zero_src[0:CAP, :].unsqueeze(1)
            with sp.Fori(2, PAIRS) as j:
                sp.wait_ge(wq_odd, j)
                sp.wait_ge(for_act, 4 * j - 2)
                load_pair(j)
                sp.dma_start(xs[bass.ds(ZSTEP * CAP * (j - 2), ZSTEP * CAP), :].rearrange("(a p) d -> p a d", p=CAP),
                             zeros.to_broadcast([CAP, ZSTEP, D])).then_inc(zero_st, 16)
            sp.dma_start(yd[E * CAP:, :].rearrange("(a p) d -> p a d", p=CAP), zeros.to_broadcast([CAP, NOV, D])
                         ).then_inc(zero_st, 16)
            with sp.Fori(0, (DB - 2) // 3) as u:
                for d in (1, 2, 3):
                    sp.wait_ge(pv_ps, 3 * u + d)
                    load_pages(3 * u + d, d % 3)
            sp.wait_ge(pv_ps, DB - 1)
            load_pages(DB - 1, 1)

            def load_expert(L, e, s, gate_free=None, up_free=None, down_free=None):
                q = S[L]
                if gate_free:
                    sp.wait_ge(*gate_free)
                sp.dma_start(wg[s], t["w_gate"][L, bass.ds(e, 1), :, :].rearrange("a (p k) f -> p (a k) f", p=P)
                             ).then_inc(q["wg_ld"][s], 16)
                if up_free:
                    sp.wait_ge(*up_free)
                sp.dma_start(wu[s], t["w_up"][L, bass.ds(e, 1), :, :].rearrange("a (p k) f -> p (a k) f", p=P)
                             ).then_inc(q["wu_ld"][s], 16)
                if down_free:
                    sp.wait_ge(*down_free)
                sp.dma_start(wd[s], t["w_down"][L, bass.ds(e, 1), :, :].rearrange("a (k p) d -> p (a k) d", p=P)
                             ).then_inc(q["wd_ld"][s], 16)

            for L in range(2):
                q = S[L]
                if L == 0:
                    load_expert(0, 0, 1, gate_free=(pv_ps, DB + 2))
                    load_expert(0, 1, 0, gate_free=(mix_ps, NT), down_free=(lg_ps, 1))
                else:
                    load_expert(1, 0, 1, (S[0]["gate_ps"][0], nh), (S[0]["up_ps"][0], 2 * nh), (S[0]["down_ps"][0], nh))
                    sp.wait_ge(S[0]["xeT_set"], 2 * nh + 1)
                    sp.wait_ge(S[0]["xe_ld"][1], 64 * (nh + 1))
                    sp.dma_start(pscale, bcast(t["pool_scale"][0])).then_inc(st_ld, 16)
                    sp.dma_start(state[0:DB * CTX, :], t["state_pool"][0].rearrange("b c d -> (b c) d")).then_inc(st_ld, 16)
                    sp.wait_ge(ln_out[0], 2 * NT)
                    sp.dma_start(t["o_pool_p"][0, 0, :, :], X[P - CTX:P, 3, :]).then_inc(pool_out, 16)
                    sp.dma_start(t["o_pool_s"][0, :, CTX - 1, :], X[0:DB, 4, :]).then_inc(pool_out, 16)
                    load_expert(1, 1, 0, (S[0]["gate_ps"][1], nh), (S[0]["up_ps"][1], 2 * nh), (S[0]["down_ps"][1], nh))
                sp.wait_ge(tab_set, 2 * L + 2)
                nh = sp.value_load(n_half[0:1, 0:1], min_val=E // 2, max_val=TILES // 2)
                with sp.Fori(1, nh) as u:
                    for s in range(2):
                        ex = sp.value_load(tile_ids[0:1, bass.ds(2 * u + s, 1)], min_val=0, max_val=E - 1)
                        load_expert(L, ex, 1 - s, (q["gate_ps"][s], u), (q["up_ps"][s], 2 * u), (q["down_ps"][s], u))
            for i in range(4):
                sp.wait_ge(ln_out[1], NT + i + 1)
                sp.dma_start(t["o_y_p"][0, P * i:P * (i + 1), :], X[:, i, :]).then_inc(out_st, 16)
            sp.wait_ge(ln_out[1], 2 * NT)
            sp.dma_start(t["o_y_s"][:, 0, :], X[0:DB, 4, :]).then_inc(out_st, 16)
            sp.wait_ge(out_st, 16 * (1 + 5))
            sp.wait_ge(pool_out, 32)

        @block.tensor
        def _(pe):
            turns = [0]

            def turn():
                n = turns[0]
                turns[0] += 1
                if n >= 3:
                    pe.wait_ge(turn_ev, n - 2)
                return turn_bank[n % 3]

            def transpose_x(i, g, b):
                n = rows_of(i)
                for kk in range(4):
                    last = nc.tensor.transpose(bank(b, 4, P)[:, kk, 0:n], X[0:n, i, P * (4 * g + kk):P * (4 * g + kk + 1)],
                                               ident[0:n, 0:n])
                return last

            for i in range(NT):
                pe.wait_ge(x_ld[i], 16 if i else 32)
                for g in range(2):
                    n = 2 * i + g
                    if n >= 4:
                        pe.wait_ge(xt_ev[g], (n - 4) // 2 + 1)
                    transpose_x(i, g, n % 4).then_inc(xt_ps, 1)
            pe.wait_ge(wdq_ld, 16)
            for g in range(2):
                pe.wait_ge(xt_ev[g], NT)
            for m in range(MQ):
                for hf in range(2):
                    n = 2 * m + hf
                    if n >= 4:
                        pe.wait_ge(cq_copied, n - 3)
                    for k in range(KD):
                        last = nc.tensor.matmul(bank(n % 4, HALF), wdq[:, k, P * m:P * (m + 1)],
                                                XT[:, k, HALF * hf:HALF * (hf + 1)], start=(k == 0), stop=(k == KD - 1))
                    last.then_inc(cq_ps, 1)

            def sum_squares():
                pe.wait_ge(c_ld, 16)
                pe.wait_ge(cq_squared, 2 * MQ)
                pe.wait_ge(cq_copied, 2 * MQ)
                for hf in range(2):
                    for m in range(MQ):
                        last = nc.tensor.matmul(bank(hf, HALF), ones, sq[:, m, HALF * hf:HALF * (hf + 1)],
                                                start=(m == 0), stop=(m == MQ - 1))
                    last.then_inc(cq_sum, 1)

            pe.wait_ge(wdkv_ld, 16)
            for i in range(NT):
                n = rows_of(i)
                if i >= 2:
                    pe.wait_ge(kv_ready, i - 1)
                for k in range(KD):
                    last = nc.tensor.matmul(bank(4 + i % 2, KVL + ROPE)[0:n, :], XT[:, k, P * i:P * i + n], wdkv[:, k, :],
                                            start=(k == 0), stop=(k == KD - 1))
                last.then_inc(kv_ps, 1)
                if i == 0:
                    sum_squares()
            for i in range(NT):
                n = rows_of(i)
                if i == 0:
                    pe.wait_ge(kv_ready, NT)
                    pe.wait_ge(kr_ready, 2)
                if i >= 2:
                    pe.wait_ge(ck_ev, i - 1)
                out = bank(6 + i % 2, 3, P)
                for c in range(MKV):
                    nc.tensor.transpose(out[:, c, 0:n], ckv[0:n, i, P * c:P * (c + 1)], ident[0:n, 0:n])
                nc.tensor.transpose(out[:, 2, 0:n], kdup[0:n, i, :, :].rearrange("p a b -> p (a b)"), ident[0:n, 0:n]
                                    ).then_inc(ck_ps, 1)

            def project_q(parity, hf, b):
                for m in range(MQ):
                    last = nc.tensor.matmul(bank(b, HALF), wuq[:, m, P * parity:P * (parity + 1)],
                                            cq[:, m, HALF * hf:HALF * (hf + 1)], start=(m == 0), stop=(m == MQ - 1))
                last.then_inc(q_ps, 1)

            def q_even(j, first):
                pe.wait_ge(wq_even, j + 1)
                if not first:
                    pe.wait_ge(act_ev, 3 if isinstance(j, int) and j == 1 else 4 * j - 2)
                project_q(0, 0, 4)
                if not first:
                    pe.wait_ge(act_ev, 4 * j - 1)
                project_q(0, 1, 7)

            def v_both(j):
                pe.wait_ge(q_ev, 4 * j + 1)
                for i in range(4):
                    for c in range(MKV):
                        last = nc.tensor.matmul(bank(4, 4, P)[:, i, :], ckT[:, c, P * i:P * (i + 1)],
                                                wuv[:, c, bass.ds(P * j, P)], start=(c == 0), stop=(c == MKV - 1))
                last.then_inc(for_act, 1)

            def q_odd(j, first):
                pe.wait_ge(wq_odd, j + 1)
                pe.wait_ge(q_ev, 4 * j + 2)
                project_q(1, 0, 7)
                pe.wait_ge(act_ev, 1 if first else 4 * j)
                project_q(1, 1, 4)

            def k_both(j):
                pe.wait_ge(q_ev, 4 * j + 3)
                pe.wait_ge(wuk_ld, 16 * (j + 1))
                for c in range(MKV):
                    last = nc.tensor.matmul(bank(7), wuk[:, c, :], ckT[:, c, 0:SEQ], start=(c == 0), stop=(c == MKV - 1))
                last.then_inc(for_act, 1)
                pe.wait_ge(q_ev, 4 * j + 4)
                for c in range(MKV):
                    last = nc.tensor.transpose(bank(4, MKV, P)[:, c, :], wuk[:, c, :], ident)
                last.then_inc(for_act, 1)

            def scores(par):
                for i in (3, 2, 1, 0):
                    nc.tensor.matmul(score(i), qT[par][:, P * i:P * (i + 1)], kT[par][:, 0:P * (i + 1)],
                                     start=True, stop=True).then_inc(s_ps, 1)

            def attend(p, par, meanwhile):
                def turned(i):
                    hold(pe, exp_set, 8 * p + 4 * par + 4 - i)
                    for k in range(i + 1):
                        last = nc.tensor.transpose(bank(5 + i % 2, 4, P)[:, k, :], prob[:, i, P * k:P * (k + 1)], ident)
                    last.then_inc(t_ps, 1)

                def weighed(i):
                    hold(pe, pt_ev[i % 2], 4 * p + 2 * par + (3 - i) // 2 + 1)
                    for k in range(i + 1):
                        last = nc.tensor.matmul(bank(3, 4, VH, off=256 * par)[:, i, :], probT[:, i % 2, P * k:P * (k + 1)],
                                                V[:, k, bass.ds(P * p + VH * par, VH)], start=(k == 0), stop=(k == i))
                    return last

                turned(3)
                turned(2)
                if meanwhile:
                    meanwhile(p + 1)
                if par:
                    pe.wait_ge(o_ev, 2 * p + 1)
                weighed(3)
                turned(1)
                weighed(2)
                turned(0)
                weighed(1)
                weighed(0).then_inc(o_ps, 1)

            def turn_heads(p):
                pe.wait_ge(o_ev, 2 * p + 2)
                for i in range(4):
                    last = nc.tensor.transpose(bank(7, 4, P)[:, i, :], osb[:, i, :], ident)
                last.then_inc(for_act, 1)

            def pair(p, after_one, more):
                pe.wait_ge(q_ev, 4 * p + 4)
                pe.wait_ge(act_ev, 4 * p + 2)
                scores(0)
                if after_one:
                    turn_heads(p - 1)
                if more:
                    q_even(p + 1, False)
                attend(p, 0, v_both if more else None)
                scores(1)
                if more:
                    q_odd(p + 1, False)
                attend(p, 1, k_both if more else None)

            pe.wait_ge(cq_done, 1)
            pe.wait_ge(ck_ev, NT)
            pe.wait_ge(wuv_ld, 16)
            q_even(0, True)
            v_both(0)
            q_odd(0, True)
            k_both(0)
            pe.wait_ge(q_ev, 4)
            pe.wait_ge(kr_ready, 3)
            pair(0, False, True)
            with pe.Fori(1, PAIRS - 1) as p:
                pair(p, True, True)
            pair(PAIRS - 1, True, False)
            turn_heads(PAIRS - 1)

            def latent_q():
                pe.wait_ge(ln_z[0], 4)
                for j in range(PAIRS):
                    for c in range(MKV):
                        last = nc.tensor.matmul(bank(3, MKV, PAIRS, 16)[:, c, j, :], wukT[:, j, P * c:P * (c + 1)], qs[:, j, :],
                                                start=True, stop=True)
                last.then_inc(ql_ps, 1)

            def turn_pages(b, s, use):
                pe.wait_ge(page_ld[s], 16 * NPAGES * use)
                n = 0
                for c in range(3):
                    if c == MKV:
                        pe.wait_ge(kr_dup, b + 1)
                    for hf in range(2):
                        if n >= 3:
                            pe.wait_ge(tp_ev[(n - 3) % 2], 3 * b + (n - 3) // 2 + 1)
                        elif n == 2 and isinstance(b, int) and b == 0:
                            pe.wait_ge(qb_set, 1)
                        for a in range(4):
                            pg = 4 * hf + a
                            src = (ckp[s][:, pg, P * c:P * (c + 1)] if c < MKV
                                   else krp[s][:, pg, :, :].rearrange("p a b -> p (a b)"))
                            last = nc.tensor.transpose(bank(page_bank[n % 3], 4, P)[:, a, :], src, ident)
                        last.then_inc(tp_ps, 1)
                        n += 1

            def turn_latent_out(b):
                hold(pe, onat_set, b + 1)
                for c in range(MKV):
                    last = nc.tensor.transpose(bank(7, MKV, H, off=256)[:, c, :], onat[0:H, P * c:P * (c + 1)], ident[0:H, 0:H])
                last.then_inc(ol_ps, 1)

            def sample(b, s, before, after_one, following):
                pe.wait_ge(tp_ev[0], 3 * b + 3)
                pe.wait_ge(tp_ev[1], 3 * b + 3)
                pe.wait_ge(qb_set, b + 1)
                for hf in range(2):
                    for c in range(3):
                        nc.tensor.matmul(bank(hf)[0:H, :], qb[s][:, c, :], kpT[:, c, 512 * hf:512 * (hf + 1)],
                                         start=(c == 0), stop=(c == 2))
                for c in range(3):
                    last = nc.tensor.matmul(bank(2, DB)[0:H, :], qb[s][:, c, :], ckT[:, c, SEQ:TOK], start=(c == 0), stop=(c == 2))
                last.then_inc(sc_ps, 1)
                if after_one:
                    weigh_pages(b - 1, before)
                if following:
                    turn_pages(*following)
                if after_one:
                    turn_latent_out(b - 1)
                hold(pe, sexp_set, b + 1)
                turned = bank(6, NPAGES + 1, H, off=256)
                for n in range(NPAGES):
                    nc.tensor.transpose(turned[:, n, :], ps_s[0:H, P * n:P * (n + 1)], ident[0:H, 0:H])
                nc.tensor.transpose(turned[0:DB, NPAGES, :], ps_s[0:H, PAST:PAST + DB], ident[0:H, 0:H]).then_inc(spT_ps, 1)
                if after_one:
                    pe.wait_ge(ol_ev, b)

            def weigh_pages(b, s):
                pe.wait_ge(spT_ev, b + 1)
                for n in range(NPAGES):
                    nc.tensor.matmul(bank(7, KVL)[0:H, :], psT_s[:, n, :], ckp[s][:, n, :], start=(n == 0), stop=False)
                nc.tensor.matmul(bank(7, KVL)[0:H, :], psT_s[0:DB, NPAGES, :], ckv[0:DB, 4, :], start=False, stop=True
                                 ).then_inc(pv_ps, 1)

            def samples():
                sample(0, 0, None, False, (1, 1, 1))
                with pe.Fori(0, (DB - 2) // 3) as u:
                    for d in (1, 2, 3):
                        sample(3 * u + d, d % 3, (d - 1) % 3, True, (3 * u + d + 1, (d + 1) % 3, u + 1 + (d + 1) // 3))
                sample(DB - 1, 1, 0, True, None)
                weigh_pages(DB - 1, 1)
                turn_latent_out(DB - 1)
                pe.wait_ge(ol_ev, DB)
                for j in range(PAIRS):
                    for c in range(MKV):
                        last = nc.tensor.matmul(bank(3, PAIRS, DB, 2, off=256)[:, j, :, :], wuv[:, c, P * j:P * (j + 1)],
                                                olat[:, c, :, 2 * j:2 * j + 2], start=(c == 0), stop=(c == MKV - 1))
                last.then_inc(uv_ps, 1)

            def mix(L, i):
                n, b0 = rows_of(i), 2 * (i % 2)
                if i >= 2:
                    pe.wait_ge(ln_z[L], i - 1)
                if L == 0:
                    for hf in range(2):
                        for k in range(KD):
                            last = nc.tensor.matmul(bank(b0 + hf)[0:n, :], oT[:, k, P * i:P * i + n],
                                                    wo[:, k, 512 * hf:512 * (hf + 1)], start=(k == 0), stop=(k == KD - 1))
                else:
                    for g in range(4):
                        for kk in range(2):
                            last = nc.tensor.matmul(view(PS, 512 * b0 + 256 * g, 256)[0:n, :],
                                                    poolT[:, 2 * g + kk, P * i:P * i + n], wpool[:, 2 * g + kk, :],
                                                    start=(kk == 0), stop=(kk == 1))
                last.then_inc(mix_ps, 1)

            def pool(i):
                pe.wait_ge(ln_out[0], NT + i + 1)
                if i < 4:
                    for g in range(2):
                        b = turn()
                        for c in range(4):
                            k = 4 * g + c
                            out = bank(b, 4, P)[:, c, :]
                            last = nc.tensor.matmul(out, X[:, i, P * k:P * (k + 1)], band[:, min(i, 1), k // 2, 0:P],
                                                    start=True, stop=(i == 0))
                            if i:
                                last = nc.tensor.matmul(out[:, 0:CTX], X[:, i - 1, P * k:P * (k + 1)], band[:, 1, k // 2, P:BAND],
                                                        start=False, stop=True)
                        last.then_inc(turn_ps, 1)
                else:
                    b = turn()
                    pe.wait_ge(st_ld, 32)
                    for k in range(KD):
                        out = bank(b, KD, DB)[:, k, :]
                        nc.tensor.matmul(out, state[0:DB * CTX, P * k:P * (k + 1)], band_s[0:DB * CTX, k // 2, :],
                                         start=True, stop=False)
                        last = nc.tensor.matmul(out, X[0:DB, 4, P * k:P * (k + 1)], own_s[0:DB, k // 2, :],
                                                start=False, stop=True)
                    last.then_inc(turn_ps, 1)

            def router(L, i):
                n = rows_of(i)
                pe.wait_ge(ln_out[L], i + 1)
                for g in range(2):
                    transpose_x(i, g, turn()).then_inc(turn_ps, 1)
                pe.wait_ge(turn_ev, turns[0])
                if i == 0:
                    pe.wait_ge(lg_zero, L + 1)
                for k in range(KD):
                    last = nc.tensor.matmul(bank(6, NT, E)[0:n, i, :], xr[L][i % 2][:, k, 0:n], wr[:, k, :],
                                            start=(k == 0), stop=(k == KD - 1))
                if i == NT - 1:
                    last.then_inc(lg_ps, 1)

            def counts(L):
                pe.wait_ge(sel_set, L + 1)
                nc.tensor.matmul(bank(6, NT * E, off=128), before, r_sel, start=True, stop=True)
                last = nc.tensor.matmul(bank(6, NT * E, off=208), ones, r_sel, start=True, stop=True)
                last.then_inc(cnt_ps, 1)

            def experts(L):
                q = S[L]

                def tile(u, s):
                    tl = 2 * u + s
                    w = 1 - s
                    pe.wait_ge(q["xeT_set"], tl + 1)
                    pe.wait_ge(q["wg_ld"][w], 16 * (u + 1))
                    for f in range(KF):
                        for k in range(KD):
                            last = nc.tensor.matmul(bank(s, KF, CAP)[:, f, :], wg[w][:, k, P * f:P * (f + 1)], xeT[s][:, k, :],
                                                    start=(k == 0), stop=(k == KD - 1))
                    last.then_inc(q["gate_ps"][s], 1)
                    pe.wait_ge(q["wu_ld"][w], 16 * (u + 1))
                    for f in range(KF):
                        out = bank(2 + s, KF, CAP)[:, f, :] if f < KF - 1 else bank(6 + s, CAP)
                        for k in range(KD):
                            last = nc.tensor.matmul(out, wu[w][:, k, P * f:P * (f + 1)], xeT[s][:, k, :],
                                                    start=(k == 0), stop=(k == KD - 1))
                        if f >= KF - 2:
                            last.then_inc(q["up_ps"][s], 1)
                    pe.wait_ge(q["h_set"], 2 * tl + 1)
                    pe.wait_ge(q["wd_ld"][w], 16 * (u + 1))
                    pe.wait_ge(q["y_set"], 2 * tl + 2)
                    for blocks in (range(KF - 1), (KF - 1,)):
                        if KF - 1 in blocks:
                            pe.wait_ge(q["h_set"], 2 * tl + 2)
                        for hf in range(2):
                            for f in blocks:
                                last = nc.tensor.matmul(bank(4 + hf)[0:CAP, :], h[s][:, f, :], wd[w][:, f, 512 * hf:512 * (hf + 1)],
                                                        start=(f == 0), stop=(f == KF - 1))
                    last.then_inc(q["down_ps"][s], 1)

                pe.wait_ge(tab_set, 2 * L + 2)
                nh = pe.value_load(n_half[0:1, 0:1], min_val=E // 2, max_val=TILES // 2)
                with pe.Fori(0, nh) as u:
                    for s in range(2):
                        tile(u, s)

            pe.wait_ge(wo_ld, 16)
            pe.wait_ge(act_ev, 4 * PAIRS)
            pe.sem_inc(pv_ps, 2)
            pe.wait_ge(router_ld, 32)
            mix(0, 0)
            for i in range(1, 4):
                mix(0, i)
                router(0, i - 1)
            latent_q()
            turn_pages(0, 0, 1)
            pe.wait_ge(tp_ev[0], 3)
            pe.wait_ge(tp_ev[1], 3)
            router(0, 3)
            samples()
            pe.wait_ge(uv_ev, 1)
            mix(0, 4)
            router(0, 4)
            counts(0)
            experts(0)
            pool_turns = []

            def pool_then(i):
                pool(i)
                pool_turns.append(turns[0])

            def mix_pooled(i):
                pe.wait_ge(turn_ev, pool_turns[i])
                if i == 0:
                    pe.wait_ge(wp_ready, 1)
                mix(1, i)

            pool_then(0)
            for i in range(1, 5):
                pool_then(i)
                mix_pooled(i - 1)
            router(1, 0)
            mix_pooled(4)
            for i in range(1, NT):
                router(1, i)
            counts(1)
            experts(1)

        @block.gpsimd
        def _(pool_e):
            nc.gpsimd.memset(zero_src, 0.0).then_inc(zero_set, 1)

            def copy_even():
                nc.gpsimd.tensor_copy(wuq[:, :, 0:HQ], wqn[:, :, 0:HQ])
                nc.gpsimd.tensor_copy(wuq[:, :, 96:112], wqn[:, :, 80:96])
                nc.gpsimd.tensor_copy(wuq[:, :, 112:128], wqn[:, :, 64:80]).then_inc(wq_even, 1)

            def copy_odd():
                nc.gpsimd.tensor_copy(wuq[:, :, 128:160], wqn[:, :, 160:192])
                nc.gpsimd.tensor_copy(wuq[:, :, 160:176], wqn[:, :, 176:192])
                nc.gpsimd.tensor_copy(wuq[:, :, 176:192], wqn[:, :, 160:176])
                nc.gpsimd.tensor_copy(wuq[:, :, 192:256], wqn[:, :, 96:160]).then_inc(wq_odd, 1)

            hold(pool_e, wqn_ld, 16)
            copy_even()
            copy_odd()
            with pool_e.Fori(1, PAIRS) as j:
                hold(pool_e, wqn_ld, 16 * (j + 1))
                hold(pool_e, q_ps, 4 * j - 2)
                copy_even()
                hold(pool_e, q_ps, 4 * j)
                copy_odd()

            def load_keys(b, s):
                for n in range(NPAGES):
                    page = pool_e.value_load(page_ids[0:1, bass.ds(b * NPAGES + n, 1)], min_val=0, max_val=NPHYS - 1)
                    pool_e.dma_start(krp[s][:, n, 0, :], t["cache_krope"][0, bass.ds(page, 1), :, :].rearrange("a p d -> (a p) d")
                                     ).then_inc(kr_ld, 16)
                hold(pool_e, kr_ld, 16 * NPAGES * (b + 1))
                nc.gpsimd.tensor_copy(krp[s][:, :, 1:4, :], krp[s][:, :, 0:1, :].to_broadcast([P, NPAGES, 3, ROPE])
                                      ).then_inc(kr_dup, 1)

            def shift(L, i):
                n = rows_of(i)
                if i == 0:
                    hold(pool_e, gb_ld[L][1], 32)
                hold(pool_e, ln_gam[L], i + 1)
                nc.gpsimd.tensor_tensor(X[0:n, i, :], X[0:n, i, :], gb[0:n, 3, :], ALU.add).then_inc(ln_out[L], 1)

            hold(pool_e, pt_ld, 16)
            load_keys(0, 0)
            with pool_e.Fori(0, (DB - 2) // 3) as u:
                for d in (1, 2, 3):
                    hold(pool_e, pv_ps, 3 * u + d)
                    load_keys(3 * u + d, d % 3)
            hold(pool_e, pv_ps, DB - 1)
            load_keys(DB - 1, 1)
            hold(pool_e, uv_ps, 1)
            pool_e.dma_start(wpool, t["w_pool"][0].rearrange("g (k p) d -> p (g k) d", p=P)).then_inc(wp_ld, 16)

            for L in range(2):
                q = S[L]
                hold(pool_e, idx_set, 2 * (L + 1))
                hold(pool_e, zero_st, 16 * (PAIRS - 1))
                hold(pool_e, ln_out[L], NT)
                for i in range(NT):
                    for idx in (idx_a, idx_b):
                        pool_e.indirect_dma_start(
                            xs[:, :], bass.IndirectOffsetOnAxis(ap=idx[0:rows_of(i), i:i + 1], axis=0),
                            X[0:rows_of(i), i, :], None).then_inc(scat, 16)
                hold(pool_e, scat, 160 * (L + 1))
                if L == 0:
                    hold(pool_e, q["xeT_set"], 1)
                    pool_e.dma_start(gb[:, 0, :], bcast(t["ln1_g"][1])).then_inc(gb_ld[1][0], 16)
                    pool_e.dma_start(gb[:, 1, :], bcast(t["ln1_b"][1])).then_inc(gb_ld[1][0], 16)
                hold(pool_e, tab_set, 2 * L + 2)
                nh = pool_e.value_load(n_half[0:1, 0:1], min_val=E // 2, max_val=TILES // 2)
                for s in range(2):
                    hold(pool_e, q["y_st"][s], 16 * nh)

                def gather(i):
                    n, s = rows_of(i), i % 3
                    if i >= 3:
                        hold(pool_e, ln_z[L], NT + i - 2)
                    for idx, y in ((idx_a, ya), (idx_b, yb)):
                        pool_e.indirect_dma_start(y[s][0:n, :], None, yd[:, :],
                                                  bass.IndirectOffsetOnAxis(ap=idx[0:n, i:i + 1], axis=0)).then_inc(gath[s], 16)

                for i in range(3):
                    gather(i)
                hold(pool_e, q["xe_ld"][1], 64 * (nh + 1))
                gather(3)
                for i in range(NT):
                    shift(L, i)
                    if i == 0:
                        gather(4)
                if L == 0:
                    hold(pool_e, ln_out[0], 2 * NT)
                    pool_e.dma_start(gb[:, 2, :], bcast(t["ln2_g"][1])).then_inc(gb_ld[1][1], 16)
                    pool_e.dma_start(gb[:, 3, :], bcast(t["ln2_b"][1])).then_inc(gb_ld[1][1], 16)

        @block.scalar
        def _(act):
            act.wait_ge(kraw_zero, 1)
            for i in range(NT):
                act.wait_ge(xt_ps, 2 * i + 2)
                nc.scalar.activation(XT[:, 4:8, P * i:P * i + rows_of(i)], bank((2 * i + 1) % 4, 4, P)[:, :, 0:rows_of(i)],
                                     ACT.Copy).then_inc(xt_ev[1], 1)
            for n in range(2 * MQ):
                act.wait_ge(cq_copied, n + 1)
                part = (slice(None), n // 2, slice(HALF * (n % 2), HALF * (n % 2 + 1)))
                nc.scalar.activation(sq[part], cq[part], ACT.Square).then_inc(cq_squared, 1)
            act.wait_ge(c_ld, 16)
            for i in range(NT):
                n = rows_of(i)
                raw = bank(4 + i % 2, KVL + ROPE)[0:n, :]
                act.wait_ge(kv_ps, i + 1)
                nc.scalar.activation(kraw[0:n, i, :], raw[:, KVL:], ACT.Copy)
                nc.scalar.activation(sqj[0:n, :], raw[:, 0:KVL], ACT.Square, accum_out=ss[0:n, i:i + 1]).then_inc(kv_ss, 1)
                act.wait_ge(kv_ss, i + 1)
                nc.scalar.activation(kstd[0:n, i:i + 1], ss[0:n, i:i + 1], ACT.Sqrt, scale=1.0 / KVL, bias=rms_eps[0:n, :]
                                     ).then_inc(kv_std, 1)
                if i == 0:
                    for hf in range(2):
                        act.wait_ge(cq_sum, hf + 1)
                        nc.scalar.activation(rq[:, HALF * hf:HALF * (hf + 1)], bank(hf, HALF), ACT.Sqrt, scale=1.0 / QL,
                                             bias=rms_eps).then_inc(rq_std, 1)
            for i in range(NT):
                n = rows_of(i)
                act.wait_ge(ck_ps, i + 1)
                nc.scalar.activation(ckT[:, :, P * i:P * i + n], bank(6 + i % 2, 3, P)[:, :, 0:n], ACT.Copy).then_inc(ck_ev, 1)

            def take_v(j, n):
                act.wait_ge(for_act, n)
                nc.scalar.activation(V[:, :, bass.ds(P * j, P)], bank(4, 4, P), ACT.Copy).then_inc(act_ev, 1)

            def take_k(j, n):
                act.wait_ge(for_act, n)
                nc.scalar.activation(kT[0][0:64, :], bank(7)[0:64, :], ACT.Copy)
                nc.scalar.activation(kT[1][64:128, :], bank(7)[64:128, :], ACT.Copy).then_inc(act_ev, 1)
                act.wait_ge(for_act, n + 1)
                nc.scalar.activation(wukT[:, bass.ds(j, 1), :], bank(4, 1, KVL), ACT.Copy).then_inc(act_ev, 1)

            def exps(p, par):
                for i in (3, 2, 1, 0):
                    act.wait_ge(min_set, 8 * p + 4 * par + scored(i))
                    c = 4 * par + i
                    nc.scalar.activation(prob[:, i, 0:P * (i + 1)], score(i), ACT.Exp, scale=-1.0,
                                         bias=mneg[:, c:c + 1], accum_out=rsum[:, c:c + 1]).then_inc(exp_set, 1)

            def take_probs(p, par, i):
                act.wait_ge(t_ps, 8 * p + 4 * par + 4 - i)
                nc.scalar.activation(probT[:, 1, 0:P * (i + 1)], bank(6, P * (i + 1)), ACT.Copy).then_inc(pt_ev[1], 1)

            def take_heads(p, n):
                act.wait_ge(for_act, n)
                nc.scalar.activation(oT[:, bass.ds(p, 1), 0:SEQ], bank(7, 1, SEQ), ACT.Copy).then_inc(act_ev, 1)

            def pair(p, after_one, more):
                if after_one:
                    take_heads(p - 1, 4 * p + 3)
                exps(p, 0)
                take_probs(p, 0, 3)
                if more:
                    take_v(p + 1, 4 * p + 4)
                take_probs(p, 0, 1)
                exps(p, 1)
                take_probs(p, 1, 3)
                if more:
                    take_k(p + 1, 4 * p + 5)
                take_probs(p, 1, 1)

            act.wait_ge(rq_std, 2)
            act.wait_ge(cq_done, 1)
            act.wait_ge(latent_st, 16 * 10)
            take_v(0, 1)
            take_k(0, 2)
            pair(0, False, True)
            with act.Fori(1, PAIRS - 1) as p:
                pair(p, True, True)
            pair(PAIRS - 1, True, False)
            take_heads(PAIRS - 1, 4 * PAIRS)

            turns = [0]

            def take_turn(dst, src_dims, cols=None):
                n = turns[0]
                turns[0] += 1
                act.wait_ge(turn_ps, n + 1)
                src = bank(turn_bank[n % 3], *src_dims)
                nc.scalar.activation(dst, src if cols is None else src[:, :, 0:cols], ACT.Copy).then_inc(turn_ev, 1)

            def deviation(L, which, i):
                n = rows_of(i)
                act.wait_ge(ln_agg[L], NT * which + i + 1)
                nc.scalar.activation(std[0:n, i:i + 1], mv[0:n, i, 1:2], ACT.Sqrt, bias=ln_eps[0:n, :]).then_inc(ln_std[L], 1)

            def normalise(L, i):
                n = rows_of(i)
                deviation(L, 1, i)
                act.wait_ge(ln_rstd[L], i + 1)
                nc.scalar.activation(X[0:n, i, :], X[0:n, i, :], ACT.Identity, scale=rstd[0:n, i:i + 1],
                                     bias=nmr[0:n, i:i + 1]).then_inc(ln_nrm[L], 1)

            def take_rows(L, i):
                for g in range(2):
                    take_turn(xr[L][i % 2][:, 4 * g:4 * g + 4, 0:rows_of(i)], (4, P), rows_of(i))

            def experts(L):
                q = S[L]

                def load_rows(s, first):
                    for c in range(4):
                        act.dma_start(xe[s][32 * c:32 * (c + 1), :, :],
                                         xs[first, 256 * c:256 * (c + 1)].rearrange("(a j) d -> j a d", j=32)
                                         ).then_inc(q["xe_ld"][s], 16)

                act.wait_ge(lg_ps, L + 1)
                nc.scalar.activation(r_exp, bank(6, NT * E), ACT.Exp, scale=-1.0).then_inc(lg_exp, 1)
                act.wait_ge(tab_set, 2 * L + 2)
                nh = act.value_load(n_half[0:1, 0:1], min_val=E // 2, max_val=TILES // 2)
                act.sem_inc(q["y_set"], 1)
                act.wait_ge(scat, 160 * (L + 1))
                load_rows(0, slice(0, CAP))
                load_rows(1, slice(CAP, 2 * CAP))
                for i in range(NT):
                    n = rows_of(i)
                    nc.scalar.activation(X[0:n, i, :], X[0:n, i, :], ACT.Copy, scale=ALPHA).then_inc(xscaled, 1)

                def tile(u, s, stored):
                    tl = 2 * u + s
                    act.wait_ge(q["xeT_set"], tl + 1)
                    load_rows(s, bass.ds(CAP * (tl + 2), CAP))
                    act.wait_ge(q["gate_ps"][s], u + 1)
                    nc.scalar.activation(sg[s], bank(s, KF, CAP), ACT.Silu).then_inc(q["sg_set"], 1)
                    act.wait_ge(q["down_ps"][s], u + 1)
                    if stored:
                        act.wait_ge(q["y_st"][s], 16 * u)
                    nc.scalar.activation(ys[s][0:CAP, 0:512], bank(4)[0:CAP, :], ACT.Copy).then_inc(q["y_set"], 1)
                    act.wait_ge(q["y_set"], 2 * tl + 4)
                    act.dma_start(yd[bass.ds(CAP * tl, CAP), :], ys[s][0:CAP, :]).then_inc(q["y_st"][s], 16)

                tile(0, 0, False)
                tile(0, 1, False)
                with act.Fori(1, nh) as u:
                    tile(u, 0, True)
                    tile(u, 1, True)

            def take_pages(b):
                for n in (1, 3, 5):
                    act.wait_ge(tp_ps, 6 * b + n + 1)
                    nc.scalar.activation(kpT[:, n // 2, 512:1024], bank(page_bank[n % 3]), ACT.Copy).then_inc(tp_ev[1], 1)

            def take_latent_out(b):
                act.wait_ge(ol_ps, b + 1)
                nc.scalar.activation(olat[:, :, bass.ds(b, 1), :], bank(7, MKV, 1, H, off=256), ACT.Copy).then_inc(ol_ev, 1)

            def sample(b, after_one, more):
                act.wait_ge(smin_set, b + 1)
                nc.scalar.activation(ps_s[0:H, :], view(PS, 0, PAST + DB)[0:H, :], ACT.Exp, scale=-1.0,
                                     bias=s_mneg[0:H, :], accum_out=s_sum[0:H, :]).then_inc(sexp_set, 1)
                if more:
                    take_pages(b + 1)
                if after_one:
                    take_latent_out(b - 1)

            def samples():
                sample(0, False, True)
                with act.Fori(1, DB - 1) as b:
                    sample(b, True, True)
                sample(DB - 1, True, False)
                take_latent_out(DB - 1)

            deviation(0, 0, 0)
            for i in range(1, 4):
                take_rows(0, i - 1)
                deviation(0, 0, i)
            act.wait_ge(zero_st, 16 * (PAIRS - 1))
            take_pages(0)
            take_rows(0, 3)
            samples()
            deviation(0, 0, 4)
            take_rows(0, 4)
            experts(0)
            for step in range(2 * NT + 1):
                if step < NT:
                    normalise(0, step)
                if 2 <= step < NT + 2:
                    i = step - 2
                    if i < 4:
                        for g in range(2):
                            take_turn(poolT[:, 4 * g:4 * g + 4, P * i:P * (i + 1)], (4, P))
                    else:
                        take_turn(poolT[:, :, SEQ:TOK], (KD, DB))
                if 4 <= step < NT + 4:
                    deviation(1, 0, step - 4)
                if step == 6:
                    act.wait_ge(ln_z[0], 2 * NT)
                if step >= 6:
                    take_rows(1, step - 6)
            experts(1)
            for i in range(NT):
                normalise(1, i)

        @block.vector
        def _(dve):
            chain = [0]

            def link(ins):
                chain[0] += 1
                ins.then_inc(dve_step, 1)
                dve.wait_ge(dve_step, chain[0])

            def mark(ins):
                chain[0] += 1
                ins.then_inc(dve_step, 1)
                return chain[0]

            def after(count):
                dve.wait_ge(dve_step, count)

            v = nc.vector
            v.memset(kraw[:, 4, :], 0.0).then_inc(kraw_zero, 1)
            v.memset(qs, 0.0)
            link(v.memset(qr, 0.0))
            for i in range(NT):
                dve.wait_ge(xt_ps, 2 * i + 1)
                v.tensor_copy(XT[:, 0:4, P * i:P * i + rows_of(i)], bank((2 * i) % 4, 4, P)[:, :, 0:rows_of(i)]).then_inc(xt_ev[0], 1)
            for n in range(2 * MQ):
                dve.wait_ge(cq_ps, n + 1)
                v.tensor_copy(cq[:, n // 2, HALF * (n % 2):HALF * (n % 2 + 1)], bank(n % 4, HALF)).then_inc(cq_copied, 1)
            dve.wait_ge(gain_ld, 32)
            dve.wait_ge(c_ld, 16)
            for i in range(NT):
                n = rows_of(i)
                dve.wait_ge(kv_std, i + 1)
                link(v.reciprocal(krs[0:n, i:i + 1], kstd[0:n, i:i + 1]))
                v.scalar_tensor_tensor(out=ckv[0:n, i, :], in0=bank(4 + i % 2, KVL)[0:n, :], scalar=krs[0:n, i:i + 1],
                                       in1=gkv[0:n, :], op0=ALU.mult, op1=ALU.mult).then_inc(kv_ready, 1)
                if i == 1:
                    dve.wait_ge(rq_std, 2)
                    link(v.reciprocal(rq, rq))
                if i >= 1 and i <= MQ:
                    m = i - 1
                    ins = v.scalar_tensor_tensor(out=cq[:, m, :], in0=cq[:, m, :], scalar=gq[:, m:m + 1], in1=rq,
                                                 op0=ALU.mult, op1=ALU.mult)
                    if m == MQ - 1:
                        ins.then_inc(cq_done, 1)
            half = ROPE // 2
            x1, x2 = kraw[:, :, 0:half], kraw[:, :, half:ROPE]
            tmp = [rtmp[:, a, :].rearrange("p (a b) -> p a b", a=NT) for a in range(4)]
            v.tensor_tensor(tmp[0], x1, cos_k, ALU.mult)
            v.tensor_tensor(tmp[1], x2, sin_k, ALU.mult)
            v.tensor_tensor(tmp[2], x1, sin_k, ALU.mult)
            link(v.tensor_tensor(tmp[3], x2, cos_k, ALU.mult))
            v.tensor_tensor(krot[:, :, 0:half], tmp[0], tmp[1], ALU.subtract)
            v.tensor_tensor(krot[:, :, half:ROPE], tmp[2], tmp[3], ALU.add).then_inc(kr_ready, 1)
            dve.wait_ge(kr_ready, 1)
            v.tensor_copy(kdup, krot.unsqueeze(2).to_broadcast([P, NT, 4, ROPE])).then_inc(kr_ready, 1)
            dve.wait_ge(ck_ev, 4)
            v.tensor_copy(kT[0][64:128, :], ckT[64:128, 2, 0:SEQ])
            v.tensor_copy(kT[1][0:64, :], ckT[0:64, 2, 0:SEQ]).then_inc(kr_ready, 1)

            def take_q(j, parity, hf, n):
                b = 7 if (parity + hf) == 1 else 4
                ps = bank(b, HALF)
                tab = rope_q[:, parity, HALF * hf:HALF * (hf + 1)]
                dve.wait_ge(q_ps, n)
                ins = v.tensor_tensor(qT[parity][:, HALF * hf:HALF * (hf + 1)], ps, tab, ALU.mult)
                if hf:
                    lo, hi = (slice(0, 64), slice(64, 128)) if parity == 0 else (slice(64, 128), slice(0, 64))
                    c = slice(HALF - DB, HALF)
                    v.tensor_tensor(qs[lo, bass.ds(j, 1), DB * parity:DB * (parity + 1)], ps[lo, c].unsqueeze(1),
                                    tab[lo, c].unsqueeze(1), ALU.mult)
                    ins = v.tensor_tensor(qr[hi, :, bass.ds(2 * j + parity, 1)], ps[hi, c].unsqueeze(2),
                                          tab[hi, c].unsqueeze(2), ALU.mult)
                ins.then_inc(q_ev, 1)

            def mins(p, par):
                for i in (3, 2, 1, 0):
                    hold(dve, s_ps, 8 * p + 4 * par + scored(i))
                    w = P * (i + 1)
                    sc = score(i)
                    v.tensor_tensor_reduce(sc, sc, causal[:, SEQ - w:SEQ], 1.0, BIG, ALU.add, ALU.min,
                                           mneg[:, 4 * par + i:4 * par + i + 1]).then_inc(min_set, 1)

            def take_probs(p, par):
                for i in (2, 0):
                    dve.wait_ge(t_ps, 8 * p + 4 * par + 4 - i)
                    v.tensor_copy(probT[:, 0, 0:P * (i + 1)], bank(5, P * (i + 1))).then_inc(pt_ev[0], 1)

            def head_out(p, par):
                dve.wait_ge(exp_set, 8 * p + 4 * par + 4)
                v.reciprocal(rinv[:, 4 * par:4 * par + 4], rsum[:, 4 * par:4 * par + 4]).then_inc(rinv_set, 1)
                dve.wait_ge(rinv_set, 2 * p + par + 1)
                dve.wait_ge(o_ps, 2 * p + par + 1)
                v.tensor_tensor(osb[:, :, VH * par:VH * (par + 1)], bank(3, 4, VH, off=256 * par),
                                rinv[:, 4 * par:4 * par + 4].unsqueeze(2).to_broadcast([P, 4, VH]), ALU.mult).then_inc(o_ev, 1)

            def pair(p, more):
                for par in range(2):
                    mins(p, par)
                    if more:
                        take_q(p + 1, par, 0, 4 * p + 5 + 2 * par)
                        take_q(p + 1, par, 1, 4 * p + 6 + 2 * par)
                    take_probs(p, par)
                    head_out(p, par)

            for par in range(2):
                for hf in range(2):
                    take_q(0, par, hf, 2 * par + hf + 1)
            with dve.Fori(0, PAIRS - 1) as p:
                pair(p, True)
            pair(PAIRS - 1, False)

            def set_qb(b, s):
                v.tensor_copy(qb[s][:, 0:MKV, :].unsqueeze(2), qlat[:, :, bass.ds(b, 1), :])
                v.tensor_copy(qb[s][:, MKV:MKV + 1, :], qr[:, bass.ds(b, 1), :]).then_inc(qb_set, 1)

            def take_pages(b):
                for n in (0, 2, 4):
                    dve.wait_ge(tp_ps, 6 * b + n + 1)
                    v.tensor_copy(kpT[:, n // 2, 0:512], bank(page_bank[n % 3])).then_inc(tp_ev[0], 1)

            def latent_out(b):
                dve.wait_ge(pv_ps, b + 3)
                v.tensor_scalar(onat[0:H, :], bank(7, KVL)[0:H, :], s_inv[0:H, :], None, ALU.mult).then_inc(onat_set, 1)

            def sample(b, after_one, more_in):
                if more_in is not None:
                    set_qb(b + 1, more_in)
                dve.wait_ge(sc_ps, b + 1)
                v.tensor_tensor(bank(2, 1, DB)[0:H, :, :], bank(2, 1, DB)[0:H, :, :], own_sample[0:H, bass.ds(b, 1), :], ALU.add
                                ).then_inc(new_masked, 1)
                dve.wait_ge(new_masked, b + 1)
                v.tensor_reduce(s_mneg[0:H, :], view(PS, 0, PAST + DB)[0:H, :], AXX, ALU.min).then_inc(smin_set, 1)
                if after_one:
                    latent_out(b - 1)
                if more_in is not None:
                    take_pages(b + 1)
                dve.wait_ge(spT_ps, b + 1)
                turned = bank(6, NPAGES + 1, H, off=256)
                v.tensor_copy(psT_s[:, 0:NPAGES, :], turned[:, 0:NPAGES, :])
                v.tensor_copy(psT_s[0:DB, NPAGES, :], turned[0:DB, NPAGES, :]).then_inc(spT_ev, 1)
                dve.wait_ge(sexp_set, b + 1)
                v.reciprocal(s_inv[0:H, :], s_sum[0:H, :]).then_inc(sinv_set, 1)
                dve.wait_ge(sinv_set, b + 1)

            def samples():
                dve.wait_ge(ql_ps, 1)
                for c in range(MKV):
                    ins = v.tensor_copy(qlat[:, c, :, :].rearrange("p b (j e) -> p j e b", e=2),
                                        bank(3, MKV, PAIRS, 16)[:, c, :, :].rearrange("p j (e b) -> p j e b", e=2))
                link(ins)
                set_qb(0, 0)
                dve.wait_ge(zero_st, 16 * (PAIRS - 1))
                take_pages(0)
                sample(0, False, 1)
                with dve.Fori(0, (DB - 2) // 3) as u:
                    for d in (1, 2, 3):
                        sample(3 * u + d, True, (d + 1) % 3)
                sample(DB - 1, True, None)
                latent_out(DB - 1)
                dve.wait_ge(uv_ps, 1)
                for e in range(2):
                    part = slice(64 * e, 64 * e + 64)
                    ins = v.tensor_copy(oT[part, :, SEQ:TOK].unsqueeze(3), bank(3, PAIRS, DB, 2, off=256)[part, :, :, e:e + 1])
                ins.then_inc(uv_ev, 1)

            def stats(L, which, i):
                n = rows_of(i)
                k = NT * which + i + 1
                x = X[0:n, i, :]
                if which == 0:
                    dve.wait_ge(mix_ps, NT * L + i + 1)
                    v.scalar_tensor_tensor(out=x, in0=x, scalar=ALPHA, in1=view(PS, 1024 * (i % 2), D)[0:n, :],
                                           op0=ALU.mult, op1=ALU.add).then_inc(ln_z[L], 1)
                else:
                    s = i % 3
                    dve.wait_ge(gath[s], 32 * ((L if s == 2 else 2 * L) + i // 3 + 1))
                    dve.wait_ge(xscaled, NT * L + i + 1)
                    link(v.scalar_tensor_tensor(out=x, in0=ya[s][0:n, :], scalar=ca[0:n, i:i + 1], in1=x,
                                                op0=ALU.mult, op1=ALU.add))
                    v.scalar_tensor_tensor(out=x, in0=yb[s][0:n, :], scalar=cb[0:n, i:i + 1], in1=x,
                                           op0=ALU.mult, op1=ALU.add).then_inc(ln_z[L], 1)
                dve.wait_ge(ln_z[L], k)
                for c in range(2):
                    ins = v.bn_stats(bn[0:n, i, 6 * c:6 * c + 6], X[0:n, i, 512 * c:512 * (c + 1)])
                link(ins)
                v.bn_aggr(mv[0:n, i, :], bn[0:n, i, :]).then_inc(ln_agg[L], 1)

            def norm1(L, i):
                n = rows_of(i)
                x, gains, offsets = X[0:n, i, :], gb[0:n, 0, :], gb[0:n, 1, :]
                stats(L, 0, i)
                if i == 0:
                    dve.wait_ge(gb_ld[L][0], 32)
                dve.wait_ge(ln_agg[L], i + 1)
                link(v.scalar_tensor_tensor(out=x, in0=x, scalar=mv[0:n, i, 0:1], in1=gains, op0=ALU.subtract, op1=ALU.mult))
                dve.wait_ge(ln_std[L], i + 1)
                link(v.reciprocal(rstd[0:n, i:i + 1], std[0:n, i:i + 1]))
                v.scalar_tensor_tensor(out=x, in0=x, scalar=rstd[0:n, i:i + 1], in1=offsets, op0=ALU.mult, op1=ALU.add
                                       ).then_inc(ln_out[L], 1)

            def spread(L, i):
                n = rows_of(i)
                dve.wait_ge(ln_std[L], NT + i + 1)
                link(v.reciprocal(rstd[0:n, i:i + 1], std[0:n, i:i + 1]))
                v.tensor_scalar(nmr[0:n, i:i + 1], mv[0:n, i, 0:1], rstd[0:n, i:i + 1], -1.0, ALU.mult, ALU.mult).then_inc(ln_rstd[L], 1)

            def gain(L, i):
                n = rows_of(i)
                dve.wait_ge(ln_nrm[L], i + 1)
                if i == 0:
                    dve.wait_ge(gb_ld[L][1], 32)
                v.tensor_tensor(X[0:n, i, :], X[0:n, i, :], gb[0:n, 2, :], ALU.mult).then_inc(ln_gam[L], 1)

            def route(L):
                def five(a):
                    return a.rearrange("p (a b) -> p a b", a=NT)

                def by_group(a):
                    return a.rearrange("p (a b) -> p a b", b=EPG)

                over = [P, NT, E]
                dve.wait_ge(lg_exp, L + 1)
                link(v.tensor_scalar_add(r_exp, r_exp, 1.0))
                link(v.reciprocal(r_s, r_exp))
                if L == 0:
                    dve.wait_ge(router_ld, 32)
                link(v.tensor_tensor(five(r_bias), five(r_s), bias_row.unsqueeze(1).to_broadcast(over), ALU.add))
                b4 = by_group(r_bias)
                sums = r_m6.rearrange("p (a b) -> p a b", b=6)
                cmp = r_big.rearrange("p (a j i) -> p a j i", j=EPG, i=2 * EPG)
                wide = [P, NT * GROUPS, EPG, EPG]
                bi, bj = b4.unsqueeze(2).to_broadcast(wide), b4.unsqueeze(3).to_broadcast(wide)
                gs, gp, gsel = (a.rearrange("p (a b) -> p a b", a=NT) for a in (r_gs, r_gp, r_gsel))
                mark(v.tensor_tensor(sums[:, :, 0:3], b4[:, :, 0:3], b4[:, :, 1:4], ALU.add))
                mark(v.tensor_tensor(sums[:, :, 3:5], b4[:, :, 0:2], b4[:, :, 2:4], ALU.add))
                all_sums = mark(v.tensor_tensor(sums[:, :, 5:6], b4[:, :, 0:1], b4[:, :, 3:4], ALU.add))
                equal = mark(v.tensor_tensor(cmp[:, :, :, EPG:], bi, bj, ALU.is_equal))
                after(all_sums)
                scored = mark(v.tensor_reduce(r_gs, sums, AXX, ALU.max))
                after(equal)
                mark(v.tensor_tensor(cmp[:, :, :, EPG:], cmp[:, :, :, EPG:], earlier.unsqueeze(1).to_broadcast(wide), ALU.mult))
                after(scored)
                best = mark(v.tensor_reduce(r_m, gs, AXX, ALU.max))
                compared = mark(v.tensor_tensor(cmp[:, :, :, 0:EPG], bi, bj, ALU.is_gt))
                after(best)
                is_best = mark(v.tensor_tensor(gp, gs, r_m.unsqueeze(2).to_broadcast([P, NT, GROUPS]), ALU.is_equal))
                after(compared)
                mark(v.tensor_reduce(by_group(r_rank), cmp, AXX, ALU.add))
                after(is_best)
                link(v.tensor_tensor(gp, gp, prefer.unsqueeze(1).to_broadcast([P, NT, GROUPS]), ALU.mult))
                link(v.tensor_reduce(r_m, gp, AXX, ALU.max))
                link(v.tensor_tensor(gsel, gp, r_m.unsqueeze(2).to_broadcast([P, NT, GROUPS]), ALU.is_equal))
                link(v.scalar_tensor_tensor(out=by_group(r_sel), in0=by_group(r_rank), scalar=float(2),
                                            in1=r_gsel.unsqueeze(2).to_broadcast([P, NT * GROUPS, EPG]),
                                            op0=ALU.is_lt, op1=ALU.mult))
                v.tensor_scalar(r_sel[:, 64:80], r_sel[:, 64:80], real_row, None, ALU.mult).then_inc(sel_set, 1)
                dve.wait_ge(sel_set, L + 1)
                link(v.tensor_tensor(r_comb, r_s, r_sel, ALU.mult))
                link(v.tensor_reduce(r_den, five(r_comb), AXX, ALU.add))
                link(v.tensor_scalar(r_den[:, NT - 1:NT], r_den[:, NT - 1:NT], no_row, None, ALU.max))
                link(v.reciprocal(r_den, r_den))
                link(v.tensor_tensor(five(r_comb), five(r_comb), r_den.unsqueeze(2).to_broadcast(over), ALU.mult))
                dve.wait_ge(cnt_ps, L + 1)
                cum, in_tile, sofar = five(r_rank), bank(6, NT, E, off=208), five(r_bias)
                link(v.tensor_copy(sofar[:, 1, :], in_tile[:, 0, :]))
                for j in range(1, NT - 1):
                    link(v.tensor_tensor(sofar[:, j + 1, :], sofar[:, j, :], in_tile[:, j, :], ALU.add))
                link(v.tensor_tensor(r_nt, sofar[:, NT - 1, :], in_tile[:, NT - 1, :], ALU.add))
                v.tensor_tensor(cum[:, 1:NT, :], sofar[:, 1:NT, :], bank(6, NT, E, off=128)[:, 1:NT, :], ALU.add)
                link(v.tensor_copy(cum[:, 0, :], bank(6, NT, E, off=128)[:, 0, :]))
                k5 = r_k[:, 0:E * KOV].rearrange("p (a b) -> p a b", a=E)
                link(v.tensor_tensor(k5, r_nt.unsqueeze(2).to_broadcast([P, E, KOV]),
                                     steps.unsqueeze(1).to_broadcast([P, E, KOV]), ALU.is_gt))
                link(v.tensor_reduce(r_ex, k5, AXX, ALU.add))
                tri = r_big[:, 0:E * E].rearrange("p (a b) -> p a b", a=E)
                link(v.tensor_tensor(tri, r_ex.unsqueeze(1).to_broadcast([P, E, E]), before_e, ALU.mult))
                link(v.tensor_reduce(r_ovb, tri, AXX, ALU.add))
                link(v.scalar_tensor_tensor(out=r_diff, in0=r_ovb, scalar=float(CAP), in1=slot_over, op0=ALU.mult, op1=ALU.add))
                link(v.tensor_scalar(five(r_slot), cum, float(CAP), None, ALU.is_ge))
                link(v.tensor_tensor(five(r_slot), five(r_slot), r_diff.unsqueeze(1).to_broadcast(over), ALU.mult))
                link(v.tensor_tensor(five(r_slot), five(r_slot), cum, ALU.add))
                link(v.tensor_tensor(five(r_slot), five(r_slot), slot0.unsqueeze(1).to_broadcast(over), ALU.add))
                link(v.scalar_tensor_tensor(out=r_slot, in0=r_slot, scalar=1.0, in1=r_sel, op0=ALU.add, op1=ALU.mult))
                v.tensor_reduce(r_all, five(r_slot), AXX, ALU.add)
                link(v.tensor_reduce(r_a, five(r_slot), AXX, ALU.max))
                v.tensor_scalar(idx_a, r_a, -1.0, None, ALU.add).then_inc(idx_set, 1)
                link(v.tensor_tensor(r_b, r_all, r_a, ALU.subtract))
                v.tensor_scalar(idx_b, r_b, -1.0, None, ALU.add).then_inc(idx_set, 1)
                link(v.tensor_tensor(five(r_bias), five(r_slot), r_a.unsqueeze(2).to_broadcast(over), ALU.is_equal))
                link(v.tensor_tensor(r_bias, r_bias, r_comb, ALU.mult))
                v.tensor_reduce(ca, five(r_bias), AXX, ALU.add)
                link(v.tensor_tensor(r_comb, r_comb, r_bias, ALU.subtract))
                v.tensor_reduce(cb, five(r_comb), AXX, ALU.add)
                one = slice(0, 1)
                v.tensor_copy(r_tab[one, 0:E], expert[one, :])
                link(v.tensor_tensor(r_end[one, :], r_ovb[one, :], r_ex[one, :], ALU.add))
                ke = r_k[one, 0:NOV * E].rearrange("p (a b) -> p a b", a=NOV)
                ks = r_big[one, 0:NOV * E].rearrange("p (a b) -> p a b", a=NOV)
                kk = over_k[one, :].unsqueeze(2).to_broadcast([1, NOV, E])
                v.tensor_tensor(ke, kk, r_ovb[one, :].unsqueeze(1).to_broadcast([1, NOV, E]), ALU.is_ge)
                link(v.tensor_tensor(ks, kk, r_end[one, :].unsqueeze(1).to_broadcast([1, NOV, E]), ALU.is_lt))
                link(v.tensor_tensor(ke, ke, ks, ALU.mult))
                link(v.tensor_tensor(ke, ke, expert[one, :].unsqueeze(1).to_broadcast([1, NOV, E]), ALU.mult))
                link(v.tensor_reduce(r_tab[one, E:TILES], ke, AXX, ALU.add))
                v.tensor_copy(tile_ids[one, 0:TILES], r_tab[one, 0:TILES]).then_inc(tab_set, 1)
                link(v.tensor_reduce(r_nov[one, :], r_ex[one, :], AXX, ALU.add))
                link(v.tensor_scalar(r_nh[one, 0:NOV // 2], even_k[one, :], r_nov[one, :], None, ALU.is_lt))
                link(v.tensor_reduce(r_nov[one, :], r_nh[one, 0:NOV // 2], AXX, ALU.add))
                v.tensor_scalar(n_half[one, :], r_nov[one, :], float(E // 2), None, ALU.add).then_inc(tab_set, 1)

            def experts(L):
                q = S[L]
                dve.wait_ge(tab_set, 2 * L + 2)
                nh = dve.value_load(n_half[0:1, 0:1], min_val=E // 2, max_val=TILES // 2)
                dve.sem_inc(q["y_set"], 1)

                def turn_rows(s):
                    v.transpose(xeT[s].rearrange("p m (a j) -> p a m j", j=32).bitcast(mybir.dt.uint32),
                                xe[s].rearrange("p a (i m) -> p a m i", i=32).bitcast(mybir.dt.uint32)
                                ).then_inc(q["xeT_set"], 1)

                dve.wait_ge(q["xe_ld"][0], 64)
                turn_rows(0)

                def tile(u, s, stored):
                    tl = 2 * u + s
                    dve.wait_ge(q["sg_set"], tl + 1)
                    dve.wait_ge(q["xe_ld"][1 - s], 64 * (u + 1 + s))
                    turn_rows(1 - s)
                    dve.wait_ge(q["up_ps"][s], 2 * u + 1)
                    v.tensor_tensor(h[s][:, 0:KF - 1, :], sg[s][:, 0:KF - 1, :], bank(2 + s, KF, CAP)[:, 0:KF - 1, :], ALU.mult
                                    ).then_inc(q["h_set"], 1)
                    dve.wait_ge(q["up_ps"][s], 2 * u + 2)
                    v.tensor_tensor(h[s][:, KF - 1, :], sg[s][:, KF - 1, :], bank(6 + s, CAP), ALU.mult).then_inc(q["h_set"], 1)
                    dve.wait_ge(q["down_ps"][s], u + 1)
                    if stored:
                        dve.wait_ge(q["y_st"][s], 16 * u)
                    v.tensor_copy(ys[s][0:CAP, 512:D], bank(5)[0:CAP, :]).then_inc(q["y_set"], 1)

                tile(0, 0, False)
                tile(0, 1, False)
                with dve.Fori(1, nh) as u:
                    tile(u, 0, True)
                    tile(u, 1, True)

            dve.wait_ge(act_ev, 4 * PAIRS)
            v.memset(bank(6, NT * E), 0.0).then_inc(lg_zero, 1)
            for i in range(4):
                norm1(0, i)
            samples()
            norm1(0, 4)
            route(0)
            experts(0)
            v.memset(bank(6, NT * E), 0.0).then_inc(lg_zero, 1)
            dve.wait_ge(wp_ld, 16)
            dve.wait_ge(st_ld, 32)
            wp4 = wpool.rearrange("p (g k) d -> p g k d", g=4)
            v.tensor_tensor(wp4, wp4, pscale.rearrange("p (g d) -> p g d", g=4).unsqueeze(2).to_broadcast([P, 4, 2, 256]),
                            ALU.mult).then_inc(wp_ready, 1)
            for step in range(NT + 4):
                if step < NT:
                    stats(0, 1, step)
                if 2 <= step <= NT:
                    gain(0, step - 1)
                if step < NT:
                    spread(0, step)
                if step == 0:
                    gain(0, 0)
                if step >= 4:
                    if step - 4 == 3:
                        dve.wait_ge(pool_out, 32)
                    norm1(1, step - 4)
            route(1)
            experts(1)
            for i in range(NT + 1):
                if i < NT:
                    stats(1, 1, i)
                if i:
                    gain(1, i - 1)
                if i < NT:
                    spread(1, i)


_INS = ["x_prompt", "x_sample", "cache_ckv", "cache_krope", "state_pool", "page_table", "w_dq", "g_q", "w_uq", "w_dkv",
        "g_kv", "w_uk", "w_uv", "w_o", "w_pool", "pool_scale", "w_router", "router_bias", "w_gate", "w_up", "w_down",
        "ln1_g", "ln1_b", "ln2_g", "ln2_b"]
_OUTS = [("o_y_p", (1, SEQ, D)), ("o_y_s", (DB, 1, D)), ("o_ckv_p", (1, 1, SEQ, KVL)), ("o_kr_p", (1, 1, SEQ, ROPE)),
         ("o_pool_p", (1, 1, CTX, D)), ("o_ckv_s", (1, DB, 1, KVL)), ("o_kr_s", (1, DB, 1, ROPE)),
         ("o_pool_s", (1, DB, CTX, D))]


def kernel(**inputs):
    import concourse.bacc as _bacc
    from concourse.bass_utils import run_bass_kernel_spmd as _run

    nc = _bacc.Bacc("TRN2", target_bir_lowering=False, num_devices=1)
    consts, place = constants()
    arrays, t = {"consts": consts}, {}
    for name in _INS:
        arrays[name] = np.ascontiguousarray(inputs[name])
    for name, a in arrays.items():
        t[name] = nc.dram_tensor(name, a.shape, mybir.dt.from_np(a.dtype), kind="ExternalInput").ap()
    for name, shape in _OUTS:
        t[name] = nc.dram_tensor(name, shape, F32, kind="ExternalOutput").ap()
    build(nc, t, consts.shape, place)
    r = _run(nc, [arrays], core_ids=[0])
    return tuple(r.results[0][name] for name, _ in _OUTS)
```
